# Optimizing a Trainium2 kernel written in Bass

```python
import math
import jax, jax.numpy as jnp
from jax import lax
import numpy as np

D_MODEL = 1024
BATCH = 1
SEQ = 512
DEPTH = 2

HEAD_DIM = 64
N_HEADS_A = 6
DILATED_PATTERNS = ((128, 1), (512, 4), (2048, 16))
N_HEADS_B = 6
Q_LORA_RANK = 384
KV_LORA_RANK = 256
QK_NOPE_DIM = 64
QK_ROPE_DIM = 32
V_HEAD_DIM = 64
ROPE_BASE = 10000.0
MLA_Q_BLOCK = 128
N_HEADS_C = 4
GRID_W = 64
NA_ROWS = 8
NA_COLS = 16
NA_COL_BLOCK = 16
NA_COL_SPAN = 32

WIDTH_A = N_HEADS_A * HEAD_DIM
WIDTH_B = N_HEADS_B * V_HEAD_DIM
WIDTH_C = N_HEADS_C * HEAD_DIM
MIX_WIDTH = WIDTH_A + WIDTH_B + WIDTH_C
SPLIT_SIZES = (WIDTH_A, WIDTH_A, WIDTH_A, Q_LORA_RANK, KV_LORA_RANK, QK_ROPE_DIM, WIDTH_C, WIDTH_C, WIDTH_C)
IN_COLS = sum(SPLIT_SIZES)
D_FF = 2816
N_EXPERTS = 8
TOP_K = 2
D_FF_EXPERT = 3584
MOE_BLOCK = 128
RMS_EPS = 1e-6
NEG_INF = -1e30

kernel_name = "hybrid_dilated_mla_neighbourhood_moe_encoder"

def rms_norm(x, g):
    xf = x.astype(jnp.float32)
    y = xf * lax.rsqrt(jnp.mean(xf * xf, axis=-1, keepdims=True) + RMS_EPS)
    return (y * g.astype(jnp.float32)).astype(x.dtype)

def alibi_slopes(n_heads):
    return 2.0 ** (-8.0 * jnp.arange(1, n_heads + 1, dtype=jnp.float32) / n_heads)

def rope(x, pos):
    r = x.shape[-1]
    inv = ROPE_BASE ** (-jnp.arange(0, r, 2, dtype=jnp.float32) / r)
    ang = pos[:, None].astype(jnp.float32) * inv[None, :]
    cos, sin = jnp.cos(ang), jnp.sin(ang)
    x1 = x[..., : r // 2].astype(jnp.float32)
    x2 = x[..., r // 2:].astype(jnp.float32)
    return jnp.concatenate([x1 * cos - x2 * sin, x1 * sin + x2 * cos], axis=-1).astype(x.dtype)

def dilated_window_branch(q, k, v, dilation, half, slopes):
    B, H, S, hd = q.shape
    n = S // dilation
    nb = -(-n // half)
    npad = nb * half

    def split(a):
        return a.reshape(B, H, n, dilation, hd).transpose(0, 1, 3, 2, 4)

    qs = jnp.pad(split(q), ((0, 0),) * 3 + ((0, npad - n), (0, 0))).reshape(B, H, dilation, nb, half, hd)

    def band(a):
        ap = jnp.pad(split(a), ((0, 0),) * 3 + ((half, npad - n + half), (0, 0)))
        ap = ap.reshape(B, H, dilation, nb + 2, half, hd)
        return jnp.concatenate([ap[:, :, :, 0:nb], ap[:, :, :, 1:nb + 1], ap[:, :, :, 2:nb + 2]], axis=4)

    kb, vb = band(k), band(v)
    qpos = jnp.arange(nb)[:, None] * half + jnp.arange(half)[None, :]
    kpos = jnp.arange(nb)[:, None] * half - half + jnp.arange(3 * half)[None, :]
    rel = kpos[:, None, :] - qpos[:, :, None]
    valid = (jnp.abs(rel) <= half) & (kpos[:, None, :] >= 0) & (kpos[:, None, :] < n)
    dist = (jnp.abs(rel) * dilation).astype(jnp.float32)
    s = jnp.einsum('bhrnqd,bhrnkd->bhrnqk', qs, kb).astype(jnp.float32) * (hd ** -0.5)
    s = s - slopes[None, :, None, None, None, None] * dist
    s = jnp.where(valid, s, NEG_INF)
    m = jnp.max(s, axis=-1, keepdims=True)
    p = jnp.exp(s - m)
    l = jnp.sum(p, axis=-1, keepdims=True)
    o = jnp.einsum('bhrnqk,bhrnkd->bhrnqd', (p / l).astype(v.dtype), vb)

    def merge(a):
        xdim = a.shape[-1]
        a = a.reshape(B, H, dilation, npad, xdim)[:, :, :, :n]
        return a.transpose(0, 1, 3, 2, 4).reshape(B, H, S, xdim)

    return merge(o), merge(m)[..., 0], merge(l)[..., 0]

def dilated_attention(q, k, v):
    slopes = alibi_slopes(q.shape[1])
    outs, ms, ls = [], [], []
    for window, dilation in DILATED_PATTERNS:
        o, m, l = dilated_window_branch(q, k, v, dilation, (window // 2) // dilation, slopes)
        outs.append(o)
        ms.append(m)
        ls.append(l)
    m_all = jnp.stack(ms)
    l_all = jnp.stack(ls)
    w = l_all * jnp.exp(m_all - jnp.max(m_all, axis=0, keepdims=True))
    w = w / jnp.sum(w, axis=0, keepdims=True)
    return jnp.einsum('gbhs,gbhsd->bhsd', w.astype(q.dtype), jnp.stack(outs))

def mla_attention(c_q, c_kv, k_rope_raw, g_q, g_kv, w_uq, w_ukv):
    B, S, _ = c_q.shape
    H = N_HEADS_B
    q = jnp.einsum('bsr,rf->bsf', rms_norm(c_q, g_q), w_uq)
    q = q.reshape(B, S, H, QK_NOPE_DIM + QK_ROPE_DIM).transpose(0, 2, 1, 3)
    kv = jnp.einsum('bsr,rf->bsf', rms_norm(c_kv, g_kv), w_ukv)
    kv = kv.reshape(B, S, H, QK_NOPE_DIM + V_HEAD_DIM).transpose(0, 2, 1, 3)
    pos = jnp.arange(S)
    q_nope, q_rope = q[..., :QK_NOPE_DIM], rope(q[..., QK_NOPE_DIM:], pos)
    k_nope, v = kv[..., :QK_NOPE_DIM], kv[..., QK_NOPE_DIM:]
    k_rope = rope(k_rope_raw, pos)
    scale = (QK_NOPE_DIM + QK_ROPE_DIM) ** -0.5
    nq = S // MLA_Q_BLOCK

    def to_blocks(a):
        return a.reshape(B, H, nq, MLA_Q_BLOCK, a.shape[-1]).transpose(2, 0, 1, 3, 4)

    def block(args):
        qn, qr = args
        s = (jnp.einsum('bhqd,bhkd->bhqk', qn, k_nope)
             + jnp.einsum('bhqr,bkr->bhqk', qr, k_rope)).astype(jnp.float32) * scale
        p = jax.nn.softmax(s, axis=-1).astype(v.dtype)
        return jnp.einsum('bhqk,bhkd->bhqd', p, v)

    o = lax.map(block, (to_blocks(q_nope), to_blocks(q_rope)))
    return o.transpose(1, 2, 0, 3, 4).reshape(B, H, S, V_HEAD_DIM)

def neighbourhood_attention(q, k, v, rpb):
    B, H, S, hd = q.shape
    rows = S // GRID_W
    kr = min(NA_ROWS, rows)
    ncb = GRID_W // NA_COL_BLOCK
    r = jnp.arange(rows)
    row_start = jnp.clip(r - kr // 2, 0, rows - kr)
    key_rows = row_start[:, None] + jnp.arange(kr)[None, :]
    cb = jnp.arange(ncb) * NA_COL_BLOCK
    col_start = jnp.clip(cb - NA_COLS // 2, 0, GRID_W - NA_COL_SPAN)
    key_cols = col_start[:, None] + jnp.arange(NA_COL_SPAN)[None, :]
    flat = key_rows[:, None, :, None] * GRID_W + key_cols[None, :, None, :]
    kg = k[:, :, flat]
    vg = v[:, :, flat]
    qg = q.reshape(B, H, rows, ncb, NA_COL_BLOCK, hd)
    s = jnp.einsum('bhrjqd,bhrjakd->bhrjqak', qg, kg).astype(jnp.float32) * (hd ** -0.5)
    qcol = cb[:, None] + jnp.arange(NA_COL_BLOCK)[None, :]
    win_start = jnp.clip(qcol - NA_COLS // 2, 0, GRID_W - NA_COLS)
    col_ok = (key_cols[:, None, :] >= win_start[:, :, None]) & (key_cols[:, None, :] < win_start[:, :, None] + NA_COLS)
    drow = key_rows - r[:, None]
    dcol = jnp.clip(key_cols[:, None, :] - qcol[:, :, None], -(NA_COLS - 1), NA_COLS - 1)
    bias = rpb[:, drow[:, None, None, :, None] + (NA_ROWS - 1), dcol[None, :, :, None, :] + (NA_COLS - 1)]
    s = s + bias[None].astype(jnp.float32)
    s = jnp.where(col_ok[None, None, None, :, :, None, :], s, NEG_INF)
    shp = s.shape
    p = jax.nn.softmax(s.reshape(shp[:5] + (kr * NA_COL_SPAN,)), axis=-1).reshape(shp)
    o = jnp.einsum('bhrjqak,bhrjakd->bhrjqd', p.astype(v.dtype), vg)
    return o.reshape(B, H, S, hd)

def hybrid_mixer(h, w_in, g_q, g_kv, w_uq, w_ukv, rpb, g_out_a, g_out_b, g_out_c, w_o):
    B, S, _ = h.shape
    proj = jnp.einsum('bsd,df->bsf', h, w_in)
    bounds = np.cumsum(SPLIT_SIZES)[:-1].tolist()
    qa, ka, va, c_q, c_kv, k_rope, qc, kc, vc = jnp.split(proj, bounds, axis=-1)

    def heads(a, n_heads):
        return a.reshape(B, S, n_heads, HEAD_DIM).transpose(0, 2, 1, 3)

    def flat(o):
        return o.transpose(0, 2, 1, 3).reshape(B, S, -1)

    out_a = dilated_attention(heads(qa, N_HEADS_A), heads(ka, N_HEADS_A), heads(va, N_HEADS_A))
    out_b = mla_attention(c_q, c_kv, k_rope, g_q, g_kv, w_uq, w_ukv)
    out_c = neighbourhood_attention(heads(qc, N_HEADS_C), heads(kc, N_HEADS_C), heads(vc, N_HEADS_C), rpb)
    y = jnp.concatenate([rms_norm(flat(out_a), g_out_a),
                         rms_norm(flat(out_b), g_out_b),
                         rms_norm(flat(out_c), g_out_c)], axis=-1)
    return jnp.einsum('bsf,fd->bsd', y, w_o)

def swiglu(h, w1, w3, w2):
    return (jax.nn.silu(h @ w1) * (h @ w3)) @ w2

def moe_swiglu(h, w_router, w1, w3, w2):
    B, S, D = h.shape
    x = h.reshape(-1, D)
    n_tok = x.shape[0]
    logits = jnp.einsum('nd,de->ne', x.astype(jnp.float32), w_router.astype(jnp.float32))
    top_logit, top_e = lax.top_k(logits, TOP_K)
    gates = jax.nn.softmax(top_logit, axis=-1)
    n_assign = n_tok * TOP_K
    flat_e = top_e.reshape(n_assign)
    order = jnp.argsort(flat_e)
    sorted_e = flat_e[order]
    sorted_tok = order // TOP_K
    sorted_gate = gates.reshape(n_assign)[order]
    counts = jnp.bincount(flat_e, length=N_EXPERTS)
    padded = (counts + MOE_BLOCK - 1) // MOE_BLOCK * MOE_BLOCK
    start = jnp.cumsum(counts) - counts
    padded_end = jnp.cumsum(padded)
    padded_start = padded_end - padded
    dest = padded_start[sorted_e] + jnp.arange(n_assign) - start[sorted_e]
    n_blocks = -(-(n_assign + N_EXPERTS * (MOE_BLOCK - 1)) // MOE_BLOCK)
    n_rows = n_blocks * MOE_BLOCK
    row_tok = jnp.zeros((n_rows,), jnp.int32).at[dest].set(sorted_tok.astype(jnp.int32))
    block_e = jnp.minimum(jnp.searchsorted(padded_end, jnp.arange(n_blocks) * MOE_BLOCK, side='right'), N_EXPERTS - 1)
    xb = x[row_tok].reshape(n_blocks, MOE_BLOCK, D)

    def expert_block(args):
        xi, e = args
        return swiglu(xi, w1[e], w3[e], w2[e])

    yb = lax.map(expert_block, (xb, block_e)).reshape(n_rows, D)
    y = jnp.zeros_like(x).at[sorted_tok].add(sorted_gate[:, None].astype(x.dtype) * yb[dest])
    return y.reshape(B, S, D)

def setup_inputs(seed: int = 0) -> dict:
    key = jax.random.key(seed)
    ks = jax.random.split(key, 24)
    f32 = jnp.float32
    n_dense = (DEPTH + 1) // 2
    n_moe = DEPTH // 2
    res = (2 * DEPTH) ** -0.5

    def normal(k, shape, fan_in, gain=1.0):
        return jax.random.normal(k, shape, f32) * (gain * fan_in ** -0.5)

    def norm_gain(k, shape):
        return 1.0 + 0.02 * jax.random.normal(k, shape, f32)

    return {
        "x": jax.random.normal(ks[0], (BATCH, SEQ, D_MODEL), f32),
        "g_mix": norm_gain(ks[1], (DEPTH, D_MODEL)),
        "w_in": normal(ks[2], (DEPTH, D_MODEL, IN_COLS), D_MODEL),
        "g_q": norm_gain(ks[3], (DEPTH, Q_LORA_RANK)),
        "g_kv": norm_gain(ks[4], (DEPTH, KV_LORA_RANK)),
        "w_uq": normal(ks[5], (DEPTH, Q_LORA_RANK, N_HEADS_B * (QK_NOPE_DIM + QK_ROPE_DIM)), Q_LORA_RANK),
        "w_ukv": normal(ks[6], (DEPTH, KV_LORA_RANK, N_HEADS_B * (QK_NOPE_DIM + V_HEAD_DIM)), KV_LORA_RANK),
        "rpb": 0.1 * jax.random.normal(ks[7], (DEPTH, N_HEADS_C, 2 * NA_ROWS - 1, 2 * NA_COLS - 1), f32),
        "g_out_a": norm_gain(ks[8], (DEPTH, WIDTH_A)),
        "g_out_b": norm_gain(ks[9], (DEPTH, WIDTH_B)),
        "g_out_c": norm_gain(ks[10], (DEPTH, WIDTH_C)),
        "w_o": normal(ks[11], (DEPTH, MIX_WIDTH, D_MODEL), MIX_WIDTH, res),
        "g_ffn": norm_gain(ks[12], (DEPTH, D_MODEL)),
        "w1": normal(ks[13], (n_dense, D_MODEL, D_FF), D_MODEL),
        "w3": normal(ks[14], (n_dense, D_MODEL, D_FF), D_MODEL),
        "w2": normal(ks[15], (n_dense, D_FF, D_MODEL), D_FF, res),
        "w_router": normal(ks[16], (n_moe, D_MODEL, N_EXPERTS), D_MODEL),
        "e_w1": normal(ks[17], (n_moe, N_EXPERTS, D_MODEL, D_FF_EXPERT), D_MODEL),
        "e_w3": normal(ks[18], (n_moe, N_EXPERTS, D_MODEL, D_FF_EXPERT), D_MODEL),
        "e_w2": normal(ks[19], (n_moe, N_EXPERTS, D_FF_EXPERT, D_MODEL), D_FF_EXPERT, res),
        "g_final": norm_gain(ks[20], (D_MODEL,)),
    }

def reference(x, g_mix, w_in, g_q, g_kv, w_uq, w_ukv, rpb, g_out_a, g_out_b, g_out_c, w_o,
              g_ffn, w1, w3, w2, w_router, e_w1, e_w3, e_w2, g_final):
    for layer in range(DEPTH):
        h = rms_norm(x, g_mix[layer])
        x = x + hybrid_mixer(h, w_in[layer], g_q[layer], g_kv[layer], w_uq[layer], w_ukv[layer], rpb[layer],
                             g_out_a[layer], g_out_b[layer], g_out_c[layer], w_o[layer])
        h = rms_norm(x, g_ffn[layer])
        j = layer // 2
        if layer % 2 == 0:
            x = x + swiglu(h, w1[j], w3[j], w2[j])
        else:
            x = x + moe_swiglu(h, w_router[j], e_w1[j], e_w3[j], e_w2[j])
    return rms_norm(x, g_final)


_drawn_inputs = setup_inputs


def setup_inputs(seed=0):
    import zlib

    import numpy as np

    out = dict(_drawn_inputs(seed))
    spreads = {}
    factors = {'g_q': 5.59,
     'g_kv': 3.313,
     'g_out_a': 4.992,
     'g_out_b': 4.04,
     'g_out_c': 5.026,
     'g_ffn': 3.173,
     'g_final': 2.965}
    for name, (base, spread) in spreads.items():
        noise = np.random.default_rng([zlib.crc32(name.encode()), seed]).standard_normal(out[name].shape)
        drawn = base * np.exp(spread * noise) if base else spread * noise
        out[name] = __import__('jax').numpy.asarray(drawn.astype(out[name].dtype))
    for name, factor in factors.items():
        out[name] = (out[name] * factor).astype(out[name].dtype)
    return out
```

```python
from contextlib import ExitStack

import concourse.bass as bass
from concourse import mybir

F32 = mybir.dt.float32
U32 = mybir.dt.uint32
I32 = mybir.dt.int32
ALU = mybir.AluOpType
ACT = mybir.ActivationFunctionType
AX = mybir.AxisListType

P = 128
SEQ, D, LAYERS = 512, 1024, 2
NT = SEQ // P
ND = D // P
HD = 64
HA, HB, HC = 6, 6, 4
NH = HA + HB + HC
RQ, RKV, ROPE = 384, 256, 32
QKB = HD + ROPE
WA, WB, WC = HA * HD, HB * HD, HC * HD
IN_COLS = 3 * WA + RQ + RKV + ROPE + 3 * WC
COL_QA, COL_KA, COL_VA = 0, WA, 2 * WA
COL_B = 3 * WA
COL_QC = COL_B + RQ + RKV + ROPE
COL_KC, COL_VC = COL_QC + WC, COL_QC + 2 * WC
DB = RQ + RKV + ROPE
DFF = 2816
NE, DFE = 8, 3584
GRID, NAR, NAC = 64, 8, 16
EPS = 1e-6
NEG = -1e30
STRIP = 2 * SEQ - P
UNIT = 2 * P
NU = (2 * SEQ) // UNIT + NE - 1
PADW = 128
RING = 6144

T_ID = 0
T_COS = T_ID + P
T_SIN = T_COS + NT * HB * 16
T_DIST = T_SIN + NT * HB * 16
T_AMASK = T_DIST + STRIP
T_CMASK = T_AMASK + STRIP
T_TRI = T_CMASK + GRID
T_ONES = T_TRI + P
T_UNIT = T_ONES + P
T_E = T_UNIT + NU * NE
T_W = T_E + NE

PAIRS = [("A", 0), ("A", 1), ("A", 2), ("B", 0), ("B", 1), ("B", 2), ("C", 0), ("C", 1)]
STEPS = NH * NT
FT = DFF // P
FE = DFE // P
UPS = 7
BACK = [3, 3, 3, 7, 4, 4, 4]
SILU_AT = [0, 1, 0, 1, 0, 1, 2]
CLASSES = [128, 144, 160, 176, 192, 256]
CH = DFF // UNIT
SLOPES = [2.0 ** (-8.0 * (h + 1) / HA) for h in range(HA)]
QSCALE = {"A": HD ** -0.5, "B": QKB ** -0.5, "C": HD ** -0.5}
ROT = 6


def front_jobs():
    j = [(("hT", t, i), "AD"[i]) for t in range(NT) for i in range(2)]
    j += [(("cb", t, i), "AD"[i]) for t in range(NT) for i in range(2)]
    j += [(("v", t, i), "AD"[i]) for t in range(NT) for i in range(2)]
    j += [(("cT", t, i), "AD"[i]) for t in range(NT) for i in range(2)]
    j += [(("qn", t, i), "A") for t in range(NT) for i in range(2)]
    j += [(("kvn", t, i), "D") for t in range(NT) for i in range(2)]
    j += prep_jobs(0)
    j += [(("S", 0), "D"), (("S", 1), "D")]
    for g in range(STEPS):
        if g + 2 < STEPS:
            j.append((("S", g + 2), "X" if PAIRS[(g + 2) // 8][0] == "B" else "D"))
        j.append((("PT", g), "AD"[g % 2]))
        p, k = g // 8, g % 8
        if p + 1 < len(PAIRS):
            j += prep_at(p + 1, k)
    j += [(("yT", t, i), "AD"[i]) for t in range(NT) for i in range(2)]
    j += [(("op", t, i), "D") for i in range(2) for t in range(NT)]
    j += [(("h2", t, i), "AD"[i]) for t in range(NT) for i in range(2)]
    return j


def prep_jobs(p):
    if PAIRS[p][0] == "B":
        return [(("qk", p, w, i), "AD"[w]) for i in range(2) for w in range(2)]
    return [(("qk", p, w), "AD"[w]) for w in range(2)]


def prep_at(p, k):
    js = prep_jobs(p)
    at = [1, 2, 3, 4] if len(js) == 4 else [1, 3]
    return [js[at.index(k)]] if k in at else []


def dense_jobs():
    j = [((m, f), "AD"[m == "u"]) for f in range(FT) for m in ("g", "u")]
    j += [(("d", i, t), "D") for i in range(2) for t in range(NT)]
    return j


def moe_front_jobs():
    return [(("lg", t), "D") for t in range(NT)] + [(("rk",), "D"), (("ct",), "D")]


class Jobs:

    def __init__(self):
        self.at, self.who, self.nth, self.count = {}, [], [], {"A": 0, "D": 0, "X": 0}
        self.exps = 0
        for l in range(LAYERS):
            for name, who in front_jobs() + (dense_jobs() if l == 0 else moe_front_jobs()):
                self.at[(l,) + name] = len(self.who)
                self.who.append(who)
                if who == "X":
                    self.nth.append(l * STEPS + name[1] + 1)
                else:
                    self.count[who] += 1
                    self.nth.append(self.count[who])
        self.n = len(self.who)

    def bank(self, *name):
        return self.at[name] % ROT

    def filled(self, *name):
        return self.at[name] + 1

    def emptied(self, *name):
        return self.nth[self.at[name]]


def trunk(nc, a):
    J = Jobs()
    ctx = ExitStack()
    with ctx:
        def sb(name, cols, dt=F32, rows=P):
            return ctx.enter_context(nc.sbuf_tensor(name, [rows, cols], dt))

        def sem(name):
            return ctx.enter_context(nc.semaphore(name))

        ps = ctx.enter_context(nc.psum_tensor("ps", [P, 8, 512], F32))
        x = sb("x_rows", NT * D)
        hT = sb("hT", ND * SEQ)
        ring = sb("weight_ring", 2 * RING)
        gains = sb("gains", 3 * D + RQ + RKV)
        tab = sb("tables", T_W)
        small = sb("small", 256)
        A0 = sb("attention_arena", 25472)
        off = [0]

        def part(n):
            s = off[0]
            off[0] += n
            assert off[0] <= 25472, off[0]
            return A0[:, s:s + n]

        qk = part(2 * 2 * 2 * SEQ)
        kvn = part(NT * HB * 160)
        qn = part(NT * HB * QKB)
        lat = part(NT * DB + 5 * SEQ)
        vac = part(NT * (WA + WC))
        soft = part(7 * SEQ)
        strips = part(2 * STRIP)
        hrow = part(2 * D)

        x3 = x[:, :].rearrange("p (t d) -> p t d", t=NT)
        hT3 = hT[:, :].rearrange("p (k s) -> p k s", k=ND)
        qk5 = qk.rearrange("p (b w h s) -> p b w h s", b=2, w=2, h=2)
        kvn4 = kvn.rearrange("p (t h c) -> p t h c", t=NT, h=HB)
        qn4 = qn.rearrange("p (t h c) -> p t h c", t=NT, h=HB)
        cn = lat[:, 0:NT * DB].rearrange("p (t c) -> p t c", t=NT)
        cT = lat[:, NT * DB:].rearrange("p (k s) -> p k s", k=5)
        on = lat[:, 0:NT * D].rearrange("p (t d) -> p t d", t=NT)
        vac3 = vac.rearrange("p (t c) -> p t c", t=NT)
        pr = soft[:, 0:3 * SEQ].rearrange("p (b s) -> p b s", b=3)
        pt = soft[:, 3 * SEQ:5 * SEQ].rearrange("p (b s) -> p b s", b=2)
        sc = soft[:, 5 * SEQ:7 * SEQ].rearrange("p (b s) -> p b s", b=2)
        st = strips.rearrange("p (b s) -> p b s", b=2)
        hr = hrow.rearrange("p (b d) -> p b d", b=2)
        g_mix, g_ffn, g_out = (gains[:, i * D:(i + 1) * D] for i in range(3))
        g_q = gains[:, 3 * D:3 * D + RQ]
        g_kv = gains[:, 3 * D + RQ:3 * D + RQ + RKV]
        ident = tab[:, T_ID:T_ID + P]
        ones = tab[:, T_ONES:T_ONES + P]
        tri = tab[:, T_TRI:T_TRI + P]
        hid = A0[:, 0:FT * SEQ].rearrange("p (f s) -> p f s", f=FT)
        sil = A0[:, FT * SEQ:(FT + 2) * SEQ].rearrange("p (b s) -> p b s", b=2)

        ssq = small[:, 0:12]
        rms = small[:, 12:24]
        rr = small[:, 24:36]
        mx = small[:, 36:40]
        nmx = small[:, 40:44]
        ls = small[:, 44:52].rearrange("p (b t) -> p b t", b=2)
        rl = small[:, 52:60].rearrange("p (b t) -> p b t", b=2)

        eh = A0[:, 0:FE * UNIT].rearrange("p (f s) -> p f s", f=FE)
        yT = A0[:, 7168:7168 + 2048].rearrange("p (k s) -> p k s", k=ND)
        esil = A0[:, 9216:9216 + 3 * UNIT].rearrange("p (b s) -> p b s", b=3)
        h4 = on
        rows = A0[:, 14336:16384].rearrange("p (b d) -> p b d", b=2)
        yrow = A0[:, 16384:18432].rearrange("p (b d) -> p b d", b=2)
        up_at = [ring[:, 7168 + 2048 * i:7168 + 2048 * (i + 1)] for i in range(2)] \
            + [A0[:, 18432 + 2048 * i:18432 + 2048 * (i + 1)] for i in range(3)] \
            + [A0[:, 10240 + 2048 * i:10240 + 2048 * (i + 1)] for i in range(2)]
        up = [v.rearrange("p (m k c) -> p m k c", m=2, k=ND) for v in up_at]
        down = [ring[:, 3584 * i:3584 * (i + 1)].rearrange("p (f c) -> p f c", f=FE) for i in range(2)]
        XT = hT[:, 0:ND * UNIT].rearrange("p (k s) -> p k s", k=ND)
        back = A0[:, 0:8 * D].rearrange("p (n d) -> p n d", n=2 * NT)
        used = [0]

        def rt(*shape):
            n = 1
            for d in shape:
                n *= d
            v = gains[:, 2 * D + used[0]:2 * D + used[0] + n]
            used[0] += n
            return v.rearrange("p (a b) -> p a b", a=shape[0]) if len(shape) == 2 else v

        logit, top, lot0, lot1, both = (rt(NT, NE) for _ in range(5))
        pick = rt(NT * NE).bitcast(U32).rearrange("p (t e) -> p t e", t=NT)
        rank, hit = rt(NT, NE), rt(NT, NE)
        pickf, slotf = rt(NT, 2), rt(NT, 2)
        gap, eg, den, g0, g1 = (rt(NT) for _ in range(5))
        cnt, more, units, incl, excl, first, tot = (rt(NE) for _ in range(7))
        past, owns, left = rt(NU, NE), rt(NU, NE), rt(NU, NE)
        planf = rt(3 * NU + 2)
        plan = rt(3 * NU + 2).bitcast(I32)
        slot = rt(NT * 2).bitcast(U32)
        wr = rt(ND * NE).rearrange("p (k e) -> p k e", k=ND)

        rows_dram = nc.dram_tensor("rows_by_slot", [(NU + 1) * UNIT, D], F32).ap()
        y_dram = nc.dram_tensor("results_by_slot", [NU * UNIT, D], F32).ap()

        pad_dram = nc.dram_tensor("padded_bias", [GRID, LAYERS * HC * 15, PADW], F32).ap()

        loaded = [sem("ring_loaded_0"), sem("ring_loaded_1")]
        tab_in, x_in, gains_in = sem("tables_loaded"), sem("x_loaded"), sem("gains_loaded")
        rpb_in, pad_set, pad_out = sem("position_bias_loaded"), sem("pad_set"), sem("pad_stored")
        filled = sem("banks_filled")
        emptied = {"A": sem("banks_emptied_by_act"), "D": sem("banks_emptied_by_dve"), "X": sem("exponentials_done")}
        sq_done, rms_ready = sem("square_sums_done"), sem("rms_ready")
        h_ready = sem("normed_rows_ready")
        lat_ready = sem("latents_normed")
        rope_ready = sem("rope_done")
        nmax_ready = sem("row_maxima_ready")
        pv_done = sem("head_steps_accumulated")
        o_out = sem("head_outputs_stored")
        strip_ready, strip_in, strip_half = sem("strips_ready"), sem("strips_loaded"), sem("strip_half_built")
        y_ready = sem("group_rows_ready")
        gains_free = sem("gains_free")
        dve_link = sem("dve_order")
        out_done = sem("output_stored")
        silu_done = sem("silu_done")
        fin_ready = sem("final_rows_ready")

        filled_before, router_in = sem("rows_filled_before_scatter"), sem("router_loaded")
        gates_sub, gates_exp, lots_ready = sem("gate_gap_ready"), sem("gate_exp_done"), sem("lots_ready")
        slots_ready, plan_ready, scattered = sem("slots_ready"), sem("plan_ready"), sem("rows_scattered")
        rows_in, up_in, down_in = sem("unit_rows_loaded"), [sem(f"up_loaded_{i}") for i in range(UPS)], \
            [sem(f"down_loaded_{i}") for i in range(2)]
        turned, turn_out = sem("unit_turns_filled"), sem("unit_turns_emptied")
        gu_filled, e_silu, gu_free = sem("gate_up_filled"), sem("expert_silu_done"), sem("gate_up_banks_given")
        y_filled, y_out, y_stored = sem("unit_results_filled"), sem("unit_results_emptied"), sem("results_stored")
        gathered, final_gain, idle_set = sem("results_gathered"), sem("final_gain_loaded"), sem("idle_rows_set")

        entries = []

        def wsrc(ap, c0, n):
            return ap[:, c0:c0 + n].rearrange("(k p) c -> p k c", p=P)

        def entry(key, loads, last):
            entries.append((key, loads, last))

        for l in range(LAYERS):
            w_in, w_uq, w_ukv, w_o = (a[n][l] for n in ("w_in", "w_uq", "w_ukv", "w_o"))
            entry((l, "b"), [(0, 8, DB, wsrc(w_in, COL_B, DB))], (l, "cb", NT - 1, 1))
            entry((l, "v"), [(0, 8, WA, wsrc(w_in, COL_VA, WA)), (8 * WA, 8, WC, wsrc(w_in, COL_VC, WC))],
                  (l, "v", NT - 1, 1))
            entry((l, "uq"), [(0, 3, HB * QKB, wsrc(w_uq, 0, HB * QKB)),
                              (3 * HB * QKB, 2, HB * P, wsrc(w_ukv, 0, HB * P))], (l, "kvn", NT - 1, 1))
            entry((l, "qkA"), [(0, 8, 2 * WA, wsrc(w_in, COL_QA, 2 * WA))], (l, "qk", 2, 1))
            entry((l, "qkC"), [(0, 8, 2 * WC, wsrc(w_in, COL_QC, 2 * WC))], (l, "qk", 7, 1))
            for i in range(2):
                entry((l, "o", i), [(0, 8, 512, wsrc(w_o, 512 * i, 512))], (l, "op", NT - 1, i))
            if l == 0:
                w1, w3, w2 = a["w1"][0], a["w3"][0], a["w2"][0]
                for c in range(CH):
                    entry((l, "f", c), [(0, 8, UNIT, wsrc(w1, UNIT * c, UNIT)),
                                        (8 * UNIT, 8, UNIT, wsrc(w3, UNIT * c, UNIT))], (l, "u", 2 * c + 1))
                for i in range(2):
                    for c in range(2):
                        entry((l, "w2", i, c),
                              [(0, FT // 2, 512, w2[c * DFF // 2:(c + 1) * DFF // 2, 512 * i:512 * i + 512]
                                .rearrange("(k p) c -> p k c", p=P))], (l, "d", i, NT - 1))
        n_of = {e[0]: n for n, e in enumerate(entries)}
        loads_to = [0, 0]
        full_at = []
        for n, e in enumerate(entries):
            loads_to[n % 2] += 16 * len(e[1])
            full_at.append(loads_to[n % 2])

        def wview(key, i=0):
            n = n_of[key]
            o, k, c, _ = entries[n][1][i]
            s = (n % 2) * RING + o
            return ring[:, s:s + k * c].rearrange("p (k c) -> p k c", k=k)

        def layer_gains(l):
            return [(g_mix, a["g_mix"][l]), (g_ffn, a["g_ffn"][l]),
                    (g_out[:, 0:WA], a["g_out_a"][l]), (g_out[:, WA:WA + WB], a["g_out_b"][l]),
                    (g_out[:, WA + WB:], a["g_out_c"][l]), (g_q, a["g_q"][l]), (g_kv, a["g_kv"][l])]

        NG = 7

        block = ctx.enter_context(nc.Block())

        @block.sync
        def _(sp):
            for t in range(NT):
                sp.dma_start(x3[:, t, :], a["x"][0, t * P:(t + 1) * P, :]).then_inc(x_in, 16)
            for n, (key, loads, last) in enumerate(entries):
                if n >= 2:
                    sp.wait_ge(filled, J.filled(*entries[n - 2][2]))
                for (o, k, c, src) in loads:
                    s = (n % 2) * RING + o
                    sp.dma_start(ring[:, s:s + k * c].rearrange("p (k c) -> p k c", k=k), src)\
                        .then_inc(loaded[n % 2], 16)
                if n == 0:
                    sp.dma_start(tab[:, :], a["tables"]).then_inc(tab_in, 16)
            sp.wait_ge(router_in, 16)
            L = LAYERS - 1
            sp.wait_ge(filled, J.filled(L, "h2", NT - 1, 1))
            sp.wait_ge(plan_ready, 1)
            n_units = sp.value_load(plan[0:1, 2 * NU:2 * NU + 1], min_val=1, max_val=NU)

            def load_up(e, u, f, s):
                sp.wait_ge(gu_filled, u * FE + f + 1)
                for m, n in ((0, "e_w1"), (1, "e_w3")):
                    sp.dma_start(up[s][:, m, :, :],
                                 a[n][0][e][:, bass.ds(f * P, P)].rearrange("(k p) c -> p k c", p=P))\
                        .then_inc(up_in[s], 16)

            def load_down(e, u, d, s):
                sp.wait_ge(y_filled, u * ND + d + 1)
                sp.dma_start(down[s], a["e_w2"][0][e][:, bass.ds(d * P, P)].rearrange("(f p) c -> p f c", p=P))\
                    .then_inc(down_in[s], 16)

            e0 = sp.value_load(plan[0:1, 0:1], min_val=0, max_val=NE - 1)
            for s in range(5):
                load_up(e0, 0, s, s)
            sp.wait_ge(scattered, 16 * 2 * NT)
            for s in range(5, UPS):
                load_up(e0, 0, s, s)
            with sp.Fori(0, NU) as u:
                with sp.If(u < n_units):
                    e = sp.value_load(plan[0:1, bass.ds(u, 1)], min_val=0, max_val=NE - 1)
                    nxt = sp.value_load(plan[0:1, bass.ds(u + 2 * NU + 1, 1)], min_val=0, max_val=NE - 1)
                    for s in range(2):
                        load_down(e, u, s, s)
                    with sp.Fori(1, FE // UPS) as i:
                        for s in range(UPS):
                            load_up(e, u, i * UPS + s, s)
                    for j in range(ND // 2):
                        if j:
                            for s in range(2):
                                load_down(e, u, 2 * j + s, s)
                        with sp.If(u + 1 < n_units):
                            for s in range(2 * j, min(2 * j + 2, UPS)):
                                load_up(nxt, u + 1, s, s)
                    sp.sem_inc(idle_set, 16)
                with sp.Else():
                    sp.dma_start(y_dram[bass.ds(u * UNIT, UNIT), :], a["x"][0][0:UNIT, :]).then_inc(idle_set, 16)
            sp.wait_ge(fin_ready, 1)
            sp.dma_start(a["out"][0].rearrange("(t p) d -> p t d", p=P), x3).then_inc(out_done, 16)
            sp.wait_ge(out_done, 16)

        @block.gpsimd
        def _(pool):
            padt = st[0:LAYERS * HC * 15, 0, 0:PADW]
            nc.gpsimd.memset(padt, NEG).then_inc(pad_set, 1)
            pool.wait_ge(pad_set, 1)
            pool.dma_start(padt[:, 48:48 + 31], a["rpb"].rearrange("l h r c -> (l h r) c")).then_inc(rpb_in, 16)
            for dst, src in layer_gains(0):
                pool.dma_start(dst, src.partition_broadcast(P)).then_inc(gains_in, 16)
            pool.wait_ge(rpb_in, 16)
            pool.dma_start(pad_dram.rearrange("c r w -> r c w"),
                           padt.unsqueeze(1).to_broadcast([LAYERS * HC * 15, GRID, PADW])).then_inc(pad_out, 16)
            pool.wait_ge(tab_in, 16)
            pool.wait_ge(pad_out, 16)
            halves = 0
            for l in range(LAYERS):
                for n in range(HA + HC):
                    if l or n >= 2:
                        m = l * (HA + HC) + n - 2
                        ll, mm = divmod(m, HA + HC)
                        last = (mm if mm < HA else mm + HB) * NT + NT - 1
                        pool.wait_ge(emptied["D"], J.emptied(ll, "S", last))
                    buf = st[:, n % 2, :]
                    if n < HA:
                        nc.gpsimd.tensor_scalar(buf, tab[:, T_DIST:T_DIST + STRIP], -SLOPES[n], None, ALU.mult)\
                            .then_inc(strip_half, 1)
                        halves += 1
                        pool.wait_ge(strip_half, halves)
                        nc.gpsimd.tensor_tensor(buf, buf, tab[:, T_AMASK:T_AMASK + STRIP], ALU.add)\
                            .then_inc(strip_ready, 1)
                    else:
                        h = n - HA
                        for r in range(2):
                            row = (l * HC + h) * 15 + 1 - r
                            src = bass.AP(tensor=pad_dram.tensor, offset=row * PADW + 63,
                                          ap=[[LAYERS * HC * 15 * PADW - 1, GRID], [PADW, 14], [1, GRID]])
                            pool.dma_start(buf[r * GRID:(r + 1) * GRID, :]
                                           .rearrange("p (a c) -> p a c", a=14), src).then_inc(strip_in, 16)
                        pool.wait_ge(strip_in, 32 * (l * HC + h + 1))
                        b3 = buf.rearrange("p (a c) -> p a c", a=14)
                        cm = tab[:, T_CMASK:T_CMASK + GRID].unsqueeze(1).to_broadcast([P, 14, GRID])
                        nc.gpsimd.tensor_tensor(b3, b3, cm, ALU.add).then_inc(strip_ready, 1)
                if l == 0:
                    for i in range((NU + 1) * UNIT // SEQ):
                        pool.dma_start(rows_dram[i * SEQ:(i + 1) * SEQ, :], a["x"][0]).then_inc(filled_before, 16)
                    pool.wait_ge(gains_free, 1)
                    for dst, src in layer_gains(1):
                        pool.dma_start(dst, src.partition_broadcast(P)).then_inc(gains_in, 16)

            pool.wait_ge(y_ready, LAYERS * NT)
            pool.dma_start(wr, a["w_router"][0].rearrange("(k p) e -> p k e", p=P)).then_inc(router_in, 16)
            pool.dma_start(g_mix, a["g_final"].partition_broadcast(P)).then_inc(final_gain, 16)
            pool.wait_ge(filled_before, 16 * ((NU + 1) * UNIT // SEQ))
            pool.wait_ge(h_ready, 2 * LAYERS * NT)
            pool.wait_ge(slots_ready, 1)
            for t in range(NT):
                for j in range(2):
                    pool.indirect_dma_start(rows_dram, bass.IndirectOffsetOnAxis(ap=slot[:, 2 * t + j:2 * t + j + 1], axis=0),
                                            h4[:, t, :], None).then_inc(scattered, 16)
            pool.wait_ge(plan_ready, 1)
            n_units = pool.value_load(plan[0:1, 2 * NU:2 * NU + 1], min_val=1, max_val=NU)
            pool.wait_ge(scattered, 16 * 2 * NT)
            pool.dma_start(rows, rows_dram[0:UNIT, :].rearrange("(b p) d -> p b d", p=P)).then_inc(rows_in, 16)
            with pool.Fori(0, NU) as u:
                with pool.If(u < n_units):
                    pool.wait_ge(turned, u * 8 + 4)
                    pool.dma_start(rows, rows_dram[bass.ds(u * UNIT + UNIT, UNIT), :]
                                   .rearrange("(b p) d -> p b d", p=P)).then_inc(rows_in, 16)
            pool.wait_ge(y_stored, n_units * 16 + 16)
            pool.sem_inc(idle_set, 16)
            pool.wait_ge(idle_set, NU * 16 + 16)
            for t in range(NT):
                for j in range(2):
                    pool.indirect_dma_start(back[:, 2 * t + j, :], None, y_dram,
                                            bass.IndirectOffsetOnAxis(ap=slot[:, 2 * t + j:2 * t + j + 1], axis=0))\
                        .then_inc(gathered, 16)
            pool.wait_ge(gathered, 16 * 2 * NT)

        @block.tensor
        def _(pe):
            pe.wait_ge(tab_in, 16)

            def take(*name):
                n = J.at[name]
                if n >= ROT:
                    pe.wait_ge(emptied[J.who[n - ROT]], J.nth[n - ROT])
                return ps[:, n % ROT, :]

            def arrived(key):
                n = n_of[key]
                pe.wait_ge(loaded[n % 2], full_at[n])

            def emptied_upto(*name):
                pe.wait_ge(emptied[J.who[J.at[name]]], J.emptied(*name))

            def turn(job, srcs):
                b = take(*job)
                for i, s in enumerate(srcs):
                    w = s.shape[1]
                    last = nc.tensor.transpose(b[0:w, i * P:(i + 1) * P], s, ident)
                last.then_inc(filled, 1)

            def rows_times(job, lhsT, w, kt, t, c0, n):
                b = take(*job)
                for k in range(kt):
                    last = nc.tensor.matmul(b[:, 0:n], lhsT[:, k, t * P:(t + 1) * P], w[:, k, c0:c0 + n],
                                            start=(k == 0), stop=(k == kt - 1))
                last.then_inc(filled, 1)

            def cols_times(job, w, c0):
                b = take(*job)
                for k in range(ND):
                    last = nc.tensor.matmul(b[:, :], w[:, k, c0:c0 + P], hT3[:, k, :],
                                            start=(k == 0), stop=(k == ND - 1))
                last.then_inc(filled, 1)

            def norm_turn(l, name):
                keep = l == LAYERS - 1 and name == "h2"
                for t in range(NT):
                    pe.wait_ge(h_ready, (2 * l + (name == "h2")) * NT + t + 1)
                    for i in range(2):
                        row = h4[:, t, :] if keep else hr[:, t % 2, :]
                        turn((l, name, t, i), [row[:, (4 * i + k) * P:(4 * i + k + 1) * P] for k in range(4)])
                emptied_upto(l, name, NT - 1, 0)
                emptied_upto(l, name, NT - 1, 1)

            def prep(l, name):
                p, w = name[1], name[2]
                kind, pp = PAIRS[p]
                if kind == "B":
                    h = 2 * pp + name[3]
                    src = kvn4 if w else qn4
                    turn((l,) + name, [src[:, t, h, 0:QKB] for t in range(NT)])
                    return
                key = (l, "qk" + kind)
                arrived(key)
                cols_times((l,) + name, wview(key), (WA if kind == "A" else WC) * w + P * pp)

            for l in range(LAYERS):
                norm_turn(l, "hT")
                arrived((l, "b"))
                wb = wview((l, "b"))
                for t in range(NT):
                    rows_times((l, "cb", t, 0), hT3, wb, ND, t, 0, RQ)
                    rows_times((l, "cb", t, 1), hT3, wb, ND, t, RQ, RKV + ROPE)
                arrived((l, "v"))
                for t in range(NT):
                    rows_times((l, "v", t, 0), hT3, wview((l, "v"), 0), ND, t, 0, WA)
                    rows_times((l, "v", t, 1), hT3, wview((l, "v"), 1), ND, t, 0, WC)
                for t in range(NT):
                    pe.wait_ge(lat_ready, l * NT + t + 1)
                    turn((l, "cT", t, 0), [cn[:, t, k * P:(k + 1) * P] for k in range(3)])
                    turn((l, "cT", t, 1), [cn[:, t, (3 + k) * P:(4 + k) * P] for k in range(2)])
                arrived((l, "uq"))
                emptied_upto(l, "cT", NT - 1, 0)
                emptied_upto(l, "cT", NT - 1, 1)
                for t in range(NT):
                    for i in range(2):
                        rows_times((l, "qn", t, i), cT[:, 0:3, :], wview((l, "uq"), 0), 3, t, 3 * QKB * i, 3 * QKB)
                for t in range(NT):
                    for i in range(2):
                        rows_times((l, "kvn", t, i), cT[:, 3:5, :], wview((l, "uq"), 1), 2, t, 3 * P * i, 3 * P)
                for name, _ in prep_jobs(0):
                    prep(l, name)

                def scores(g):
                    h, t = divmod(g, NT)
                    p, i = divmod(h, 2)
                    kind = PAIRS[p][0]
                    rows = QKB if kind == "B" else HD
                    if t == 0:
                        for name, _ in prep_jobs(p):
                            emptied_upto(l, *name)
                    b = take(l, "S", g)
                    nc.tensor.matmul(b[:, :], qk5[0:rows, p % 2, 0, i, t * P:(t + 1) * P],
                                     qk5[0:rows, p % 2, 1, i, :], start=True, stop=True).then_inc(filled, 1)

                scores(0)
                scores(1)
                def weigh(g):
                    h, t = divmod(g, NT)
                    p, i = divmod(h, 2)
                    kind, pp = PAIRS[p]
                    emptied_upto(l, "PT", g)
                    if t == 0 and l * NH + h >= 2:
                        pe.wait_ge(o_out, l * NH + h - 1)
                    ob = ps[:, ROT + h % 2, :]
                    for k in range(NT):
                        if kind == "B":
                            v = kvn4[:, k, 2 * pp + i, HD:160]
                        else:
                            c = P * pp + (WA if kind == "C" else 0)
                            v = vac3[:, k, c:c + P]
                        last = nc.tensor.matmul(ob[:, t * P:t * P + v.shape[1]], pt[:, g % 2, k * P:(k + 1) * P], v,
                                                start=(k == 0), stop=(k == NT - 1))
                    last.then_inc(pv_done, 1)

                for g in range(STEPS):
                    p = g // 8
                    if g + 2 < STEPS:
                        scores(g + 2)
                    pe.wait_ge(emptied["X"], l * STEPS + g + 1)
                    turn((l, "PT", g), [pr[:, g % 3, k * P:(k + 1) * P] for k in range(NT)])
                    if g:
                        weigh(g - 1)
                    if p + 1 < len(PAIRS):
                        for name, _ in prep_at(p + 1, g % 8):
                            if PAIRS[p + 1][0] == "B":
                                pe.wait_ge(rope_ready, l + 1)
                            prep(l, name)
                weigh(STEPS - 1)
                for t in range(NT):
                    pe.wait_ge(y_ready, l * NT + t + 1)
                    for i in range(2):
                        turn((l, "yT", t, i), [on[:, t, (4 * i + k) * P:(4 * i + k + 1) * P] for k in range(4)])
                emptied_upto(l, "yT", NT - 1, 0)
                emptied_upto(l, "yT", NT - 1, 1)
                for i in range(2):
                    arrived((l, "o", i))
                    for t in range(NT):
                        rows_times((l, "op", t, i), hT3, wview((l, "o", i)), ND, t, 0, 512)
                norm_turn(l, "h2")
                if l == 0:
                    for c in range(CH):
                        arrived((l, "f", c))
                        for f in (2 * c, 2 * c + 1):
                            cols_times((l, "g", f), wview((l, "f", c), 0), (f % 2) * P)
                            cols_times((l, "u", f), wview((l, "f", c), 1), (f % 2) * P)
                    for i in range(2):
                        banks = [take(l, "d", i, t) for t in range(NT)]
                        for f in range(FT):
                            c, k = divmod(f, FT // 2)
                            if k == 0:
                                arrived((l, "w2", i, c))
                            if i == 0:
                                emptied_upto(l, "u", f)
                            for t in range(NT):
                                last = nc.tensor.matmul(banks[t], hid[:, f, t * P:(t + 1) * P],
                                                        wview((l, "w2", i, c))[:, k, :],
                                                        start=(f == 0), stop=(f == FT - 1))
                                if f == FT - 1:
                                    last.then_inc(filled, 1)

            l = LAYERS - 1
            pe.wait_ge(router_in, 16)
            for t in range(NT):
                rows_times((l, "lg", t), hT3, wr, ND, t, 0, NE)
            pe.wait_ge(lots_ready, 1)
            b = take(l, "rk")
            for t in range(NT):
                for s in range(t + 1):
                    last = nc.tensor.matmul(b[:, t * NE:(t + 1) * NE], tri if s == t else ones, both[:, s, :],
                                            start=(s == 0), stop=(s == t))
            last.then_inc(filled, 1)
            b = take(l, "ct")
            for s in range(NT):
                last = nc.tensor.matmul(b[:, 0:NE], ones, both[:, s, :], start=(s == 0), stop=(s == NT - 1))
            last.then_inc(filled, 1)

            pe.wait_ge(plan_ready, 1)
            pe.wait_ge(emptied["D"], J.emptied(l, "ct"))
            pe.sem_inc(gu_filled, UPS)
            pe.sem_inc(y_filled, 2)
            n_units = pe.value_load(plan[0:1, 2 * NU:2 * NU + 1], min_val=1, max_val=NU)

            def unit_body(u, n):
                with pe.Fori(0, FE // UPS) as i:
                    for s in range(UPS):
                        f = u * FE + i * UPS + s
                        if s == 0:
                            pe.wait_ge(turn_out, u * 8 + 6)
                        pe.wait_ge(up_in[s], (u * (FE // UPS) + i + 1) * 32)
                        pe.wait_ge(gu_free, f + 5 - BACK[s])
                        gb = ps[:, s % 4, :]
                        for m in range(2):
                            for k in range(ND):
                                last = nc.tensor.matmul(gb[:, m * UNIT:m * UNIT + n], up[s][:, m, k, :], XT[:, k, 0:n],
                                                        start=(k == 0), stop=(k == ND - 1))
                        last.then_inc(gu_filled, 1)
                with pe.Fori(0, ND // 2) as j:
                    for s in range(2):
                        if s == 0:
                            pe.wait_ge(gu_free, u * FE + FE + 4)
                        pe.wait_ge(down_in[s], (u * (ND // 2) + j + 1) * 16)
                        pe.wait_ge(y_out, u * ND + j * 2 + s + 1)
                        for f in range(FE):
                            last = nc.tensor.matmul(ps[:, 4 + s, 0:n], down[s][:, f, :], eh[:, f, 0:n],
                                                    start=(f == 0), stop=(f == FE - 1))
                        last.then_inc(y_filled, 1)

            def choose(u, held, classes):
                if len(classes) == 1:
                    return unit_body(u, classes[0])
                with pe.If(held < classes[0] + 1):
                    unit_body(u, classes[0])
                with pe.Else():
                    choose(u, held, classes[1:])

            def turn_rows(after):
                for i in range(4):
                    pe.wait_ge(turn_out, after + i + 1)
                    for k in range(2):
                        for r in range(2):
                            last = nc.tensor.transpose(ps[:, 6 + i % 2, (2 * k + r) * P:(2 * k + r + 1) * P],
                                                       rows[:, r, (2 * i + k) * P:(2 * i + k + 1) * P], ident)
                    last.then_inc(turned, 1)

            pe.wait_ge(rows_in, 16)
            turn_rows(0)
            with pe.Fori(0, NU) as u:
                with pe.If(u < n_units):
                    held = pe.value_load(plan[0:1, bass.ds(u + NU, 1)], min_val=0, max_val=UNIT)
                    choose(u, held, CLASSES)
                    pe.wait_ge(rows_in, u * 16 + 32)
                    turn_rows(u * 8 + 4)
                    for i in range(4):
                        if i == 0:
                            pe.wait_ge(y_out, u * ND + ND + 2)
                        pe.wait_ge(turn_out, u * 8 + 8 + i + 1)
                        for k in range(4):
                            d = 4 * (i % 2) + k
                            last = nc.tensor.transpose(ps[:, 6 + i % 2, k * P:(k + 1) * P],
                                                       yT[:, d, (i // 2) * P:(i // 2 + 1) * P], ident)
                        last.then_inc(turned, 1)

        @block.scalar
        def _(act):
            def bank(*name):
                act.wait_ge(filled, J.filled(*name))
                return ps[:, J.bank(*name), :]

            def copy_out(dst, job, n=512):
                nc.scalar.copy(dst, bank(*job)[:, 0:n]).then_inc(emptied["A"], 1)

            roots = [0]

            def root(n):
                roots[0] += 1
                act.wait_ge(sq_done, roots[0])
                nc.scalar.activation(rms[:, 0:n], ssq[:, 0:n], ACT.Sqrt).then_inc(rms_ready, 1)

            def split(job):
                l, name, t, i = job
                return hT3[:, 4 * i:4 * i + 4, t * P:(t + 1) * P]

            def prep(l, name):
                p, w = name[1], name[2]
                kind, pp = PAIRS[p]
                if kind == "B":
                    b = bank(l, *name)
                    nc.scalar.copy(qk5[0:QKB, p % 2, 0, name[3], :], b[0:QKB, :]).then_inc(emptied["A"], 1)
                    return
                b = bank(l, *name)
                for i in range(2):
                    last = nc.scalar.mul(qk5[0:HD, p % 2, 0, i, :], b[i * HD:(i + 1) * HD, :], QSCALE[kind])
                last.then_inc(emptied["A"], 1)

            def prep_mine(js, l):
                for name, who in js:
                    if who == "A":
                        prep(l, name)

            def expo(l, g):
                h, t = divmod(g, NT)
                act.wait_ge(nmax_ready, l * STEPS + g + 1)
                if l * STEPS + g >= 3:
                    ll, gg = divmod(l * STEPS + g - 3, STEPS)
                    act.wait_ge(filled, J.filled(ll, "PT", gg))
                if t == 0 and l * NH + h >= 2:
                    act.wait_ge(o_out, l * NH + h - 1)
                src = ps[:, J.bank(l, "S", g), :] if PAIRS[h // 2][0] == "B" else sc[:, g % 2, :]
                nc.scalar.activation(pr[:, g % 3, :], src, ACT.Exp, bias=nmx[:, g % 4:g % 4 + 1],
                                     accum_out=ls[:, h % 2, t:t + 1]).then_inc(emptied["X"], 1)

            for l in range(LAYERS):
                root(NT)
                for t in range(NT):
                    copy_out(split((l, "hT", t, 0)), (l, "hT", t, 0))
                for t in range(NT):
                    copy_out(cn[:, t, 0:RQ], (l, "cb", t, 0), RQ)
                root(2 * NT)
                for t in range(NT):
                    copy_out(vac3[:, t, 0:WA], (l, "v", t, 0), WA)
                for t in range(NT):
                    copy_out(cT[:, 0:3, t * P:(t + 1) * P], (l, "cT", t, 0), 3 * P)
                for t in range(NT):
                    for i in range(2):
                        b = bank(l, "qn", t, i)
                        nc.scalar.mul(qn4[:, t, 3 * i:3 * i + 3, :], b[:, 0:3 * QKB], QSCALE["B"])\
                            .then_inc(emptied["A"], 1)
                prep_mine(prep_jobs(0), l)
                expo(l, 0)
                expo(l, 1)
                for g in range(STEPS):
                    if g + 2 < STEPS:
                        expo(l, g + 2)
                    if g % 2 == 0:
                        b = bank(l, "PT", g)
                        if l * STEPS + g >= 2:
                            act.wait_ge(pv_done, l * STEPS + g - 1)
                        nc.scalar.copy(pt[:, 0, :], b).then_inc(emptied["A"], 1)
                    if g // 8 + 1 < len(PAIRS):
                        prep_mine(prep_at(g // 8 + 1, g % 8), l)
                root(3 * NT)
                for t in range(NT):
                    copy_out(split((l, "yT", t, 0)), (l, "yT", t, 0))
                root(NT)
                for t in range(NT):
                    copy_out(split((l, "h2", t, 0)), (l, "h2", t, 0))
                if l == 0:
                    for f in range(FT):
                        b = bank(l, "g", f)
                        if f >= 2:
                            act.wait_ge(emptied["D"], J.emptied(l, "u", f - 2))
                        nc.scalar.activation(sil[:, f % 2, :], b, ACT.Silu).then_inc(emptied["A"], 1)
            act.wait_ge(gates_sub, 1)
            nc.scalar.activation(eg, gap, ACT.Exp).then_inc(gates_exp, 1)
            act.wait_ge(plan_ready, 1)
            act.sem_inc(turn_out, 2)
            act.sem_inc(y_stored, 16)
            n_units = act.value_load(plan[0:1, 2 * NU:2 * NU + 1], min_val=1, max_val=NU)
            for i in range(4):
                act.wait_ge(turned, i + 1)
                nc.scalar.copy(XT[:, 2 * i:2 * i + 2, :], ps[:, 6 + i % 2, :]).then_inc(turn_out, 1)
            with act.Fori(0, NU) as u:
                with act.If(u < n_units):
                    with act.Fori(0, FE // UPS) as i:
                        for s in range(UPS):
                            act.wait_ge(gu_filled, u * FE + i * UPS + (s + 1 + UPS))
                            act.wait_ge(gu_free, u * FE + i * UPS + s + 3)
                            nc.scalar.activation(esil[:, SILU_AT[s], :], ps[:, s % 4, 0:UNIT], ACT.Silu).then_inc(e_silu, 1)
                    for i in range(4):
                        act.wait_ge(turned, u * 8 + i + 5)
                        nc.scalar.copy(XT[:, 2 * i:2 * i + 2, :], ps[:, 6 + i % 2, :]).then_inc(turn_out, 1)
                    for i in range(4):
                        act.wait_ge(turned, u * 8 + i + 9)
                        if i == 0:
                            act.wait_ge(y_stored, u * 16 + 16)
                        nc.scalar.copy(yrow[:, i // 2, (i % 2) * 512:(i % 2) * 512 + 512], ps[:, 6 + i % 2, :])\
                            .then_inc(turn_out, 1)
                    act.wait_ge(turn_out, u * 8 + 14)
                    act.dma_start(y_dram[bass.ds(u * UNIT, UNIT), :].rearrange("(b p) d -> p b d", p=P), yrow)\
                        .then_inc(y_stored, 16)
            root(NT)

        @block.vector
        def _(dve):
            links = [0]

            def link(ins):
                links[0] += 1
                ins.then_inc(dve_link, 1)
                dve.wait_ge(dve_link, links[0])

            def bank(*name):
                dve.wait_ge(filled, J.filled(*name))
                return ps[:, J.bank(*name), :]

            def copy_out(dst, job, n=512):
                nc.vector.tensor_copy(dst, bank(*job)[:, 0:n]).then_inc(emptied["D"], 1)

            def square(src, scratch, col, width):
                link(nc.vector.tensor_tensor_reduce(scratch, src, src, 1.0 / width, 0.0, ALU.mult, ALU.add,
                                                    ssq[:, col:col + 1]))

            roots = [0]

            def inverse(n):
                nc.vector.tensor_scalar(ssq[:, 0:n], ssq[:, 0:n], EPS, None, ALU.add).then_inc(sq_done, 1)
                roots[0] += 1
                dve.wait_ge(rms_ready, roots[0])
                link(nc.vector.reciprocal(rr[:, 0:n], rms[:, 0:n]))

            def norm_rows(l, name, gain):
                keep = l == LAYERS - 1 and name == "h2"
                for t in range(NT):
                    if name == "h2" and t < 2:
                        dve.wait_ge(filled, J.filled(l, "hT", t + 2, 1))
                    elif l and t < 2:
                        dve.wait_ge(filled, J.filled(l - 1, "h2", t + 2, 1))
                    square(x3[:, t, :], hr[:, t % 2, :], t, D)
                inverse(NT)
                for t in range(NT):
                    if t >= 2:
                        dve.wait_ge(filled, J.filled(l, name, t - 2, 1))
                    nc.vector.scalar_tensor_tensor(out=h4[:, t, :] if keep else hr[:, t % 2, :], in0=x3[:, t, :], scalar=rr[:, t:t + 1],
                                                   in1=gain, op0=ALU.mult, op1=ALU.mult).then_inc(h_ready, 1)
                    if t >= 1:
                        copy_out(hT3[:, 4:8, (t - 1) * P:t * P], (l, name, t - 1, 1))
                copy_out(hT3[:, 4:8, (NT - 1) * P:], (l, name, NT - 1, 1))

            def prep_mine(js, l):
                for name, who in js:
                    if who != "D":
                        continue
                    p = name[1]
                    b = bank(l, *name)
                    if PAIRS[p][0] == "B":
                        nc.vector.tensor_copy(qk5[0:QKB, p % 2, 1, name[3], :], b[0:QKB, :])\
                            .then_inc(emptied["D"], 1)
                    else:
                        for i in range(2):
                            last = nc.vector.tensor_copy(qk5[0:HD, p % 2, 1, i, :], b[i * HD:(i + 1) * HD, :])
                        last.then_inc(emptied["D"], 1)

            def row_max(l, g):
                h, t = divmod(g, NT)
                kind = PAIRS[h // 2][0]
                b = bank(l, "S", g)
                if l * STEPS + g >= 4:
                    dve.wait_ge(emptied["X"], l * STEPS + g - 3)
                m = mx[:, g % 4:g % 4 + 1]
                if kind == "B":
                    link(nc.vector.tensor_reduce(m, b, AX.X, ALU.max))
                else:
                    n = h if kind == "A" else h - HB
                    if t == 0:
                        dve.wait_ge(strip_ready, l * (HA + HC) + n + 1)
                    if l * STEPS + g >= 2:
                        dve.wait_ge(emptied["X"], l * STEPS + g - 1)
                    s = SEQ - P - P * t
                    nc.vector.tensor_tensor_reduce(sc[:, g % 2, :], b, st[:, n % 2, s:s + SEQ], 1.0, NEG * 4,
                                                   ALU.add, ALU.max, m).then_inc(emptied["D"], 1)
                    dve.wait_ge(emptied["D"], J.emptied(l, "S", g))
                nc.vector.tensor_scalar(nmx[:, g % 4:g % 4 + 1], m, -1.0, None, ALU.mult).then_inc(nmax_ready, 1)

            def head_out(l, h):
                p, i = divmod(h, 2)
                kind, pp = PAIRS[p]
                dve.wait_ge(emptied["X"], l * STEPS + NT * h + NT)
                link(nc.vector.reciprocal(rl[:, h % 2, :], ls[:, h % 2, :]))
                dve.wait_ge(pv_done, l * STEPS + NT * h + NT)
                c = ROPE if kind == "B" else HD * i
                o = ps[:, ROT + h % 2, :].rearrange("p (t c) -> p t c", t=NT)[:, :, c:c + HD]
                r = rl[:, h % 2, :].unsqueeze(2).to_broadcast([P, NT, HD])
                nc.vector.tensor_tensor(on[:, :, h * HD:(h + 1) * HD], o, r, ALU.mult).then_inc(o_out, 1)

            def rotate(x1, x2, cos, sin, n):
                w = [sc_flat[:, i * 384:i * 384 + n * 16].rearrange("p (n c) -> p n c", c=16) for i in range(2)]
                w += [st_flat[:, i * 384:i * 384 + n * 16].rearrange("p (n c) -> p n c", c=16) for i in range(2)]
                for dst, s, f in ((w[0], x1, cos), (w[1], x2, sin), (w[2], x1, sin), (w[3], x2, cos)):
                    last = nc.vector.tensor_tensor(dst, s, f, ALU.mult)
                link(last)
                nc.vector.tensor_tensor(x1, w[0], w[1], ALU.subtract)
                return nc.vector.tensor_tensor(x2, w[2], w[3], ALU.add)

            yT_flat = hr[:, 0, :]
            sc_flat = soft[:, 5 * SEQ:7 * SEQ]
            st_flat = soft[:, 3 * SEQ:5 * SEQ]
            dve.wait_ge(tab_in, 16)
            dve.wait_ge(x_in, 16 * NT)
            for l in range(LAYERS):
                dve.wait_ge(gains_in, 16 * NG * (l + 1))
                norm_rows(l, "hT", g_mix)
                for t in range(NT):
                    copy_out(cn[:, t, RQ:DB], (l, "cb", t, 1), RKV + ROPE)
                dve.wait_ge(emptied["A"], J.emptied(l, "cb", NT - 1, 0))
                dve.wait_ge(emptied["D"], J.emptied(l, "cb", NT - 1, 1))
                for t in range(NT):
                    square(cn[:, t, 0:RQ], hr[:, 0, 0:RQ], t, RQ)
                    square(cn[:, t, RQ:RQ + RKV], hr[:, 0, 0:RKV], NT + t, RKV)
                inverse(2 * NT)
                for t in range(NT):
                    nc.vector.scalar_tensor_tensor(out=cn[:, t, 0:RQ], in0=cn[:, t, 0:RQ], scalar=rr[:, t:t + 1],
                                                   in1=g_q, op0=ALU.mult, op1=ALU.mult)
                    kv = cn[:, t, RQ:RQ + RKV]
                    nc.vector.scalar_tensor_tensor(out=kv, in0=kv, scalar=rr[:, NT + t:NT + t + 1],
                                                   in1=g_kv, op0=ALU.mult, op1=ALU.mult).then_inc(lat_ready, 1)
                for t in range(NT):
                    copy_out(vac3[:, t, WA:WA + WC], (l, "v", t, 1), WC)
                kr = cn[:, :, RQ + RKV:DB]
                cosk = tab[:, T_COS:T_SIN].rearrange("p (t h c) -> p t h c", t=NT, h=HB)[:, :, 0, :]
                sink = tab[:, T_SIN:T_DIST].rearrange("p (t h c) -> p t h c", t=NT, h=HB)[:, :, 0, :]
                link(rotate(kr[:, :, 0:16], kr[:, :, 16:32], cosk, sink, NT))
                for t in range(NT):
                    copy_out(cT[:, 3:5, t * P:(t + 1) * P], (l, "cT", t, 1), 2 * P)
                for t in range(NT):
                    for i in range(2):
                        b = bank(l, "kvn", t, i)[:, 0:3 * P].rearrange("p (h w c) -> p h w c", h=3, w=2)
                        kv = kvn4[:, t, 3 * i:3 * i + 3, :]
                        nc.vector.tensor_copy(kv[:, :, 0:HD], b[:, :, 0, :])
                        nc.vector.tensor_copy(kv[:, :, QKB:160], b[:, :, 1, :]).then_inc(emptied["D"], 1)
                prep_mine(prep_jobs(0), l)
                for t in range(NT):
                    nc.vector.tensor_copy(kvn4[:, t, :, HD:QKB], kr[:, t, :].unsqueeze(1).to_broadcast([P, HB, ROPE]))
                dve.wait_ge(emptied["A"], J.emptied(l, "qn", NT - 1, 1))
                q3 = qn.rearrange("p (n c) -> p n c", c=QKB)
                cosq = tab[:, T_COS:T_SIN].rearrange("p (n c) -> p n c", c=16)
                sinq = tab[:, T_SIN:T_DIST].rearrange("p (n c) -> p n c", c=16)
                rotate(q3[:, :, HD:HD + 16], q3[:, :, HD + 16:QKB], cosq, sinq, NT * HB).then_inc(rope_ready, 1)
                dve.wait_ge(rope_ready, l + 1)
                row_max(l, 0)
                row_max(l, 1)
                for g in range(STEPS):
                    if g + 2 < STEPS:
                        row_max(l, g + 2)
                    if g % 2 == 1:
                        b = bank(l, "PT", g)
                        if l * STEPS + g >= 2:
                            dve.wait_ge(pv_done, l * STEPS + g - 1)
                        nc.vector.tensor_copy(pt[:, 1, :], b).then_inc(emptied["D"], 1)
                    if g % NT == 1 and g > 1:
                        head_out(l, g // NT - 1)
                    if g // 8 + 1 < len(PAIRS):
                        prep_mine(prep_at(g // 8 + 1, g % 8), l)
                head_out(l, NH - 1)
                dve.wait_ge(o_out, (l + 1) * NH)
                groups = [(0, WA), (WA, WA + WB), (WA + WB, D)]
                for t in range(NT):
                    for i, (c0, c1) in enumerate(groups):
                        square(on[:, t, c0:c1], hr[:, 0, c0:c1], 3 * t + i, c1 - c0)
                inverse(3 * NT)
                for t in range(NT):
                    for i, (c0, c1) in enumerate(groups):
                        last = nc.vector.scalar_tensor_tensor(out=on[:, t, c0:c1], in0=on[:, t, c0:c1],
                                                              scalar=rr[:, 3 * t + i:3 * t + i + 1],
                                                              in1=g_out[:, c0:c1], op0=ALU.mult, op1=ALU.mult)
                    last.then_inc(y_ready, 1)
                for t in range(NT):
                    copy_out(hT3[:, 4:8, t * P:(t + 1) * P], (l, "yT", t, 1))
                for i in range(2):
                    for t in range(NT):
                        xs = x3[:, t, 512 * i:512 * i + 512]
                        nc.vector.tensor_tensor(xs, bank(l, "op", t, i), xs, ALU.add).then_inc(emptied["D"], 1)
                dve.wait_ge(emptied["D"], J.emptied(l, "op", NT - 1, 1))
                norm_rows(l, "h2", g_ffn)
                if l == 0:
                    nc.vector.memset(small[:, 255:256], 0.0).then_inc(gains_free, 1)
                    for f in range(FT):
                        b = bank(l, "u", f)
                        dve.wait_ge(emptied["A"], J.emptied(l, "g", f))
                        nc.vector.tensor_tensor(hid[:, f, :], b, sil[:, f % 2, :], ALU.mult)\
                            .then_inc(emptied["D"], 1)
                    for i in range(2):
                        for t in range(NT):
                            xs = x3[:, t, 512 * i:512 * i + 512]
                            nc.vector.tensor_tensor(xs, bank(l, "d", i, t), xs, ALU.add).then_inc(emptied["D"], 1)
                    dve.wait_ge(emptied["D"], J.emptied(l, "d", 1, NT - 1))

            l = LAYERS - 1
            tt, V = nc.vector.tensor_tensor, nc.vector
            for t in range(NT):
                V.tensor_copy(logit[:, t, :], bank(l, "lg", t)[:, 0:NE]).then_inc(emptied["D"], 1)
            dve.wait_ge(emptied["D"], J.emptied(l, "lg", NT - 1))
            for t in range(NT):
                last = V.max(top[:, t, :], logit[:, t, :])
            link(last)
            for t in range(NT):
                last = V.max_index(pick[:, t, :], top[:, t, :], logit[:, t, :])
            link(last)
            tt(gap, top[:, :, 1], top[:, :, 0], ALU.subtract).then_inc(gates_sub, 1)
            link(V.tensor_copy(pickf, pick[:, :, 0:2]))
            eno = tab[:, T_E:T_E + NE].unsqueeze(1).to_broadcast([P, NT, NE])
            for j, lot in enumerate((lot0, lot1)):
                last = tt(lot, eno, pickf[:, :, j:j + 1].to_broadcast([P, NT, NE]), ALU.is_equal)
            link(last)
            tt(both, lot0, lot1, ALU.add).then_inc(lots_ready, 1)
            dve.wait_ge(gates_exp, 1)
            link(V.tensor_scalar(den, eg, 1.0, None, ALU.add))
            link(V.reciprocal(g0, den))
            link(tt(g1, eg, g0, ALU.mult))
            V.tensor_copy(rank, bank(l, "rk")[:, 0:NT * NE].rearrange("p (t e) -> p t e", t=NT))\
                .then_inc(emptied["D"], 1)
            V.tensor_copy(cnt, bank(l, "ct")[:, 0:NE]).then_inc(emptied["D"], 1)
            dve.wait_ge(emptied["D"], J.emptied(l, "ct"))
            V.tensor_scalar(more, cnt, float(UNIT), None, ALU.is_gt)
            link(V.tensor_scalar(units, cnt, 0.0, None, ALU.is_gt))
            link(tt(units, units, more, ALU.add))
            link(V.tensor_tensor_scan(incl, tab[:, T_ONES:T_ONES + NE], units, 0.0, ALU.mult, ALU.add))
            link(tt(excl, incl, units, ALU.subtract))
            link(V.tensor_scalar(first, excl, float(UNIT), None, ALU.mult))
            link(tt(rank, rank, first.unsqueeze(1).to_broadcast([P, NT, NE]), ALU.add))
            for j, lot in enumerate((lot0, lot1)):
                link(tt(hit, lot, rank, ALU.mult))
                link(V.tensor_reduce(slotf[:, :, j], hit, AX.X, ALU.add))
            V.tensor_copy(slot, slotf.rearrange("p t j -> p (t j)")).then_inc(slots_ready, 1)
            unit = tab[:, T_UNIT:T_UNIT + NU * NE].rearrange("p (u e) -> p u e", u=NU)

            def over(v):
                return v.unsqueeze(1).to_broadcast([P, NU, NE])

            tt(past, unit, over(incl), ALU.is_ge)
            link(tt(owns, unit, over(excl), ALU.is_ge))
            link(tt(owns, owns, past, ALU.subtract))
            link(V.tensor_reduce(planf[:, 0:NU], past, AX.X, ALU.add))
            link(tt(tot, cnt, first, ALU.add))
            link(V.scalar_tensor_tensor(out=left, in0=unit, scalar=-float(UNIT), in1=over(tot),
                                        op0=ALU.mult, op1=ALU.add))
            link(tt(left, left, owns, ALU.mult))
            link(V.tensor_reduce(planf[:, NU:2 * NU], left, AX.X, ALU.add))
            link(V.tensor_scalar(planf[:, 0:NU], planf[:, 0:NU], float(NE - 1), None, ALU.min))
            link(V.tensor_scalar(planf[:, NU:2 * NU], planf[:, NU:2 * NU], float(UNIT), None, ALU.min))
            V.tensor_copy(planf[:, 2 * NU + 1:3 * NU], planf[:, 1:NU])
            V.memset(planf[:, 3 * NU:3 * NU + 2], 0.0)
            link(V.tensor_copy(planf[:, 2 * NU:2 * NU + 1], incl[:, NE - 1:NE]))
            V.tensor_copy(plan, planf).then_inc(plan_ready, 1)
            dve.wait_ge(plan_ready, 1)
            dve.sem_inc(gu_free, 4)
            dve.sem_inc(y_out, 2)
            n_units = dve.value_load(plan[0:1, 2 * NU:2 * NU + 1], min_val=1, max_val=NU)
            with dve.Fori(0, NU) as u:
                with dve.If(u < n_units):
                    with dve.Fori(0, FE // UPS) as i:
                        for s in range(UPS):
                            dve.wait_ge(e_silu, u * FE + i * UPS + s + 1)
                            tt(eh[:, bass.ds(i * UPS + s, 1), :], ps[:, s % 4:s % 4 + 1, UNIT:2 * UNIT],
                               esil[:, SILU_AT[s]:SILU_AT[s] + 1, :], ALU.mult).then_inc(gu_free, 1)
                    with dve.Fori(0, ND // 2) as j:
                        for s in range(2):
                            dve.wait_ge(y_filled, u * ND + j * 2 + s + 3)
                            V.tensor_copy(yT[:, bass.ds(j * 2 + s, 1), :], ps[:, 4 + s:5 + s, 0:UNIT]).then_inc(y_out, 1)
            dve.wait_ge(gathered, 16 * 2 * NT)
            dve.wait_ge(final_gain, 16)
            for t in range(NT):
                for j, gt in enumerate((g0, g1)):
                    link(V.scalar_tensor_tensor(out=x3[:, t, :], in0=back[:, 2 * t + j, :], scalar=gt[:, t:t + 1],
                                                in1=x3[:, t, :], op0=ALU.mult, op1=ALU.add))
            for t in range(NT):
                square(x3[:, t, :], yT_flat, t, D)
            inverse(NT)
            for t in range(NT):
                last = V.scalar_tensor_tensor(out=x3[:, t, :], in0=x3[:, t, :], scalar=rr[:, t:t + 1], in1=g_mix,
                                              op0=ALU.mult, op1=ALU.mult)
            last.then_inc(fin_ready, 1)


def shape_tables():
    import numpy as np

    tab = np.zeros((P, T_W), np.float32)
    tab[:, T_ID:T_ID + P] = np.eye(P)
    inv = np.float32(10000.0) ** (-np.arange(0, ROPE, 2, dtype=np.float32) / np.float32(ROPE))
    ang = np.arange(SEQ, dtype=np.float32)[:, None] * inv.astype(np.float32)[None, :]
    for at, f in ((T_COS, np.cos), (T_SIN, np.sin)):
        v = f(ang).astype(np.float32).reshape(NT, P, 1, 16).transpose(1, 0, 2, 3)
        tab[:, at:at + NT * HB * 16] = np.broadcast_to(v, (P, NT, HB, 16)).reshape(P, -1)
    gap = np.abs(np.arange(STRIP)[None, :] - (SEQ - P) - np.arange(P)[:, None])
    reach = (gap <= 64).astype(int) + ((gap % 4 == 0) & (gap <= 256)) + ((gap % 16 == 0) & (gap <= 1024))
    tab[:, T_DIST:T_DIST + STRIP] = gap
    tab[:, T_AMASK:T_AMASK + STRIP] = np.where(reach > 0, np.log(np.maximum(reach, 1)), NEG)
    qc = np.arange(P)[:, None] % GRID
    first = np.clip(qc - NAC // 2, 0, GRID - NAC)
    kc = np.arange(GRID)[None, :]
    tab[:, T_CMASK:T_CMASK + GRID] = np.where((kc >= first) & (kc < first + NAC), 0.0, NEG)
    tab[:, T_TRI:T_TRI + P] = np.arange(P)[:, None] < np.arange(P)[None, :]
    tab[:, T_ONES:T_ONES + P] = 1.0
    tab[:, T_UNIT:T_UNIT + NU * NE] = np.repeat(np.arange(NU), NE)[None, :]
    tab[:, T_E:T_E + NE] = np.arange(NE)[None, :]
    return tab


_INS = ["x", "g_mix", "w_in", "g_q", "g_kv", "w_uq", "w_ukv", "rpb", "g_out_a", "g_out_b", "g_out_c", "w_o",
        "g_ffn", "w1", "w3", "w2", "w_router", "e_w1", "e_w3", "e_w2", "g_final"]


def kernel(**inputs):
    import numpy as _np
    import concourse.bacc as _bacc
    from concourse import mybir as _mybir
    from concourse.bass_utils import run_bass_kernel_spmd as _run

    nc = _bacc.Bacc("TRN2", target_bir_lowering=False, num_devices=1)
    arrays, aps = {}, {}
    for name in _INS + ["tables"]:
        v = shape_tables() if name == "tables" else _np.ascontiguousarray(inputs[name])
        arrays[f"in_{name}_dram"] = v
        aps[name] = nc.dram_tensor(f"in_{name}_dram", v.shape, _mybir.dt.from_np(v.dtype), kind="ExternalInput").ap()
    aps["out"] = nc.dram_tensor("out_0_dram", (1, SEQ, D), F32, kind="ExternalOutput").ap()
    trunk(nc, aps)
    r = _run(nc, [arrays], core_ids=[0])
    return r.results[0]["out_0_dram"]
```

```python
from contextlib import ExitStack

import concourse.bass as bass
from concourse import mybir

F32 = mybir.dt.float32
U32 = mybir.dt.uint32
I32 = mybir.dt.int32
ALU = mybir.AluOpType
ACT = mybir.ActivationFunctionType
AX = mybir.AxisListType

P = 128
SEQ, D, LAYERS = 512, 1024, 2
NT = SEQ // P
ND = D // P
HD = 64
HA, HB, HC = 6, 6, 4
NH = HA + HB + HC
RQ, RKV, ROPE = 384, 256, 32
QKB = HD + ROPE
WA, WB, WC = HA * HD, HB * HD, HC * HD
IN_COLS = 3 * WA + RQ + RKV + ROPE + 3 * WC
COL_QA, COL_KA, COL_VA = 0, WA, 2 * WA
COL_B = 3 * WA
COL_QC = COL_B + RQ + RKV + ROPE
COL_KC, COL_VC = COL_QC + WC, COL_QC + 2 * WC
DB = RQ + RKV + ROPE
DFF = 2816
NE, DFE = 8, 3584
GRID, NAR, NAC = 64, 8, 16
EPS = 1e-6
NEG = -1e30
STRIP = 2 * SEQ - P
UNIT = 2 * P
NU = (2 * SEQ) // UNIT + NE - 1
PADW = 128
RING = 6144

T_ID = 0
T_EPS = T_ID + P
T_COS = T_EPS + 1
T_SIN = T_COS + NT * HB * 16
T_DIST = T_SIN + NT * HB * 16
T_AMASK = T_DIST + STRIP
T_CMASK = T_AMASK + STRIP
T_TRI = T_CMASK + GRID
T_ONES = T_TRI + P
T_UNIT = T_ONES + P
T_E = T_UNIT + NU * NE
T_W = T_E + NE

PAIRS = [("A", 0), ("A", 1), ("A", 2), ("B", 0), ("B", 1), ("B", 2), ("C", 0), ("C", 1)]
STEPS = NH * NT
FT = DFF // P
FE = DFE // P
UPS = 4
DNS = 4
CLASSES = [128, 144, 160, 176, 192, 256]
GROUPS = [(0, WA), (WA, WA + WB), (WA + WB, D)]
CH = DFF // UNIT
SLOPES = [2.0 ** (-8.0 * (h + 1) / HA) for h in range(HA)]
QSCALE = {"A": HD ** -0.5, "B": QKB ** -0.5, "C": HD ** -0.5}
ROT = 6


def front_jobs():
    j = [(("hT", t, i), "AD"[i]) for t in range(NT) for i in range(2)]
    j += [(("cb", t, i), "AD"[i]) for t in range(NT) for i in range(2)]
    j += [(("v", t, i), "AD"[i]) for t in range(NT) for i in range(2)]
    j += [(("cT", t, i), "AD"[i]) for t in range(NT) for i in range(2)]
    j += [(("qn", t, i), "A") for t in range(NT) for i in range(2)]
    j += [(("kvn", t, i), "D") for t in range(NT) for i in range(2)]
    j += prep_jobs(0)
    j += [(("S", 0), "D"), (("S", 1), "D")]
    for g in range(STEPS):
        if g + 2 < STEPS:
            j.append((("S", g + 2), "X" if PAIRS[(g + 2) // 8][0] == "B" else "D"))
        j.append((("PT", g), "AD"[g % 2]))
        p, k = g // 8, g % 8
        if p + 1 < len(PAIRS):
            j += prep_at(p + 1, k)
    for t in range(NT + 1):
        j += [(("yT", t, i), "AD"[i]) for i in range(2)] if t < NT else []
        j += [(("op", t - 1, 0), "D")] if t else []
    j += [(("op", t, 1), "D") for t in range(NT)]
    j += [(("h2", t, i), "AD"[i]) for t in range(NT) for i in range(2)]
    return j


def prep_jobs(p):
    if PAIRS[p][0] == "B":
        return [(("qk", p, w, i), "AD"[w]) for i in range(2) for w in range(2)]
    return [(("qk", p, w), "AD"[w]) for w in range(2)]


def prep_at(p, k):
    js = prep_jobs(p)
    at = [1, 2, 3, 4] if len(js) == 4 else [1, 3]
    return [js[at.index(k)]] if k in at else []


def dense_jobs():
    j = [((m, f), "AD"[m == "u"]) for f in range(FT) for m in ("g", "u")]
    j += [(("d", i, t), "D") for i in range(2) for t in range(NT)]
    return j


def moe_front_jobs():
    return [(("lg", t), "D") for t in range(NT)] + [(("rk",), "D"), (("ct",), "D")]


class Jobs:

    def __init__(self):
        self.at, self.who, self.nth, self.count = {}, [], [], {"A": 0, "D": 0, "X": 0}
        self.exps = 0
        for l in range(LAYERS):
            for name, who in front_jobs() + (dense_jobs() if l == 0 else moe_front_jobs()):
                self.at[(l,) + name] = len(self.who)
                self.who.append(who)
                if who == "X":
                    self.nth.append(l * STEPS + name[1] + 1)
                else:
                    self.count[who] += 1
                    self.nth.append(self.count[who])
        self.n = len(self.who)

    def bank(self, *name):
        return self.at[name] % ROT

    def filled(self, *name):
        return self.at[name] + 1

    def emptied(self, *name):
        return self.nth[self.at[name]]


def trunk(nc, a):
    J = Jobs()
    ctx = ExitStack()
    with ctx:
        def sb(name, cols, dt=F32, rows=P):
            return ctx.enter_context(nc.sbuf_tensor(name, [rows, cols], dt))

        def sem(name):
            return ctx.enter_context(nc.semaphore(name))

        ps = ctx.enter_context(nc.psum_tensor("ps", [P, 8, 512], F32))
        x = sb("x_rows", NT * D)
        hT = sb("hT", ND * SEQ)
        ring = sb("weight_ring", 2 * RING)
        gains = sb("gains", 3 * D + RQ + RKV)
        tab = sb("tables", T_W)
        small = sb("small", 256)
        A0 = sb("attention_arena", 25472)
        off = [0]

        def part(n):
            s = off[0]
            off[0] += n
            assert off[0] <= 25472, off[0]
            return A0[:, s:s + n]

        lat = part(NT * DB + 5 * SEQ)
        qk = part(2 * 2 * 2 * SEQ)
        kvn = part(NT * HB * 160)
        qn = part(NT * HB * QKB)
        vac = part(NT * (WA + WC))
        soft = part(7 * SEQ)
        strips = part(2 * STRIP)
        hrow = part(2 * D)

        x3 = x[:, :].rearrange("p (t d) -> p t d", t=NT)
        hT3 = hT[:, :].rearrange("p (k s) -> p k s", k=ND)
        qk5 = qk.rearrange("p (b w h s) -> p b w h s", b=2, w=2, h=2)
        kvn4 = kvn.rearrange("p (t h c) -> p t h c", t=NT, h=HB)
        qn4 = qn.rearrange("p (t h c) -> p t h c", t=NT, h=HB)
        cn = lat[:, 0:NT * DB].rearrange("p (t c) -> p t c", t=NT)
        cT = lat[:, NT * DB:].rearrange("p (k s) -> p k s", k=5)
        on = lat[:, 0:NT * D].rearrange("p (t d) -> p t d", t=NT)
        vac3 = vac.rearrange("p (t c) -> p t c", t=NT)
        pr = soft[:, 0:3 * SEQ].rearrange("p (b s) -> p b s", b=3)
        pt = soft[:, 3 * SEQ:5 * SEQ].rearrange("p (b s) -> p b s", b=2)
        sc = soft[:, 5 * SEQ:7 * SEQ].rearrange("p (b s) -> p b s", b=2)
        st = strips.rearrange("p (b s) -> p b s", b=2)
        hr = hrow.rearrange("p (b d) -> p b d", b=2)
        at_vac = NT * DB + 5 * SEQ + 2 * 2 * 2 * SEQ + NT * HB * (160 + QKB)
        mixed = A0[:, at_vac:at_vac + NT * D].rearrange("p (t d) -> p t d", t=NT)
        g_mix, g_ffn, g_out = (gains[:, i * D:(i + 1) * D] for i in range(3))
        g_q = gains[:, 3 * D:3 * D + RQ]
        g_kv = gains[:, 3 * D + RQ:3 * D + RQ + RKV]
        ident = tab[:, T_ID:T_ID + P]
        eps = tab[:, T_EPS:T_EPS + 1]
        ones = tab[:, T_ONES:T_ONES + P]
        tri = tab[:, T_TRI:T_TRI + P]
        hid = A0[:, 0:FT * SEQ].rearrange("p (f s) -> p f s", f=FT)
        sil = A0[:, FT * SEQ:(FT + 2) * SEQ].rearrange("p (b s) -> p b s", b=2)

        ssq = small[:, 0:12]
        rms = small[:, 12:24]
        rr = small[:, 24:36]
        mx = small[:, 36:40]
        nmx = small[:, 40:44]
        ls = small[:, 44:52].rearrange("p (b t) -> p b t", b=2)
        rl = small[:, 52:60].rearrange("p (b t) -> p b t", b=2)

        down_at = [ring[:, 3584 * i:3584 * (i + 1)] for i in range(3)] + [A0[:, 0:3584]]
        down = [v.rearrange("p (f c) -> p f c", f=FE) for v in down_at]
        esil = ring[:, 10752:10752 + 2 * UNIT].rearrange("p (b s) -> p b s", b=2)
        eh = A0[:, 3584:10752].rearrange("p (f s) -> p f s", f=FE)
        yT = A0[:, 10752:12800].rearrange("p (k s) -> p k s", k=ND)
        rows = A0[:, 12800:14848].rearrange("p (b d) -> p b d", b=2)
        yrow = A0[:, 14848:16896].rearrange("p (b d) -> p b d", b=2)
        up = [A0[:, 16896 + 2048 * i:16896 + 2048 * (i + 1)].rearrange("p (m k c) -> p m k c", m=2, k=ND)
              for i in range(UPS)]
        h4 = on
        XT = hT[:, 0:ND * UNIT].rearrange("p (k s) -> p k s", k=ND)
        back = A0[:, 0:8 * D].rearrange("p (n d) -> p n d", n=2 * NT)
        used = [0]

        def rt(*shape):
            n = 1
            for d in shape:
                n *= d
            v = gains[:, 2 * D + used[0]:2 * D + used[0] + n]
            used[0] += n
            return v.rearrange("p (a b) -> p a b", a=shape[0]) if len(shape) == 2 else v

        logit, top, lot0, lot1, both = (rt(NT, NE) for _ in range(5))
        pick = rt(NT * NE).bitcast(U32).rearrange("p (t e) -> p t e", t=NT)
        rank, hit = rt(NT, NE), rt(NT, NE)
        pickf, slotf = rt(NT, 2), rt(NT, 2)
        gap, eg, den, g0, g1 = (rt(NT) for _ in range(5))
        cnt, more, units, incl, excl, first, tot = (rt(NE) for _ in range(7))
        past, owns, left = rt(NU, NE), rt(NU, NE), rt(NU, NE)
        planf = rt(3 * NU + 2)
        plan = rt(3 * NU + 2).bitcast(I32)
        slot = rt(NT * 2).bitcast(U32)
        wr = rt(ND * NE).rearrange("p (k e) -> p k e", k=ND)

        rows_dram = nc.dram_tensor("rows_by_slot", [(NU + 1) * UNIT, D], F32).ap()
        y_dram = nc.dram_tensor("results_by_slot", [NU * UNIT, D], F32).ap()

        pad_dram = nc.dram_tensor("padded_bias", [GRID, LAYERS * HC * 15, PADW], F32).ap()

        loaded = [sem("ring_loaded_0"), sem("ring_loaded_1")]
        tab_in, gains_in = sem("tables_loaded"), sem("gains_loaded")
        x_in = [sem(f"x_loaded_{t}") for t in range(NT)]
        ident_in, mix_in = sem("identity_loaded"), sem("first_gain_loaded")
        act_link = sem("act_order")
        rpb_in, pad_set, pad_out = sem("position_bias_loaded"), sem("pad_set"), sem("pad_stored")
        filled = sem("banks_filled")
        emptied = {"A": sem("banks_emptied_by_act"), "D": sem("banks_emptied_by_dve"), "X": sem("exponentials_done")}
        sq_done, rms_ready = sem("square_sums_done"), sem("rms_ready")
        h_ready = sem("normed_rows_ready")
        lat_ready = sem("latents_normed")
        rope_ready = sem("rope_done")
        nmax_ready = sem("row_maxima_ready")
        pv_done = sem("head_steps_accumulated")
        o_out = sem("head_outputs_stored")
        strip_ready, strip_in, strip_half = sem("strips_ready"), sem("strips_loaded"), sem("strip_half_built")
        y_ready = sem("group_rows_ready")
        gains_free = sem("gains_free")
        dve_link = sem("dve_order")
        out_done = sem("output_stored")
        silu_done = sem("silu_done")
        fin_ready, sums_ready = sem("final_rows_ready"), sem("final_sums_ready")

        filled_before, router_in = sem("rows_filled_before_scatter"), sem("router_loaded")
        gates_sub, gates_exp, lots_ready = sem("gate_gap_ready"), sem("gate_exp_done"), sem("lots_ready")
        slots_ready, plan_ready, scattered = sem("slots_ready"), sem("plan_ready"), sem("rows_scattered")
        rows_in, up_in, down_in = sem("unit_rows_loaded"), [sem(f"up_loaded_{i}") for i in range(UPS)], \
            [sem(f"down_loaded_{i}") for i in range(DNS)]
        turned, turn_out = sem("unit_turns_filled"), sem("unit_turns_emptied")
        gu_filled, e_silu, gu_free = sem("gate_up_filled"), sem("expert_silu_done"), sem("gate_up_banks_given")
        y_filled, y_out, y_stored = sem("unit_results_filled"), sem("unit_results_emptied"), sem("results_stored")
        gathered = [sem(f"results_gathered_{t}") for t in range(NT)]
        final_gain, idle_set = sem("final_gain_loaded"), sem("idle_rows_set")

        entries = []

        def wsrc(ap, c0, n):
            return ap[:, c0:c0 + n].rearrange("(k p) c -> p k c", p=P)

        def entry(key, loads, last):
            entries.append((key, loads, last))

        for l in range(LAYERS):
            w_in, w_uq, w_ukv, w_o = (a[n][l] for n in ("w_in", "w_uq", "w_ukv", "w_o"))
            entry((l, "b"), [(0, 8, DB, wsrc(w_in, COL_B, DB))], (l, "cb", NT - 1, 1))
            entry((l, "v"), [(0, 8, WA, wsrc(w_in, COL_VA, WA)), (8 * WA, 8, WC, wsrc(w_in, COL_VC, WC))],
                  (l, "v", NT - 1, 1))
            entry((l, "uq"), [(0, 3, HB * QKB, wsrc(w_uq, 0, HB * QKB)),
                              (3 * HB * QKB, 2, HB * P, wsrc(w_ukv, 0, HB * P))], (l, "kvn", NT - 1, 1))
            entry((l, "qkA"), [(0, 8, 2 * WA, wsrc(w_in, COL_QA, 2 * WA))], (l, "qk", 2, 1))
            entry((l, "qkC"), [(0, 8, 2 * WC, wsrc(w_in, COL_QC, 2 * WC))], (l, "qk", 7, 1))
            for i in range(2):
                entry((l, "o", i), [(0, 8, 512, wsrc(w_o, 512 * i, 512))], (l, "op", NT - 1, i))
            if l == 0:
                w1, w3, w2 = a["w1"][0], a["w3"][0], a["w2"][0]
                for c in range(CH):
                    entry((l, "f", c), [(0, 8, UNIT, wsrc(w1, UNIT * c, UNIT)),
                                        (8 * UNIT, 8, UNIT, wsrc(w3, UNIT * c, UNIT))], (l, "u", 2 * c + 1))
                for i in range(2):
                    for c in range(2):
                        entry((l, "w2", i, c),
                              [(0, FT // 2, 512, w2[c * DFF // 2:(c + 1) * DFF // 2, 512 * i:512 * i + 512]
                                .rearrange("(k p) c -> p k c", p=P))], (l, "d", i, NT - 1))
        n_of = {e[0]: n for n, e in enumerate(entries)}
        loads_to = [0, 0]
        full_at = []
        for n, e in enumerate(entries):
            loads_to[n % 2] += 16 * len(e[1])
            full_at.append(loads_to[n % 2])

        def wview(key, i=0):
            n = n_of[key]
            o, k, c, _ = entries[n][1][i]
            s = (n % 2) * RING + o
            return ring[:, s:s + k * c].rearrange("p (k c) -> p k c", k=k)

        def layer_gains(l):
            return [(g_mix, a["g_mix"][l]), (g_ffn, a["g_ffn"][l]),
                    (g_out[:, 0:WA], a["g_out_a"][l]), (g_out[:, WA:WA + WB], a["g_out_b"][l]),
                    (g_out[:, WA + WB:], a["g_out_c"][l]), (g_q, a["g_q"][l]), (g_kv, a["g_kv"][l])]

        NG = 7

        block = ctx.enter_context(nc.Block())

        @block.sync
        def _(sp):
            for t in range(NT):
                sp.dma_start(x3[:, t, :], a["x"][0, t * P:(t + 1) * P, :]).then_inc(x_in[t], 16)
            for n, (key, loads, last) in enumerate(entries):
                if n >= 2:
                    sp.wait_ge(filled, J.filled(*entries[n - 2][2]))
                for (o, k, c, src) in loads:
                    s = (n % 2) * RING + o
                    sp.dma_start(ring[:, s:s + k * c].rearrange("p (k c) -> p k c", k=k), src)\
                        .then_inc(loaded[n % 2], 16)
                if n == 0:
                    sp.dma_start(tab[:, T_COS:], a["tables"][:, T_COS:]).then_inc(tab_in, 16)
            sp.wait_ge(router_in, 16)
            L = LAYERS - 1
            sp.wait_ge(filled, J.filled(L, "h2", NT - 1, 1))

            def load_up(e, u, f, s):
                sp.wait_ge(gu_filled, u * FE + f + 1)
                for m, n in ((0, "e_w1"), (1, "e_w3")):
                    sp.dma_start(up[s][:, m, :, :],
                                 a[n][0][e][:, bass.ds(f * P, P)].rearrange("(k p) c -> p k c", p=P))\
                        .then_inc(up_in[s], 16)

            def load_down(e, u, d, s):
                sp.wait_ge(y_filled, u * ND + d + 1)
                sp.dma_start(down[s], a["e_w2"][0][e][:, bass.ds(d * P, P)].rearrange("(f p) c -> p f c", p=P))\
                    .then_inc(down_in[s], 16)

            for s in range(UPS):
                load_up(0, 0, s, s)
            for s in range(DNS - 1):
                load_down(0, 0, s, s)
            sp.wait_ge(scattered, 16 * 2 * NT)
            load_down(0, 0, DNS - 1, DNS - 1)
            sp.wait_ge(plan_ready, 1)
            n_units = sp.value_load(plan[0:1, 2 * NU:2 * NU + 1], min_val=1, max_val=NU)
            with sp.Fori(0, NU) as u:
                with sp.If(u < n_units):
                    e = sp.value_load(plan[0:1, bass.ds(u, 1)], min_val=0, max_val=NE - 1)
                    nxt = sp.value_load(plan[0:1, bass.ds(u + 2 * NU + 1, 1)], min_val=0, max_val=NE - 1)
                    with sp.Fori(1, FE // UPS) as i:
                        for s in range(UPS):
                            load_up(e, u, i * UPS + s, s)
                    for s in range(DNS):
                        load_down(e, u, DNS + s, s)
                        with sp.If(u + 1 < n_units):
                            load_up(nxt, u + 1, s, s)
                    with sp.If(u + 1 < n_units):
                        for s in range(DNS):
                            load_down(nxt, u + 1, s, s)
                    sp.sem_inc(idle_set, 16)
                with sp.Else():
                    sp.dma_start(y_dram[bass.ds(u * UNIT, UNIT), :], a["x"][0][0:UNIT, :]).then_inc(idle_set, 16)
            for t in range(NT):
                sp.wait_ge(fin_ready, t + 1)
                sp.dma_start(a["out"][0][t * P:(t + 1) * P, :], x3[:, t, :]).then_inc(out_done, 16)
            sp.wait_ge(out_done, 16 * NT)

        @block.gpsimd
        def _(pool):
            padt = st[0:LAYERS * HC * 15, 0, 0:PADW]
            nc.gpsimd.memset(padt, NEG).then_inc(pad_set, 1)
            pool.wait_ge(pad_set, 1)
            pool.dma_start(padt[:, 48:48 + 31], a["rpb"].rearrange("l h r c -> (l h r) c")).then_inc(rpb_in, 16)
            for dst, src in layer_gains(0)[1:]:
                pool.dma_start(dst, src.partition_broadcast(P)).then_inc(gains_in, 16)
            pool.wait_ge(rpb_in, 16)
            pool.wait_ge(tab_in, 16)
            pool.dma_start(pad_dram.rearrange("c r w -> r c w"),
                           padt.unsqueeze(1).to_broadcast([LAYERS * HC * 15, GRID, PADW])).then_inc(pad_out, 16)
            pool.wait_ge(pad_out, 16)
            halves = 0
            for l in range(LAYERS):
                for n in range(HA + HC):
                    if l or n >= 2:
                        m = l * (HA + HC) + n - 2
                        ll, mm = divmod(m, HA + HC)
                        last = (mm if mm < HA else mm + HB) * NT + NT - 1
                        pool.wait_ge(emptied["D"], J.emptied(ll, "S", last))
                    buf = st[:, n % 2, :]
                    if n < HA:
                        nc.gpsimd.tensor_scalar(buf, tab[:, T_DIST:T_DIST + STRIP], -SLOPES[n], None, ALU.mult)\
                            .then_inc(strip_half, 1)
                        halves += 1
                        pool.wait_ge(strip_half, halves)
                        nc.gpsimd.tensor_tensor(buf, buf, tab[:, T_AMASK:T_AMASK + STRIP], ALU.add)\
                            .then_inc(strip_ready, 1)
                    else:
                        h = n - HA
                        for r in range(2):
                            row = (l * HC + h) * 15 + 1 - r
                            src = bass.AP(tensor=pad_dram.tensor, offset=row * PADW + 63,
                                          ap=[[LAYERS * HC * 15 * PADW - 1, GRID], [PADW, 14], [1, GRID]])
                            pool.dma_start(buf[r * GRID:(r + 1) * GRID, :]
                                           .rearrange("p (a c) -> p a c", a=14), src).then_inc(strip_in, 16)
                        pool.wait_ge(strip_in, 32 * (l * HC + h + 1))
                        b3 = buf.rearrange("p (a c) -> p a c", a=14)
                        cm = tab[:, T_CMASK:T_CMASK + GRID].unsqueeze(1).to_broadcast([P, 14, GRID])
                        nc.gpsimd.tensor_tensor(b3, b3, cm, ALU.add).then_inc(strip_ready, 1)
                if l == 0:
                    for i in range((NU + 1) * UNIT // SEQ):
                        pool.dma_start(rows_dram[i * SEQ:(i + 1) * SEQ, :], a["x"][0]).then_inc(filled_before, 16)
                    pool.wait_ge(gains_free, 1)
                    for dst, src in layer_gains(1):
                        pool.dma_start(dst, src.partition_broadcast(P)).then_inc(gains_in, 16)

            pool.wait_ge(y_ready, LAYERS * NT)
            pool.dma_start(wr, a["w_router"][0].rearrange("(k p) e -> p k e", p=P)).then_inc(router_in, 16)
            pool.dma_start(g_mix, a["g_final"].partition_broadcast(P)).then_inc(final_gain, 16)
            pool.wait_ge(filled_before, 16 * ((NU + 1) * UNIT // SEQ))
            pool.wait_ge(h_ready, 2 * LAYERS * NT)
            pool.wait_ge(slots_ready, 1)
            for t in range(NT):
                for j in range(2):
                    pool.indirect_dma_start(rows_dram, bass.IndirectOffsetOnAxis(ap=slot[:, 2 * t + j:2 * t + j + 1], axis=0),
                                            h4[:, t, :], None).then_inc(scattered, 16)
            pool.wait_ge(plan_ready, 1)
            n_units = pool.value_load(plan[0:1, 2 * NU:2 * NU + 1], min_val=1, max_val=NU)
            pool.wait_ge(scattered, 16 * 2 * NT)
            pool.dma_start(rows, rows_dram[0:UNIT, :].rearrange("(b p) d -> p b d", p=P)).then_inc(rows_in, 16)
            with pool.Fori(0, NU) as u:
                with pool.If(u < n_units):
                    pool.wait_ge(turned, u * 8 + 4)
                    pool.dma_start(rows, rows_dram[bass.ds(u * UNIT + UNIT, UNIT), :]
                                   .rearrange("(b p) d -> p b d", p=P)).then_inc(rows_in, 16)
            pool.wait_ge(y_stored, n_units * 16 + 16)
            pool.sem_inc(idle_set, 16)
            pool.wait_ge(idle_set, NU * 16 + 16)
            for t in range(NT):
                for j in range(2):
                    pool.indirect_dma_start(back[:, 2 * t + j, :], None, y_dram,
                                            bass.IndirectOffsetOnAxis(ap=slot[:, 2 * t + j:2 * t + j + 1], axis=0))\
                        .then_inc(gathered[t], 16)
            for t in range(NT):
                pool.wait_ge(gathered[t], 32)

        @block.tensor
        def _(pe):
            pe.wait_ge(ident_in, 16)

            def take(*name):
                n = J.at[name]
                if n >= ROT:
                    pe.wait_ge(emptied[J.who[n - ROT]], J.nth[n - ROT])
                return ps[:, n % ROT, :]

            def arrived(key):
                n = n_of[key]
                pe.wait_ge(loaded[n % 2], full_at[n])

            def emptied_upto(*name):
                pe.wait_ge(emptied[J.who[J.at[name]]], J.emptied(*name))

            def turn(job, srcs):
                b = take(*job)
                for i, s in enumerate(srcs):
                    w = s.shape[1]
                    last = nc.tensor.transpose(b[0:w, i * P:(i + 1) * P], s, ident)
                last.then_inc(filled, 1)

            def rows_times(job, lhsT, w, kt, t, c0, n):
                b = take(*job)
                for k in range(kt):
                    last = nc.tensor.matmul(b[:, 0:n], lhsT[:, k, t * P:(t + 1) * P], w[:, k, c0:c0 + n],
                                            start=(k == 0), stop=(k == kt - 1))
                last.then_inc(filled, 1)

            def cols_times(job, w, c0):
                b = take(*job)
                for k in range(ND):
                    last = nc.tensor.matmul(b[:, :], w[:, k, c0:c0 + P], hT3[:, k, :],
                                            start=(k == 0), stop=(k == ND - 1))
                last.then_inc(filled, 1)

            def norm_turn(l, name):
                rows = h4 if name == "h2" else mixed
                for t in range(NT):
                    pe.wait_ge(h_ready, (2 * l + (name == "h2")) * NT + t + 1)
                    for i in range(2):
                        turn((l, name, t, i), [rows[:, t, (4 * i + k) * P:(4 * i + k + 1) * P] for k in range(4)])
                emptied_upto(l, name, NT - 1, 0)
                emptied_upto(l, name, NT - 1, 1)

            def prep(l, name):
                p, w = name[1], name[2]
                kind, pp = PAIRS[p]
                if kind == "B":
                    h = 2 * pp + name[3]
                    src = kvn4 if w else qn4
                    turn((l,) + name, [src[:, t, h, 0:QKB] for t in range(NT)])
                    return
                key = (l, "qk" + kind)
                arrived(key)
                cols_times((l,) + name, wview(key), (WA if kind == "A" else WC) * w + P * pp)

            for l in range(LAYERS):
                norm_turn(l, "hT")
                arrived((l, "b"))
                wb = wview((l, "b"))
                for t in range(NT):
                    rows_times((l, "cb", t, 0), hT3, wb, ND, t, 0, RQ)
                    rows_times((l, "cb", t, 1), hT3, wb, ND, t, RQ, RKV + ROPE)
                arrived((l, "v"))
                for t in range(NT):
                    rows_times((l, "v", t, 0), hT3, wview((l, "v"), 0), ND, t, 0, WA)
                    rows_times((l, "v", t, 1), hT3, wview((l, "v"), 1), ND, t, 0, WC)
                for t in range(NT):
                    pe.wait_ge(lat_ready, l * NT + t + 1)
                    turn((l, "cT", t, 0), [cn[:, t, k * P:(k + 1) * P] for k in range(3)])
                    turn((l, "cT", t, 1), [cn[:, t, (3 + k) * P:(4 + k) * P] for k in range(2)])
                arrived((l, "uq"))
                emptied_upto(l, "cT", NT - 1, 0)
                emptied_upto(l, "cT", NT - 1, 1)
                for t in range(NT):
                    for i in range(2):
                        rows_times((l, "qn", t, i), cT[:, 0:3, :], wview((l, "uq"), 0), 3, t, 3 * QKB * i, 3 * QKB)
                for t in range(NT):
                    for i in range(2):
                        rows_times((l, "kvn", t, i), cT[:, 3:5, :], wview((l, "uq"), 1), 2, t, 3 * P * i, 3 * P)
                for name, _ in prep_jobs(0):
                    prep(l, name)

                def scores(g):
                    h, t = divmod(g, NT)
                    p, i = divmod(h, 2)
                    kind = PAIRS[p][0]
                    rows = QKB if kind == "B" else HD
                    if t == 0:
                        for name, _ in prep_jobs(p):
                            emptied_upto(l, *name)
                    b = take(l, "S", g)
                    nc.tensor.matmul(b[:, :], qk5[0:rows, p % 2, 0, i, t * P:(t + 1) * P],
                                     qk5[0:rows, p % 2, 1, i, :], start=True, stop=True).then_inc(filled, 1)

                scores(0)
                scores(1)
                def weigh(g):
                    h, t = divmod(g, NT)
                    p, i = divmod(h, 2)
                    kind, pp = PAIRS[p]
                    emptied_upto(l, "PT", g)
                    if t == 0 and l * NH + h >= 2:
                        pe.wait_ge(o_out, l * NH + h - 1)
                    ob = ps[:, ROT + h % 2, :]
                    for k in range(NT):
                        if kind == "B":
                            v = kvn4[:, k, 2 * pp + i, HD:160]
                        else:
                            c = P * pp + (WA if kind == "C" else 0)
                            v = vac3[:, k, c:c + P]
                        last = nc.tensor.matmul(ob[:, t * P:t * P + v.shape[1]], pt[:, g % 2, k * P:(k + 1) * P], v,
                                                start=(k == 0), stop=(k == NT - 1))
                    last.then_inc(pv_done, 1)

                for g in range(STEPS):
                    p = g // 8
                    if g + 2 < STEPS:
                        scores(g + 2)
                    pe.wait_ge(emptied["X"], l * STEPS + g + 1)
                    turn((l, "PT", g), [pr[:, g % 3, k * P:(k + 1) * P] for k in range(NT)])
                    if g:
                        weigh(g - 1)
                    if p + 1 < len(PAIRS):
                        for name, _ in prep_at(p + 1, g % 8):
                            if PAIRS[p + 1][0] == "B":
                                pe.wait_ge(rope_ready, l + 1)
                            prep(l, name)
                weigh(STEPS - 1)
                arrived((l, "o", 0))
                for t in range(NT + 1):
                    if t < NT:
                        pe.wait_ge(y_ready, l * NT + t + 1)
                        for i in range(2):
                            turn((l, "yT", t, i), [on[:, t, (4 * i + k) * P:(4 * i + k + 1) * P] for k in range(4)])
                    if t:
                        emptied_upto(l, "yT", t - 1, 0)
                        emptied_upto(l, "yT", t - 1, 1)
                        rows_times((l, "op", t - 1, 0), hT3, wview((l, "o", 0)), ND, t - 1, 0, 512)
                arrived((l, "o", 1))
                for t in range(NT):
                    rows_times((l, "op", t, 1), hT3, wview((l, "o", 1)), ND, t, 0, 512)
                norm_turn(l, "h2")
                if l == 0:
                    for c in range(CH):
                        arrived((l, "f", c))
                        for f in (2 * c, 2 * c + 1):
                            cols_times((l, "g", f), wview((l, "f", c), 0), (f % 2) * P)
                            cols_times((l, "u", f), wview((l, "f", c), 1), (f % 2) * P)
                    for i in range(2):
                        banks = [take(l, "d", i, t) for t in range(NT)]
                        for c in range(2):
                            arrived((l, "w2", i, c))
                            emptied_upto(l, "u", (c + 1) * FT // 2 - 1)
                            for t in range(NT):
                                for k in range(FT // 2):
                                    f = c * FT // 2 + k
                                    last = nc.tensor.matmul(banks[t], hid[:, f, t * P:(t + 1) * P],
                                                            wview((l, "w2", i, c))[:, k, :],
                                                            start=(f == 0), stop=(f == FT - 1))
                                if c:
                                    last.then_inc(filled, 1)

            pe.sem_inc(gu_filled, UPS)
            pe.sem_inc(y_filled, DNS)
            l = LAYERS - 1
            pe.wait_ge(router_in, 16)
            for t in range(NT):
                rows_times((l, "lg", t), hT3, wr, ND, t, 0, NE)
            pe.wait_ge(lots_ready, 1)
            b = take(l, "rk")
            for t in range(NT):
                for s in range(t + 1):
                    last = nc.tensor.matmul(b[:, t * NE:(t + 1) * NE], tri if s == t else ones, both[:, s, :],
                                            start=(s == 0), stop=(s == t))
            last.then_inc(filled, 1)
            b = take(l, "ct")
            for s in range(NT):
                last = nc.tensor.matmul(b[:, 0:NE], ones, both[:, s, :], start=(s == 0), stop=(s == NT - 1))
            last.then_inc(filled, 1)

            pe.wait_ge(plan_ready, 1)
            pe.wait_ge(emptied["D"], J.emptied(l, "ct"))
            n_units = pe.value_load(plan[0:1, 2 * NU:2 * NU + 1], min_val=1, max_val=NU)

            def unit_body(u, n):
                with pe.Fori(0, FE // UPS) as i:
                    for s in range(UPS):
                        f = u * FE + i * UPS + s
                        if s == 0:
                            pe.wait_ge(turn_out, u * 8 + 6)
                        pe.wait_ge(up_in[s], (u * (FE // UPS) + i + 1) * 32)
                        pe.wait_ge(gu_free, f + 1)
                        gb = ps[:, s, :]
                        for m in range(2):
                            for k in range(ND):
                                last = nc.tensor.matmul(gb[:, m * UNIT:m * UNIT + n], up[s][:, m, k, :], XT[:, k, 0:n],
                                                        start=(k == 0), stop=(k == ND - 1))
                        last.then_inc(gu_filled, 1)
                with pe.Fori(0, ND // DNS) as j:
                    for s in range(DNS):
                        if s == 0:
                            pe.wait_ge(gu_free, u * FE + FE + 4)
                        pe.wait_ge(down_in[s], (u * (ND // DNS) + j + 1) * 16)
                        pe.wait_ge(y_out, u * ND + j * DNS + s + 1)
                        for f in range(FE):
                            last = nc.tensor.matmul(ps[:, 4 + s % 2, 0:n], down[s][:, f, :], eh[:, f, 0:n],
                                                    start=(f == 0), stop=(f == FE - 1))
                        last.then_inc(y_filled, 1)

            def choose(u, held, classes):
                if len(classes) == 1:
                    return unit_body(u, classes[0])
                with pe.If(held < classes[0] + 1):
                    unit_body(u, classes[0])
                with pe.Else():
                    choose(u, held, classes[1:])

            def turn_rows(after):
                for i in range(4):
                    pe.wait_ge(turn_out, after + i + 1)
                    for k in range(2):
                        for r in range(2):
                            last = nc.tensor.transpose(ps[:, 6 + i % 2, (2 * k + r) * P:(2 * k + r + 1) * P],
                                                       rows[:, r, (2 * i + k) * P:(2 * i + k + 1) * P], ident)
                    last.then_inc(turned, 1)

            pe.wait_ge(rows_in, 16)
            turn_rows(0)
            with pe.Fori(0, NU) as u:
                with pe.If(u < n_units):
                    held = pe.value_load(plan[0:1, bass.ds(u + NU, 1)], min_val=0, max_val=UNIT)
                    choose(u, held, CLASSES)
                    pe.wait_ge(rows_in, u * 16 + 32)
                    turn_rows(u * 8 + 4)
                    for i in range(4):
                        if i == 0:
                            pe.wait_ge(y_out, u * ND + ND + 2)
                        pe.wait_ge(turn_out, u * 8 + 8 + i + 1)
                        for k in range(4):
                            d = 4 * (i % 2) + k
                            last = nc.tensor.transpose(ps[:, 6 + i % 2, k * P:(k + 1) * P],
                                                       yT[:, d, (i // 2) * P:(i // 2 + 1) * P], ident)
                        last.then_inc(turned, 1)

        @block.scalar
        def _(act):
            def bank(*name):
                act.wait_ge(filled, J.filled(*name))
                return ps[:, J.bank(*name), :]

            def copy_out(dst, job, n=512):
                nc.scalar.copy(dst, bank(*job)[:, 0:n]).then_inc(emptied["A"], 1)

            roots = [0, 0]

            def root(n):
                roots[0] += 1
                act.wait_ge(sq_done, roots[0])
                nc.scalar.activation(rms[:, 0:n], ssq[:, 0:n], ACT.Sqrt).then_inc(rms_ready, 1)

            links = [0]

            def square(src, col):
                n = src.shape[1]
                if links[0]:
                    act.wait_ge(act_link, links[0])
                links[0] += 1
                nc.scalar.activation(hr[:, 1, 0:n], src, ACT.Square, scale=n ** -0.5,
                                     accum_out=ssq[:, col:col + 1]).then_inc(act_link, 1)

            def own_root(c0, c1):
                roots[1] += 1
                act.wait_ge(act_link, links[0])
                nc.scalar.activation(rms[:, c0:c1], ssq[:, c0:c1], ACT.Sqrt, bias=eps).then_inc(rms_ready, 1)

            def x_root(t):
                square(x3[:, t, :], t)
                own_root(t, t + 1)

            def group(l, i):
                c0, c1 = GROUPS[i]
                act.wait_ge(o_out, l * NH + c1 // HD)
                for t in range(NT):
                    square(on[:, t, c0:c1], 3 * t + i)

            act.dma_start(tab[:, 0:T_COS], a["tables"][:, 0:T_COS]).then_inc(ident_in, 16)
            act.dma_start(g_mix, a["g_mix"][0].partition_broadcast(P)).then_inc(mix_in, 16)
            act.wait_ge(ident_in, 16)

            def split(job):
                l, name, t, i = job
                return hT3[:, 4 * i:4 * i + 4, t * P:(t + 1) * P]

            def prep(l, name):
                p, w = name[1], name[2]
                kind, pp = PAIRS[p]
                if kind == "B":
                    b = bank(l, *name)
                    nc.scalar.copy(qk5[0:QKB, p % 2, 0, name[3], :], b[0:QKB, :]).then_inc(emptied["A"], 1)
                    return
                b = bank(l, *name)
                for i in range(2):
                    last = nc.scalar.mul(qk5[0:HD, p % 2, 0, i, :], b[i * HD:(i + 1) * HD, :], QSCALE[kind])
                last.then_inc(emptied["A"], 1)

            def prep_mine(js, l):
                for name, who in js:
                    if who == "A":
                        prep(l, name)

            def expo(l, g):
                h, t = divmod(g, NT)
                act.wait_ge(nmax_ready, l * STEPS + g + 1)
                if l * STEPS + g >= 3:
                    ll, gg = divmod(l * STEPS + g - 3, STEPS)
                    act.wait_ge(filled, J.filled(ll, "PT", gg))
                if t == 0 and l * NH + h >= 2:
                    act.wait_ge(o_out, l * NH + h - 1)
                src = ps[:, J.bank(l, "S", g), :] if PAIRS[h // 2][0] == "B" else sc[:, g % 2, :]
                nc.scalar.activation(pr[:, g % 3, :], src, ACT.Exp, bias=nmx[:, g % 4:g % 4 + 1],
                                     accum_out=ls[:, h % 2, t:t + 1]).then_inc(emptied["X"], 1)

            for l in range(LAYERS):
                for t in range(NT):
                    if l:
                        act.wait_ge(emptied["D"], J.emptied(l - 1, "d", 1, t))
                    else:
                        act.wait_ge(x_in[t], 16)
                    x_root(t)
                for t in range(NT):
                    copy_out(split((l, "hT", t, 0)), (l, "hT", t, 0))
                for t in range(NT):
                    copy_out(cn[:, t, 0:RQ], (l, "cb", t, 0), RQ)
                root(2 * NT)
                for t in range(NT):
                    copy_out(vac3[:, t, 0:WA], (l, "v", t, 0), WA)
                for t in range(NT):
                    copy_out(cT[:, 0:3, t * P:(t + 1) * P], (l, "cT", t, 0), 3 * P)
                for t in range(NT):
                    for i in range(2):
                        b = bank(l, "qn", t, i)
                        nc.scalar.mul(qn4[:, t, 3 * i:3 * i + 3, :], b[:, 0:3 * QKB], QSCALE["B"])\
                            .then_inc(emptied["A"], 1)
                prep_mine(prep_jobs(0), l)
                expo(l, 0)
                expo(l, 1)
                for g in range(STEPS):
                    if g + 2 < STEPS:
                        expo(l, g + 2)
                    if g % 2 == 0:
                        b = bank(l, "PT", g)
                        if l * STEPS + g >= 2:
                            act.wait_ge(pv_done, l * STEPS + g - 1)
                        nc.scalar.copy(pt[:, 0, :], b).then_inc(emptied["A"], 1)
                    if g // 8 + 1 < len(PAIRS):
                        prep_mine(prep_at(g // 8 + 1, g % 8), l)
                    if g in (HA * NT + 4, (HA + HB) * NT + 4):
                        group(l, 0 if g < (HA + HB) * NT else 1)
                group(l, 2)
                own_root(0, 3 * NT)
                for t in range(NT):
                    copy_out(split((l, "yT", t, 0)), (l, "yT", t, 0))
                for t in range(NT):
                    act.wait_ge(emptied["D"], J.emptied(l, "op", t, 1))
                    x_root(t)
                for t in range(NT):
                    copy_out(split((l, "h2", t, 0)), (l, "h2", t, 0))
                if l == 0:
                    for f in range(FT):
                        b = bank(l, "g", f)
                        if f >= 2:
                            act.wait_ge(emptied["D"], J.emptied(l, "u", f - 2))
                        nc.scalar.activation(sil[:, f % 2, :], b, ACT.Silu).then_inc(emptied["A"], 1)
            act.wait_ge(gates_sub, 1)
            nc.scalar.activation(eg, gap, ACT.Exp).then_inc(gates_exp, 1)
            act.wait_ge(plan_ready, 1)
            act.sem_inc(turn_out, 2)
            act.sem_inc(y_stored, 16)
            n_units = act.value_load(plan[0:1, 2 * NU:2 * NU + 1], min_val=1, max_val=NU)
            for i in range(4):
                act.wait_ge(turned, i + 1)
                nc.scalar.copy(XT[:, 2 * i:2 * i + 2, :], ps[:, 6 + i % 2, :]).then_inc(turn_out, 1)
            with act.Fori(0, NU) as u:
                with act.If(u < n_units):
                    with act.Fori(0, FE // UPS) as i:
                        for s in range(UPS):
                            act.wait_ge(gu_filled, u * FE + i * UPS + (s + 1 + UPS))
                            act.wait_ge(gu_free, u * FE + i * UPS + s + 3)
                            nc.scalar.activation(esil[:, s % 2, :], ps[:, s, 0:UNIT], ACT.Silu).then_inc(e_silu, 1)
                    for i in range(4):
                        act.wait_ge(turned, u * 8 + i + 5)
                        nc.scalar.copy(XT[:, 2 * i:2 * i + 2, :], ps[:, 6 + i % 2, :]).then_inc(turn_out, 1)
                    for i in range(4):
                        act.wait_ge(turned, u * 8 + i + 9)
                        if i == 0:
                            act.wait_ge(y_stored, u * 16 + 16)
                        nc.scalar.copy(yrow[:, i // 2, (i % 2) * 512:(i % 2) * 512 + 512], ps[:, 6 + i % 2, :])\
                            .then_inc(turn_out, 1)
                    act.wait_ge(turn_out, u * 8 + 14)
                    act.dma_start(y_dram[bass.ds(u * UNIT, UNIT), :].rearrange("(b p) d -> p b d", p=P), yrow)\
                        .then_inc(y_stored, 16)
            for t in range(NT):
                act.wait_ge(sums_ready, t + 1)
                x_root(t)

        @block.vector
        def _(dve):
            links = [0]

            def link(ins):
                links[0] += 1
                ins.then_inc(dve_link, 1)
                dve.wait_ge(dve_link, links[0])

            def bank(*name):
                dve.wait_ge(filled, J.filled(*name))
                return ps[:, J.bank(*name), :]

            def copy_out(dst, job, n=512):
                nc.vector.tensor_copy(dst, bank(*job)[:, 0:n]).then_inc(emptied["D"], 1)

            def square(src, scratch, col, width):
                link(nc.vector.tensor_tensor_reduce(scratch, src, src, 1.0 / width, 0.0, ALU.mult, ALU.add,
                                                    ssq[:, col:col + 1]))

            roots = [0]

            def roots_in(c0, c1):
                roots[0] += 1
                dve.wait_ge(rms_ready, roots[0])
                link(nc.vector.reciprocal(rr[:, c0:c1], rms[:, c0:c1]))

            def inverse(n):
                nc.vector.tensor_scalar(ssq[:, 0:n], ssq[:, 0:n], EPS, None, ALU.add).then_inc(sq_done, 1)
                roots_in(0, n)

            def norm_rows(l, name, gain, ready):
                out = h4 if name == "h2" else mixed
                for t in range(NT):
                    ready(t)
                    if t == NT - 1:
                        copy_out(hT3[:, 4:8, 0:P], (l, name, 0, 1))
                    roots_in(t, t + 1)
                    nc.vector.scalar_tensor_tensor(out=out[:, t, :], in0=x3[:, t, :], scalar=rr[:, t:t + 1],
                                                   in1=gain, op0=ALU.mult, op1=ALU.mult).then_inc(h_ready, 1)
                for t in range(1, NT):
                    copy_out(hT3[:, 4:8, t * P:(t + 1) * P], (l, name, t, 1))

            def prep_mine(js, l):
                for name, who in js:
                    if who != "D":
                        continue
                    p = name[1]
                    b = bank(l, *name)
                    if PAIRS[p][0] == "B":
                        nc.vector.tensor_copy(qk5[0:QKB, p % 2, 1, name[3], :], b[0:QKB, :])\
                            .then_inc(emptied["D"], 1)
                    else:
                        for i in range(2):
                            last = nc.vector.tensor_copy(qk5[0:HD, p % 2, 1, i, :], b[i * HD:(i + 1) * HD, :])
                        last.then_inc(emptied["D"], 1)

            def row_max(l, g):
                h, t = divmod(g, NT)
                kind = PAIRS[h // 2][0]
                b = bank(l, "S", g)
                if l * STEPS + g >= 4:
                    dve.wait_ge(emptied["X"], l * STEPS + g - 3)
                m = mx[:, g % 4:g % 4 + 1]
                if kind == "B":
                    link(nc.vector.tensor_reduce(m, b, AX.X, ALU.max))
                else:
                    n = h if kind == "A" else h - HB
                    if t == 0:
                        dve.wait_ge(strip_ready, l * (HA + HC) + n + 1)
                    if l * STEPS + g >= 2:
                        dve.wait_ge(emptied["X"], l * STEPS + g - 1)
                    s = SEQ - P - P * t
                    nc.vector.tensor_tensor_reduce(sc[:, g % 2, :], b, st[:, n % 2, s:s + SEQ], 1.0, NEG * 4,
                                                   ALU.add, ALU.max, m).then_inc(emptied["D"], 1)
                    dve.wait_ge(emptied["D"], J.emptied(l, "S", g))
                nc.vector.tensor_scalar(nmx[:, g % 4:g % 4 + 1], m, -1.0, None, ALU.mult).then_inc(nmax_ready, 1)

            def head_out(l, h):
                p, i = divmod(h, 2)
                kind, pp = PAIRS[p]
                dve.wait_ge(emptied["X"], l * STEPS + NT * h + NT)
                link(nc.vector.reciprocal(rl[:, h % 2, :], ls[:, h % 2, :]))
                dve.wait_ge(pv_done, l * STEPS + NT * h + NT)
                c = ROPE if kind == "B" else HD * i
                o = ps[:, ROT + h % 2, :].rearrange("p (t c) -> p t c", t=NT)[:, :, c:c + HD]
                r = rl[:, h % 2, :].unsqueeze(2).to_broadcast([P, NT, HD])
                nc.vector.tensor_tensor(on[:, :, h * HD:(h + 1) * HD], o, r, ALU.mult).then_inc(o_out, 1)

            def rotate(x1, x2, cos, sin, n):
                w = [sc_flat[:, i * 384:i * 384 + n * 16].rearrange("p (n c) -> p n c", c=16) for i in range(2)]
                w += [st_flat[:, i * 384:i * 384 + n * 16].rearrange("p (n c) -> p n c", c=16) for i in range(2)]
                for dst, s, f in ((w[0], x1, cos), (w[1], x2, sin), (w[2], x1, sin), (w[3], x2, cos)):
                    last = nc.vector.tensor_tensor(dst, s, f, ALU.mult)
                link(last)
                nc.vector.tensor_tensor(x1, w[0], w[1], ALU.subtract)
                return nc.vector.tensor_tensor(x2, w[2], w[3], ALU.add)

            sc_flat = soft[:, 5 * SEQ:7 * SEQ]
            st_flat = soft[:, 3 * SEQ:5 * SEQ]
            def add_to_x(l, job, t, i):
                xs = x3[:, t, 512 * i:512 * i + 512]
                nc.vector.tensor_tensor(xs, bank(l, *job), xs, ALU.add).then_inc(emptied["D"], 1)

            for l in range(LAYERS):
                if l:
                    dve.wait_ge(gains_in, 16 * (2 * NG - 1))
                    norm_rows(l, "hT", g_mix, lambda t: add_to_x(l - 1, ("d", 1, t), t, 1))
                else:
                    dve.wait_ge(mix_in, 16)
                    norm_rows(l, "hT", g_mix, lambda t: dve.wait_ge(x_in[t], 16))
                    dve.wait_ge(gains_in, 16 * (NG - 1))
                    dve.wait_ge(tab_in, 16)
                for t in range(NT):
                    copy_out(cn[:, t, RQ:DB], (l, "cb", t, 1), RKV + ROPE)
                dve.wait_ge(emptied["A"], J.emptied(l, "cb", NT - 1, 0))
                dve.wait_ge(emptied["D"], J.emptied(l, "cb", NT - 1, 1))
                for t in range(NT):
                    square(cn[:, t, 0:RQ], hr[:, 0, 0:RQ], t, RQ)
                    square(cn[:, t, RQ:RQ + RKV], hr[:, 0, 0:RKV], NT + t, RKV)
                inverse(2 * NT)
                for t in range(NT):
                    nc.vector.scalar_tensor_tensor(out=cn[:, t, 0:RQ], in0=cn[:, t, 0:RQ], scalar=rr[:, t:t + 1],
                                                   in1=g_q, op0=ALU.mult, op1=ALU.mult)
                    kv = cn[:, t, RQ:RQ + RKV]
                    nc.vector.scalar_tensor_tensor(out=kv, in0=kv, scalar=rr[:, NT + t:NT + t + 1],
                                                   in1=g_kv, op0=ALU.mult, op1=ALU.mult).then_inc(lat_ready, 1)
                for t in range(NT):
                    copy_out(vac3[:, t, WA:WA + WC], (l, "v", t, 1), WC)
                kr = cn[:, :, RQ + RKV:DB]
                cosk = tab[:, T_COS:T_SIN].rearrange("p (t h c) -> p t h c", t=NT, h=HB)[:, :, 0, :]
                sink = tab[:, T_SIN:T_DIST].rearrange("p (t h c) -> p t h c", t=NT, h=HB)[:, :, 0, :]
                link(rotate(kr[:, :, 0:16], kr[:, :, 16:32], cosk, sink, NT))
                for t in range(NT):
                    copy_out(cT[:, 3:5, t * P:(t + 1) * P], (l, "cT", t, 1), 2 * P)
                for t in range(NT):
                    for i in range(2):
                        b = bank(l, "kvn", t, i)[:, 0:3 * P].rearrange("p (h w c) -> p h w c", h=3, w=2)
                        kv = kvn4[:, t, 3 * i:3 * i + 3, :]
                        nc.vector.tensor_copy(kv[:, :, 0:HD], b[:, :, 0, :])
                        nc.vector.tensor_copy(kv[:, :, QKB:160], b[:, :, 1, :]).then_inc(emptied["D"], 1)
                prep_mine(prep_jobs(0), l)
                for t in range(NT):
                    nc.vector.tensor_copy(kvn4[:, t, :, HD:QKB], kr[:, t, :].unsqueeze(1).to_broadcast([P, HB, ROPE]))
                dve.wait_ge(emptied["A"], J.emptied(l, "qn", NT - 1, 1))
                q3 = qn.rearrange("p (n c) -> p n c", c=QKB)
                cosq = tab[:, T_COS:T_SIN].rearrange("p (n c) -> p n c", c=16)
                sinq = tab[:, T_SIN:T_DIST].rearrange("p (n c) -> p n c", c=16)
                rotate(q3[:, :, HD:HD + 16], q3[:, :, HD + 16:QKB], cosq, sinq, NT * HB).then_inc(rope_ready, 1)
                dve.wait_ge(rope_ready, l + 1)
                row_max(l, 0)
                row_max(l, 1)
                for g in range(STEPS):
                    if g + 2 < STEPS:
                        row_max(l, g + 2)
                    if g % 2 == 1:
                        b = bank(l, "PT", g)
                        if l * STEPS + g >= 2:
                            dve.wait_ge(pv_done, l * STEPS + g - 1)
                        nc.vector.tensor_copy(pt[:, 1, :], b).then_inc(emptied["D"], 1)
                    if g % NT == 1 and g > 1:
                        head_out(l, g // NT - 1)
                    if g // 8 + 1 < len(PAIRS):
                        prep_mine(prep_at(g // 8 + 1, g % 8), l)
                head_out(l, NH - 1)
                dve.wait_ge(o_out, (l + 1) * NH)
                roots_in(0, 3 * NT)
                for t in range(NT + 2):
                    if t < NT:
                        for i, (c0, c1) in enumerate(GROUPS):
                            last = nc.vector.scalar_tensor_tensor(out=on[:, t, c0:c1], in0=on[:, t, c0:c1],
                                                                  scalar=rr[:, 3 * t + i:3 * t + i + 1],
                                                                  in1=g_out[:, c0:c1], op0=ALU.mult, op1=ALU.mult)
                        last.then_inc(y_ready, 1)
                    if 1 <= t <= NT:
                        copy_out(hT3[:, 4:8, (t - 1) * P:t * P], (l, "yT", t - 1, 1))
                    if t >= 2:
                        add_to_x(l, ("op", t - 2, 0), t - 2, 0)
                norm_rows(l, "h2", g_ffn, lambda t: add_to_x(l, ("op", t, 1), t, 1))
                if l == 0:
                    nc.vector.memset(small[:, 255:256], 0.0).then_inc(gains_free, 1)
                    for f in range(FT):
                        b = bank(l, "u", f)
                        dve.wait_ge(emptied["A"], J.emptied(l, "g", f))
                        nc.vector.tensor_tensor(hid[:, f, :], b, sil[:, f % 2, :], ALU.mult)\
                            .then_inc(emptied["D"], 1)
                    for t in range(NT):
                        add_to_x(l, ("d", 0, t), t, 0)

            l = LAYERS - 1
            tt, V = nc.vector.tensor_tensor, nc.vector
            for t in range(NT):
                V.tensor_copy(logit[:, t, :], bank(l, "lg", t)[:, 0:NE]).then_inc(emptied["D"], 1)
            dve.wait_ge(emptied["D"], J.emptied(l, "lg", NT - 1))
            for t in range(NT):
                last = V.max(top[:, t, :], logit[:, t, :])
            link(last)
            for t in range(NT):
                last = V.max_index(pick[:, t, :], top[:, t, :], logit[:, t, :])
            link(last)
            tt(gap, top[:, :, 1], top[:, :, 0], ALU.subtract).then_inc(gates_sub, 1)
            link(V.tensor_copy(pickf, pick[:, :, 0:2]))
            eno = tab[:, T_E:T_E + NE].unsqueeze(1).to_broadcast([P, NT, NE])
            for j, lot in enumerate((lot0, lot1)):
                last = tt(lot, eno, pickf[:, :, j:j + 1].to_broadcast([P, NT, NE]), ALU.is_equal)
            link(last)
            tt(both, lot0, lot1, ALU.add).then_inc(lots_ready, 1)
            dve.wait_ge(gates_exp, 1)
            link(V.tensor_scalar(den, eg, 1.0, None, ALU.add))
            link(V.reciprocal(g0, den))
            link(tt(g1, eg, g0, ALU.mult))
            V.tensor_copy(rank, bank(l, "rk")[:, 0:NT * NE].rearrange("p (t e) -> p t e", t=NT))\
                .then_inc(emptied["D"], 1)
            V.tensor_copy(cnt, bank(l, "ct")[:, 0:NE]).then_inc(emptied["D"], 1)
            dve.wait_ge(emptied["D"], J.emptied(l, "ct"))
            V.tensor_scalar(more, cnt, float(UNIT), None, ALU.is_gt)
            link(V.tensor_scalar(units, cnt, 0.0, None, ALU.is_gt))
            link(tt(units, units, more, ALU.add))
            link(V.tensor_scalar(units[:, 0:1], units[:, 0:1], 1.0, None, ALU.max))
            link(V.tensor_tensor_scan(incl, tab[:, T_ONES:T_ONES + NE], units, 0.0, ALU.mult, ALU.add))
            link(tt(excl, incl, units, ALU.subtract))
            link(V.tensor_scalar(first, excl, float(UNIT), None, ALU.mult))
            link(tt(rank, rank, first.unsqueeze(1).to_broadcast([P, NT, NE]), ALU.add))
            for j, lot in enumerate((lot0, lot1)):
                link(tt(hit, lot, rank, ALU.mult))
                link(V.tensor_reduce(slotf[:, :, j], hit, AX.X, ALU.add))
            V.tensor_copy(slot, slotf.rearrange("p t j -> p (t j)")).then_inc(slots_ready, 1)
            unit = tab[:, T_UNIT:T_UNIT + NU * NE].rearrange("p (u e) -> p u e", u=NU)

            def over(v):
                return v.unsqueeze(1).to_broadcast([P, NU, NE])

            tt(past, unit, over(incl), ALU.is_ge)
            link(tt(owns, unit, over(excl), ALU.is_ge))
            link(tt(owns, owns, past, ALU.subtract))
            link(V.tensor_reduce(planf[:, 0:NU], past, AX.X, ALU.add))
            link(tt(tot, cnt, first, ALU.add))
            link(V.scalar_tensor_tensor(out=left, in0=unit, scalar=-float(UNIT), in1=over(tot),
                                        op0=ALU.mult, op1=ALU.add))
            link(tt(left, left, owns, ALU.mult))
            link(V.tensor_reduce(planf[:, NU:2 * NU], left, AX.X, ALU.add))
            link(V.tensor_scalar(planf[:, 0:NU], planf[:, 0:NU], float(NE - 1), None, ALU.min))
            link(V.tensor_scalar(planf[:, NU:2 * NU], planf[:, NU:2 * NU], float(UNIT), None, ALU.min))
            V.tensor_copy(planf[:, 2 * NU + 1:3 * NU], planf[:, 1:NU])
            V.memset(planf[:, 3 * NU:3 * NU + 2], 0.0)
            link(V.tensor_copy(planf[:, 2 * NU:2 * NU + 1], incl[:, NE - 1:NE]))
            V.tensor_copy(plan, planf).then_inc(plan_ready, 1)
            dve.wait_ge(plan_ready, 1)
            dve.sem_inc(gu_free, 4)
            dve.sem_inc(y_out, 2)
            n_units = dve.value_load(plan[0:1, 2 * NU:2 * NU + 1], min_val=1, max_val=NU)
            with dve.Fori(0, NU) as u:
                with dve.If(u < n_units):
                    with dve.Fori(0, FE // UPS) as i:
                        for s in range(UPS):
                            dve.wait_ge(e_silu, u * FE + i * UPS + s + 1)
                            tt(eh[:, bass.ds(i * UPS + s, 1), :], ps[:, s:s + 1, UNIT:2 * UNIT],
                               esil[:, s % 2:s % 2 + 1, :], ALU.mult).then_inc(gu_free, 1)
                    with dve.Fori(0, ND // 2) as j:
                        for s in range(2):
                            dve.wait_ge(y_filled, u * ND + j * 2 + s + 1 + DNS)
                            V.tensor_copy(yT[:, bass.ds(j * 2 + s, 1), :], ps[:, 4 + s:5 + s, 0:UNIT]).then_inc(y_out, 1)
            dve.wait_ge(final_gain, 16)
            for t in range(NT + 1):
                if t < NT:
                    dve.wait_ge(gathered[t], 32)
                    for j, gt in enumerate((g0, g1)):
                        last = V.scalar_tensor_tensor(out=x3[:, t, :], in0=back[:, 2 * t + j, :], scalar=gt[:, t:t + 1],
                                                      in1=x3[:, t, :], op0=ALU.mult, op1=ALU.add)
                        if j == 0:
                            link(last)
                    last.then_inc(sums_ready, 1)
                if t:
                    roots_in(t - 1, t)
                    V.scalar_tensor_tensor(out=x3[:, t - 1, :], in0=x3[:, t - 1, :], scalar=rr[:, t - 1:t],
                                           in1=g_mix, op0=ALU.mult, op1=ALU.mult).then_inc(fin_ready, 1)


def shape_tables():
    import numpy as np

    tab = np.zeros((P, T_W), np.float32)
    tab[:, T_ID:T_ID + P] = np.eye(P)
    tab[:, T_EPS] = EPS
    inv = np.float32(10000.0) ** (-np.arange(0, ROPE, 2, dtype=np.float32) / np.float32(ROPE))
    ang = np.arange(SEQ, dtype=np.float32)[:, None] * inv.astype(np.float32)[None, :]
    for at, f in ((T_COS, np.cos), (T_SIN, np.sin)):
        v = f(ang).astype(np.float32).reshape(NT, P, 1, 16).transpose(1, 0, 2, 3)
        tab[:, at:at + NT * HB * 16] = np.broadcast_to(v, (P, NT, HB, 16)).reshape(P, -1)
    gap = np.abs(np.arange(STRIP)[None, :] - (SEQ - P) - np.arange(P)[:, None])
    reach = (gap <= 64).astype(int) + ((gap % 4 == 0) & (gap <= 256)) + ((gap % 16 == 0) & (gap <= 1024))
    tab[:, T_DIST:T_DIST + STRIP] = gap
    tab[:, T_AMASK:T_AMASK + STRIP] = np.where(reach > 0, np.log(np.maximum(reach, 1)), NEG)
    qc = np.arange(P)[:, None] % GRID
    first = np.clip(qc - NAC // 2, 0, GRID - NAC)
    kc = np.arange(GRID)[None, :]
    tab[:, T_CMASK:T_CMASK + GRID] = np.where((kc >= first) & (kc < first + NAC), 0.0, NEG)
    tab[:, T_TRI:T_TRI + P] = np.arange(P)[:, None] < np.arange(P)[None, :]
    tab[:, T_ONES:T_ONES + P] = 1.0
    tab[:, T_UNIT:T_UNIT + NU * NE] = np.repeat(np.arange(NU), NE)[None, :]
    tab[:, T_E:T_E + NE] = np.arange(NE)[None, :]
    return tab


_INS = ["x", "g_mix", "w_in", "g_q", "g_kv", "w_uq", "w_ukv", "rpb", "g_out_a", "g_out_b", "g_out_c", "w_o",
        "g_ffn", "w1", "w3", "w2", "w_router", "e_w1", "e_w3", "e_w2", "g_final"]


def kernel(**inputs):
    import numpy as _np
    import concourse.bacc as _bacc
    from concourse import mybir as _mybir
    from concourse.bass_utils import run_bass_kernel_spmd as _run

    nc = _bacc.Bacc("TRN2", target_bir_lowering=False, num_devices=1)
    arrays, aps = {}, {}
    for name in _INS + ["tables"]:
        v = shape_tables() if name == "tables" else _np.ascontiguousarray(inputs[name])
        arrays[f"in_{name}_dram"] = v
        aps[name] = nc.dram_tensor(f"in_{name}_dram", v.shape, _mybir.dt.from_np(v.dtype), kind="ExternalInput").ap()
    aps["out"] = nc.dram_tensor("out_0_dram", (1, SEQ, D), F32, kind="ExternalOutput").ap()
    trunk(nc, aps)
    r = _run(nc, [arrays], core_ids=[0])
    return r.results[0]["out_0_dram"]
```

```python
from contextlib import ExitStack

import concourse.bass as bass
from concourse import mybir

F32 = mybir.dt.float32
F32R = mybir.dt.float32r
U32 = mybir.dt.uint32
I32 = mybir.dt.int32
ALU = mybir.AluOpType
ACT = mybir.ActivationFunctionType
AX = mybir.AxisListType

P = 128
SEQ, D, LAYERS = 512, 1024, 2
NT = SEQ // P
ND = D // P
HD = 64
HA, HB, HC = 6, 6, 4
NH = HA + HB + HC
RQ, RKV, ROPE = 384, 256, 32
QKB = HD + ROPE
WA, WB, WC = HA * HD, HB * HD, HC * HD
IN_COLS = 3 * WA + RQ + RKV + ROPE + 3 * WC
COL_QA, COL_KA, COL_VA = 0, WA, 2 * WA
COL_B = 3 * WA
COL_QC = COL_B + RQ + RKV + ROPE
COL_KC, COL_VC = COL_QC + WC, COL_QC + 2 * WC
DB = RQ + RKV + ROPE
DFF = 2816
NE, DFE = 8, 3584
GRID, NAR, NAC = 64, 8, 16
EPS = 1e-6
NEG = -1e30
STRIP = 2 * SEQ - P
UNIT = 2 * P
NU = (2 * SEQ) // UNIT + NE - 1
PADW = 128
RING = 6144

T_ID = 0
T_EPS = T_ID + P
T_COS = T_EPS + 1
T_SIN = T_COS + NT * HB * 16
T_DIST = T_SIN + NT * HB * 16
T_AMASK = T_DIST + STRIP
T_CMASK = T_AMASK + STRIP
T_TRI = T_CMASK + GRID
T_ONES = T_TRI + P
T_UNIT = T_ONES + P
T_E = T_UNIT + NU * NE
T_W = T_E + NE

PAIRS = [("A", 0), ("A", 1), ("A", 2), ("B", 0), ("B", 1), ("B", 2), ("C", 0), ("C", 1)]
STEPS = NH * NT
FT = DFF // P
FE = DFE // P
UPS = 4
DNS = 4
ARENA = 25472
DOWN, GATE_UP, ROWS = FE * P, 2 * D, 2 * D
TURNS = [("row", 0), ("row", 1), ("y", 0), ("row", 2), ("y", 1), ("row", 3), ("y", 2), None, ("y", 3)]
TURN_ORDER = [j for j in TURNS if j]
CLASSES = [128, 132, 136, 140, 144, 148, 152, 156, 160, 168, 176, 184, 192, 208, 224, 256]
HIGH = -(1 << 12)
WS = 3
VS = 3
GROUPS = [(0, WA), (WA, WA + WB), (WA + WB, D)]
CH = DFF // UNIT
SLOPES = [2.0 ** (-8.0 * (h + 1) / HA) for h in range(HA)]
QSCALE = {"A": HD ** -0.5, "B": QKB ** -0.5, "C": HD ** -0.5}
ROT = 6


def front_jobs():
    j = []
    for t in range(NT + 1):
        j += [(("hT", t, i), "AD"[i]) for i in range(2)] if t < NT else []
        j += [(("cb", t - 1, i), "AD"[i]) for i in range(2)] if t else []
    j += [(("v", t, i), "AD"[i]) for t in range(NT) for i in range(2)]
    j += [(("cT", t, i), "AD"[i]) for t in range(NT) for i in range(2)]
    j += [(("qn", t, i), "A") for t in range(NT) for i in range(2)]
    j += [(("kvn", t, i), "D") for t in range(NT) for i in range(2)]
    j += prep_jobs(0)
    j += [(("S", 0), "D"), (("S", 1), "D")]
    for g in range(STEPS):
        if g + 2 < STEPS:
            j.append((("S", g + 2), "X" if PAIRS[(g + 2) // 8][0] == "B" else "D"))
        j.append((("PT", g), "AD"[g % 2]))
        p, k = g // 8, g % 8
        if p + 1 < len(PAIRS):
            j += prep_at(p + 1, k)
    for t in range(NT + 1):
        j += [(("yT", t, i), "AD"[i]) for i in range(2)] if t < NT else []
        j += [(("op", t - 1, 0), "D")] if t else []
    return j


def second_norm_jobs(l):
    j = []
    for t in range(NT + 2):
        j += [(("op", t, 1), "D")] if t < NT else []
        j += [(("h2", t - 1, i), "AD"[i]) for i in range(2)] if 1 <= t <= NT else []
        j += [(("lg", t - 2), "D")] if t >= 2 and l == LAYERS - 1 else []
    return j


def prep_jobs(p):
    if PAIRS[p][0] == "B":
        return [(("qk", p, w, i), "AD"[w]) for i in range(2) for w in range(2)]
    return [(("qk", p, w), "AD"[w]) for w in range(2)]


def prep_at(p, k):
    js = prep_jobs(p)
    at = [1, 2, 3, 4] if len(js) == 4 else [1, 3]
    return [js[at.index(k)]] if k in at else []


def dense_jobs():
    j = [((m, f), "AD"[m == "u"]) for f in range(FT) for m in ("g", "u")]
    j += [(("d", i, t), "D") for i in range(2) for t in range(NT)]
    return j


def moe_front_jobs():
    return [(("lt",), "D"), (("rk",), "D")]


def split_order():
    order = [("w", 0), ("w", 1), ("x", 0), ("w", 2), ("x", 1), ("x", 2), ("x", 3)]
    order += [("w", j) for j in range(WS, 2 * FT)] + [("h", 0), ("v", 0), ("v", 1)]
    for f in range(1, FT):
        order += [("h", f), ("v", f + 1)]
    return order + [("v", n) for n in range(FT + 1, 2 * FT)]


SPLITS = split_order()


def split_of(kind, j):
    return SPLITS.index((kind, j))


class Jobs:

    def __init__(self):
        self.at, self.who, self.nth, self.count = {}, [], [], {"A": 0, "D": 0, "X": 0}
        self.exps = 0
        for l in range(LAYERS):
            for name, who in front_jobs() + second_norm_jobs(l) + (dense_jobs() if l == 0 else moe_front_jobs()):
                self.at[(l,) + name] = len(self.who)
                self.who.append(who)
                if who == "X":
                    self.nth.append(l * STEPS + name[1] + 1)
                else:
                    self.count[who] += 1
                    self.nth.append(self.count[who])
        self.n = len(self.who)

    def bank(self, *name):
        return self.at[name] % ROT

    def filled(self, *name):
        return self.at[name] + 1

    def emptied(self, *name):
        return self.nth[self.at[name]]


def trunk(nc, a):
    J = Jobs()
    ctx = ExitStack()
    with ctx:
        def sb(name, cols, dt=F32, rows=P):
            return ctx.enter_context(nc.sbuf_tensor(name, [rows, cols], dt))

        def sem(name):
            return ctx.enter_context(nc.semaphore(name))

        ps = ctx.enter_context(nc.psum_tensor("ps", [P, 8, 512], F32))
        x = sb("x_rows", NT * D)
        hT_at = nc.sbuf_base
        hT = sb("hT", ND * SEQ)
        ring = sb("weight_ring", 2 * RING)
        gains = sb("gains", 3 * D + RQ + RKV)
        tab = sb("tables", T_W)
        small = sb("small", 256)
        A0_at = nc.sbuf_base
        A0 = sb("attention_arena", ARENA)
        off = [0]

        def part(n):
            s = off[0]
            off[0] += n
            assert off[0] <= ARENA, off[0]
            return A0[:, s:s + n]

        lat = part(NT * DB + 5 * SEQ)
        qk = part(2 * 2 * 2 * SEQ)
        kvn = part(NT * HB * 160)
        qn = part(NT * HB * QKB)
        vac = part(NT * (WA + WC))
        soft = part(7 * SEQ)
        strips = part(2 * STRIP)
        hrow = part(2 * D)

        x3 = x[:, :].rearrange("p (t d) -> p t d", t=NT)
        hT3 = hT[:, :].rearrange("p (k s) -> p k s", k=ND)
        qk5 = qk.rearrange("p (b w h s) -> p b w h s", b=2, w=2, h=2)
        kvn4 = kvn.rearrange("p (t h c) -> p t h c", t=NT, h=HB)
        qn4 = qn.rearrange("p (t h c) -> p t h c", t=NT, h=HB)
        cn = lat[:, 0:NT * DB].rearrange("p (t c) -> p t c", t=NT)
        cT = lat[:, NT * DB:].rearrange("p (k s) -> p k s", k=5)
        on = lat[:, 0:NT * D].rearrange("p (t d) -> p t d", t=NT)
        vac3 = vac.rearrange("p (t c) -> p t c", t=NT)
        pr = soft[:, 0:3 * SEQ].rearrange("p (b s) -> p b s", b=3)
        pt = soft[:, 3 * SEQ:5 * SEQ].rearrange("p (b s) -> p b s", b=2)
        sc = soft[:, 5 * SEQ:7 * SEQ].rearrange("p (b s) -> p b s", b=2)
        st = strips.rearrange("p (b s) -> p b s", b=2)
        hr = hrow.rearrange("p (b d) -> p b d", b=2)
        at_vac = NT * DB + 5 * SEQ + 2 * 2 * 2 * SEQ + NT * HB * (160 + QKB)
        at_parts = (FT + 2) * SEQ
        mixed = A0[:, at_parts:at_parts + NT * D].rearrange("p (t d) -> p t d", t=NT)
        g_mix, g_ffn, g_out = (gains[:, i * D:(i + 1) * D] for i in range(3))
        g_q = gains[:, 3 * D:3 * D + RQ]
        g_kv = gains[:, 3 * D + RQ:3 * D + RQ + RKV]
        ident = tab[:, T_ID:T_ID + P]
        eps = tab[:, T_EPS:T_EPS + 1]
        ones = tab[:, T_ONES:T_ONES + P]
        tri = tab[:, T_TRI:T_TRI + P]
        hid = A0[:, 0:FT * SEQ].rearrange("p (f s) -> p f s", f=FT)
        x_high = nc.alloc_sbuf_tensor_at("x_high", [P, ND * SEQ], F32R, offset=hT_at)
        x_low = nc.alloc_sbuf_tensor_at("x_low", [P, ND * SEQ], F32R, offset=A0_at + 4 * at_parts)
        w_parts = nc.alloc_sbuf_tensor_at("w_parts", [P, WS * 2 * D], F32R, offset=A0_at + 4 * (FT + 10) * SEQ)
        xh3, xl3 = (v[:, :].rearrange("p (k s) -> p k s", k=ND) for v in (x_high, x_low))
        h_high = nc.alloc_sbuf_tensor_at("h_high", [P, FT * SEQ], F32R, offset=A0_at)
        h_low0 = nc.alloc_sbuf_tensor_at("h_low_0", [P, SEQ], F32R, offset=A0_at + 4 * (FT + 26) * SEQ)
        hh3 = h_high[:, :].rearrange("p (f s) -> p f s", f=FT)
        hl3 = [h_low0[:, :]] + [x_low[:, i * SEQ:(i + 1) * SEQ] for i in range(ND)] \
            + [x_high[:, i * SEQ:(i + 1) * SEQ] for i in range(ND)] \
            + [w_parts[:, i * SEQ:(i + 1) * SEQ] for i in range(FT - 1 - 2 * ND)]
        v_parts = [w_parts[:, o:o + 2 * SEQ].rearrange("p (j c) -> p j c", j=2) for o in (4 * D, 5 * D, 3 * D)]
        w5 = w_parts[:, :].rearrange("p (b j k c) -> p b j k c", b=WS, j=2, k=ND)
        at = (FT + 22) * SEQ
        high = A0[:, at:at + 2 * D].rearrange("p (b k c) -> p b k c", b=2, k=ND)
        sil = A0[:, FT * SEQ:(FT + 2) * SEQ].rearrange("p (b s) -> p b s", b=2)

        ssq = small[:, 0:12]
        rms = small[:, 12:24]
        rr = small[:, 24:36]
        mx = small[:, 36:40]
        nmx = small[:, 40:44]
        ls = small[:, 44:52].rearrange("p (b t) -> p b t", b=2)
        rl = small[:, 52:60].rearrange("p (b t) -> p b t", b=2)

        down_at = [ring[:, DOWN * i:DOWN * (i + 1)] for i in range(DNS - 1)] + [A0[:, 0:DOWN]]
        down = [v.rearrange("p (f c) -> p f c", f=FE) for v in down_at]
        esil = ring[:, (DNS - 1) * DOWN:(DNS - 1) * DOWN + 2 * UNIT].rearrange("p (b s) -> p b s", b=2)
        at = DOWN
        eh = A0[:, at:at + FE * UNIT].rearrange("p (f s) -> p f s", f=FE)
        at += FE * UNIT
        yT = A0[:, at:at + ND * UNIT].rearrange("p (k s) -> p k s", k=ND)
        at += ND * UNIT
        rows = A0[:, at:at + ROWS].rearrange("p (b d) -> p b d", b=2)
        at += ROWS
        yrow = A0[:, at:at + ROWS].rearrange("p (b d) -> p b d", b=2)
        at += ROWS
        up = [A0[:, at + GATE_UP * i:at + GATE_UP * (i + 1)].rearrange("p (m k c) -> p m k c", m=2, k=ND)
              for i in range(UPS)]
        h4 = on
        XT = hT[:, 0:ND * UNIT].rearrange("p (k s) -> p k s", k=ND)
        back = A0[:, 0:8 * D].rearrange("p (n d) -> p n d", n=2 * NT)
        used = [0]

        def rt(*shape):
            n = 1
            for d in shape:
                n *= d
            v = gains[:, 2 * D + used[0]:2 * D + used[0] + n]
            used[0] += n
            return v.rearrange("p (a b) -> p a b", a=shape[0]) if len(shape) == 2 else v

        logit, top, lot0, lot1, both = (rt(NT, NE) for _ in range(5))
        pick = rt(NT * NE).bitcast(U32).rearrange("p (t e) -> p t e", t=NT)
        rank, hit = rt(NT, NE), rt(NT, NE)
        pickf, slotf = rt(NT, 2), rt(NT, 2)
        gap, eg, den, g0, g1 = (rt(NT) for _ in range(5))
        logitT = A0[0:NE, at_vac:at_vac + SEQ]
        tile_cnt = rt(NT, NE)
        cnt, more, units, incl, excl, first, tot = (rt(NE) for _ in range(7))
        past, owns, left = rt(NU, NE), rt(NU, NE), rt(NU, NE)
        planf = rt(3 * NU + 2)
        plan = rt(3 * NU + 2).bitcast(I32)
        slot = rt(NT * 2).bitcast(U32)
        wr = rt(ND * NE).rearrange("p (k e) -> p k e", k=ND)

        rows_dram = nc.dram_tensor("rows_by_slot", [(NU + 1) * UNIT, D], F32).ap()
        y_dram = nc.dram_tensor("results_by_slot", [NU * UNIT, D], F32).ap()

        pad_dram = nc.dram_tensor("padded_bias", [GRID, LAYERS * HC * 15, PADW], F32).ap()

        loaded = [sem("ring_loaded_0"), sem("ring_loaded_1")]
        tab_in, gains_in = sem("tables_loaded"), sem("gains_loaded")
        x_in = [sem(f"x_loaded_{t}") for t in range(NT)]
        ident_in, mix_in = sem("identity_loaded"), sem("first_gain_loaded")
        act_link = sem("act_order")
        rpb_in, pad_set, pad_out = sem("position_bias_loaded"), sem("pad_set"), sem("pad_stored")
        filled = sem("banks_filled")
        emptied = {"A": sem("banks_emptied_by_act"), "D": sem("banks_emptied_by_dve"), "X": sem("exponentials_done")}
        sq_done, rms_ready = sem("square_sums_done"), sem("rms_ready")
        h_ready = sem("normed_rows_ready")
        lat_ready = sem("latents_normed")
        rope_ready = sem("rope_done")
        nmax_ready = sem("row_maxima_ready")
        pv_done = sem("head_steps_accumulated")
        o_out = sem("head_outputs_stored")
        strip_ready, strip_in, strip_half = sem("strips_ready"), sem("strips_loaded"), sem("strip_half_built")
        y_ready = sem("group_rows_ready")
        gains_free = sem("gains_free")
        dve_link = sem("dve_order")
        out_done = sem("output_stored")
        masked, low_made, high_made = sem("bits_masked"), sem("low_parts_made"), sem("high_parts_made")
        fin_ready, sums_ready = sem("final_rows_ready"), sem("final_sums_ready")

        filled_before, router_in = sem("rows_filled_before_scatter"), sem("router_loaded")
        gates_sub, gates_exp, lots_ready = sem("gate_gap_ready"), sem("gate_exp_done"), sem("lots_ready")
        slots_ready, plan_ready, scattered = sem("slots_ready"), sem("plan_ready"), sem("rows_scattered")
        rows_in, up_in, down_in = sem("unit_rows_loaded"), [sem(f"up_loaded_{i}") for i in range(UPS)], \
            [sem(f"down_loaded_{i}") for i in range(DNS)]
        turned, turn_out = sem("unit_turns_filled"), sem("unit_turns_emptied")
        gu_filled, e_silu, gu_free = sem("gate_up_filled"), sem("expert_silu_done"), sem("gate_up_banks_given")
        y_filled, y_out, y_stored = sem("unit_results_filled"), sem("unit_results_emptied"), sem("results_stored")
        w2_used = sem("slices_of_w2_used")
        gathered = [sem(f"results_gathered_{t}") for t in range(NT)]
        final_gain, idle_set = sem("final_gain_loaded"), sem("idle_rows_set")

        entries = []

        def wsrc(ap, c0, n):
            return ap[:, c0:c0 + n].rearrange("(k p) c -> p k c", p=P)

        def entry(key, loads, last):
            entries.append((key, loads, last))

        for l in range(LAYERS):
            w_in, w_uq, w_ukv, w_o = (a[n][l] for n in ("w_in", "w_uq", "w_ukv", "w_o"))
            entry((l, "b"), [(0, 8, DB, wsrc(w_in, COL_B, DB))], (l, "cb", NT - 1, 1))
            entry((l, "v"), [(0, 8, WA, wsrc(w_in, COL_VA, WA)), (8 * WA, 8, WC, wsrc(w_in, COL_VC, WC))],
                  (l, "v", NT - 1, 1))
            entry((l, "uq"), [(0, 3, HB * QKB, wsrc(w_uq, 0, HB * QKB)),
                              (3 * HB * QKB, 2, HB * P, wsrc(w_ukv, 0, HB * P))], (l, "kvn", NT - 1, 1))
            entry((l, "qkA"), [(0, 8, 2 * WA, wsrc(w_in, COL_QA, 2 * WA))], (l, "qk", 2, 1))
            entry((l, "qkC"), [(0, 8, 2 * WC, wsrc(w_in, COL_QC, 2 * WC))], (l, "qk", 7, 1))
            for i in range(2):
                entry((l, "o", i), [(0, 8, 512, wsrc(w_o, 512 * i, 512))], (l, "op", NT - 1, i))
            if l == 0:
                w1, w3, w2 = a["w1"][0], a["w3"][0], a["w2"][0]
                for c in range(CH):
                    entry((l, "f", c), [(0, 8, UNIT, wsrc(w1, UNIT * c, UNIT)),
                                        (8 * UNIT, 8, UNIT, wsrc(w3, UNIT * c, UNIT))], ("split", "w", 4 * c + 3))
                for i in range(2):
                    for c in range(2):
                        entry((l, "w2", i, c),
                              [(0, FT // 2, 512, w2[c * DFF // 2:(c + 1) * DFF // 2, 512 * i:512 * i + 512]
                                .rearrange("(k p) c -> p k c", p=P))],
                              ("split", "v", i * FT + (c + 1) * FT // 2 - 1))
        n_of = {e[0]: n for n, e in enumerate(entries)}
        loads_to = [0, 0]
        full_at = []
        for n, e in enumerate(entries):
            loads_to[n % 2] += 16 * len(e[1])
            full_at.append(loads_to[n % 2])

        def wview(key, i=0):
            n = n_of[key]
            o, k, c, _ = entries[n][1][i]
            s = (n % 2) * RING + o
            return ring[:, s:s + k * c].rearrange("p (k c) -> p k c", k=k)

        def layer_gains(l):
            return [(g_mix, a["g_mix"][l]), (g_ffn, a["g_ffn"][l]),
                    (g_out[:, 0:WA], a["g_out_a"][l]), (g_out[:, WA:WA + WB], a["g_out_b"][l]),
                    (g_out[:, WA + WB:], a["g_out_c"][l]), (g_q, a["g_q"][l]), (g_kv, a["g_kv"][l])]

        NG = 7

        block = ctx.enter_context(nc.Block())

        def parts_free(engine, kind, j):
            if kind == "w" and j >= WS:
                engine.wait_ge(filled, J.filled(0, "gu"[(j - WS) % 2], (j - WS) // 2))
            elif kind == "v" and j < VS:
                engine.wait_ge(filled, J.filled(0, "u", FT - 2 if j < 2 else FT - 1))
            elif kind == "v" and j - VS == FT - 1:
                engine.wait_ge(filled, J.filled(0, "d", 0, NT - 1))
            elif kind == "v":
                engine.wait_ge(w2_used, j - VS + 1 - (j - VS >= FT))

        @block.sync
        def _(sp):
            sp.dma_start(x3[:, 0, :], a["x"][0, 0:P, :]).then_inc(x_in[0], 16)
            sp.dma_start(tab[:, 0:T_COS], a["tables"][:, 0:T_COS]).then_inc(ident_in, 16)
            sp.dma_start(g_mix, a["g_mix"][0].partition_broadcast(P)).then_inc(mix_in, 16)
            sp.dma_start(x3[:, 1, :], a["x"][0, P:2 * P, :]).then_inc(x_in[1], 16)
            for n, (key, loads, last) in enumerate(entries):
                if n >= 2:
                    last_use = entries[n - 2][2]
                    if last_use[0] == "split":
                        sp.wait_ge(low_made, split_of(*last_use[1:]) + 1)
                    else:
                        sp.wait_ge(filled, J.filled(*last_use))
                for (o, k, c, src) in loads:
                    s = (n % 2) * RING + o
                    sp.dma_start(ring[:, s:s + k * c].rearrange("p (k c) -> p k c", k=k), src)\
                        .then_inc(loaded[n % 2], 16)
                if n == 0:
                    for t in range(2, NT):
                        sp.dma_start(x3[:, t, :], a["x"][0, t * P:(t + 1) * P, :]).then_inc(x_in[t], 16)
                    sp.dma_start(tab[:, T_COS:], a["tables"][:, T_COS:]).then_inc(tab_in, 16)
            sp.wait_ge(router_in, 16)
            L = LAYERS - 1
            sp.wait_ge(filled, J.filled(L, "h2", NT - 1, 1))

            def load_up(e, u, f, s):
                sp.wait_ge(gu_filled, u * FE + f + 1)
                for m, n in ((0, "e_w1"), (1, "e_w3")):
                    sp.dma_start(up[s][:, m, :, :],
                                 a[n][0][e][:, bass.ds(f * P, P)].rearrange("(k p) c -> p k c", p=P))\
                        .then_inc(up_in[s], 16)

            def load_down(e, u, d, s):
                sp.wait_ge(y_filled, u * ND + d + 1)
                sp.dma_start(down[s], a["e_w2"][0][e][:, bass.ds(d * P, P)].rearrange("(f p) c -> p f c", p=P))\
                    .then_inc(down_in[s], 16)

            for s in range(UPS):
                load_up(0, 0, s, s)
            sp.wait_ge(rows_in, 16)
            for s in range(DNS):
                load_down(0, 0, s, s)
            sp.wait_ge(plan_ready, 1)
            n_units = sp.value_load(plan[0:1, 2 * NU:2 * NU + 1], min_val=1, max_val=NU)
            with sp.Fori(0, NU) as u:
                with sp.If(u < n_units):
                    e = sp.value_load(plan[0:1, bass.ds(u, 1)], min_val=0, max_val=NE - 1)
                    nxt = sp.value_load(plan[0:1, bass.ds(u + 2 * NU + 1, 1)], min_val=0, max_val=NE - 1)
                    with sp.Fori(1, FE // UPS) as i:
                        for s in range(UPS):
                            load_up(e, u, i * UPS + s, s)
                    for s in range(DNS):
                        load_down(e, u, DNS + s, s)
                        with sp.If(u + 1 < n_units):
                            load_up(nxt, u + 1, s, s)
                    with sp.If(u + 1 < n_units):
                        for s in range(DNS):
                            load_down(nxt, u + 1, s, s)
                    sp.sem_inc(idle_set, 16)
                with sp.Else():
                    sp.dma_start(y_dram[bass.ds(u * UNIT, UNIT), :], a["x"][0][0:UNIT, :]).then_inc(idle_set, 16)
            for t in range(NT):
                sp.wait_ge(fin_ready, t + 1)
                sp.dma_start(a["out"][0][t * P:(t + 1) * P, :], x3[:, t, :]).then_inc(out_done, 16)
            sp.wait_ge(out_done, 16 * NT)

        @block.gpsimd
        def _(pool):
            padt = st[0:LAYERS * HC * 15, 0, 0:PADW]
            nc.gpsimd.memset(padt, NEG).then_inc(pad_set, 1)
            pool.wait_ge(pad_set, 1)
            pool.dma_start(padt[:, 48:48 + 31], a["rpb"].rearrange("l h r c -> (l h r) c")).then_inc(rpb_in, 16)
            pool.wait_ge(x_in[NT - 1], 16)
            for dst, src in layer_gains(0)[1:]:
                pool.dma_start(dst, src.partition_broadcast(P)).then_inc(gains_in, 16)
            pool.wait_ge(rpb_in, 16)
            pool.wait_ge(tab_in, 16)
            pool.dma_start(pad_dram.rearrange("c r w -> r c w"),
                           padt.unsqueeze(1).to_broadcast([LAYERS * HC * 15, GRID, PADW])).then_inc(pad_out, 16)
            pool.wait_ge(pad_out, 16)
            halves = 0
            for l in range(LAYERS):
                for n in range(HA + HC):
                    if l and n == 0:
                        pool.wait_ge(filled, J.filled(0, "d", 1, NT - 1))
                    if l or n >= 2:
                        m = l * (HA + HC) + n - 2
                        ll, mm = divmod(m, HA + HC)
                        last = (mm if mm < HA else mm + HB) * NT + NT - 1
                        pool.wait_ge(emptied["D"], J.emptied(ll, "S", last))
                    buf = st[:, n % 2, :]
                    if n < HA:
                        nc.gpsimd.tensor_scalar(buf, tab[:, T_DIST:T_DIST + STRIP], -SLOPES[n], None, ALU.mult)\
                            .then_inc(strip_half, 1)
                        halves += 1
                        pool.wait_ge(strip_half, halves)
                        nc.gpsimd.tensor_tensor(buf, buf, tab[:, T_AMASK:T_AMASK + STRIP], ALU.add)\
                            .then_inc(strip_ready, 1)
                    else:
                        h = n - HA
                        for r in range(2):
                            row = (l * HC + h) * 15 + 1 - r
                            src = bass.AP(tensor=pad_dram.tensor, offset=row * PADW + 63,
                                          ap=[[LAYERS * HC * 15 * PADW - 1, GRID], [PADW, 14], [1, GRID]])
                            pool.dma_start(buf[r * GRID:(r + 1) * GRID, :]
                                           .rearrange("p (a c) -> p a c", a=14), src).then_inc(strip_in, 16)
                        pool.wait_ge(strip_in, 32 * (l * HC + h + 1))
                        b3 = buf.rearrange("p (a c) -> p a c", a=14)
                        cm = tab[:, T_CMASK:T_CMASK + GRID].unsqueeze(1).to_broadcast([P, 14, GRID])
                        nc.gpsimd.tensor_tensor(b3, b3, cm, ALU.add).then_inc(strip_ready, 1)
                if l == 0:
                    for i in range((NU + 1) * UNIT // SEQ):
                        pool.dma_start(rows_dram[i * SEQ:(i + 1) * SEQ, :], a["x"][0]).then_inc(filled_before, 16)
                    pool.wait_ge(gains_free, 1)
                    for dst, src in layer_gains(1):
                        pool.dma_start(dst, src.partition_broadcast(P)).then_inc(gains_in, 16)

            pool.wait_ge(y_ready, LAYERS * NT)
            pool.dma_start(wr, a["w_router"][0].rearrange("(k p) e -> p k e", p=P)).then_inc(router_in, 16)
            pool.dma_start(g_mix, a["g_final"].partition_broadcast(P)).then_inc(final_gain, 16)
            pool.wait_ge(filled_before, 16 * ((NU + 1) * UNIT // SEQ))
            pool.wait_ge(h_ready, 2 * LAYERS * NT)
            pool.wait_ge(slots_ready, 1)
            for t in range(NT):
                for j in range(2):
                    pool.indirect_dma_start(rows_dram, bass.IndirectOffsetOnAxis(ap=slot[:, 2 * t + j:2 * t + j + 1], axis=0),
                                            h4[:, t, :], None).then_inc(scattered, 16)
            pool.wait_ge(plan_ready, 1)
            n_units = pool.value_load(plan[0:1, 2 * NU:2 * NU + 1], min_val=1, max_val=NU)
            pool.wait_ge(scattered, 16 * 2 * NT)
            pool.dma_start(rows, rows_dram[0:UNIT, :].rearrange("(b p) d -> p b d", p=P)).then_inc(rows_in, 16)
            pool.wait_ge(turned, 4)
            with pool.Fori(0, NU) as u:
                with pool.If(u < n_units):
                    pool.wait_ge(turned, u * 8 + 2)
                    pool.dma_start(rows, rows_dram[bass.ds(u * UNIT + UNIT, UNIT), :]
                                   .rearrange("(b p) d -> p b d", p=P)).then_inc(rows_in, 16)
            pool.wait_ge(y_stored, n_units * 16 + 16)
            pool.sem_inc(idle_set, 16)
            pool.wait_ge(idle_set, NU * 16 + 16)
            for t in range(NT):
                for j in range(2):
                    pool.indirect_dma_start(back[:, 2 * t + j, :], None, y_dram,
                                            bass.IndirectOffsetOnAxis(ap=slot[:, 2 * t + j:2 * t + j + 1], axis=0))\
                        .then_inc(gathered[t], 16)
            for t in range(NT):
                pool.wait_ge(gathered[t], 32)

        @block.tensor
        def _(pe):
            pe.wait_ge(ident_in, 16)

            def take(*name):
                n = J.at[name]
                if n >= ROT:
                    pe.wait_ge(emptied[J.who[n - ROT]], J.nth[n - ROT])
                return ps[:, n % ROT, :]

            def arrived(key):
                n = n_of[key]
                pe.wait_ge(loaded[n % 2], full_at[n])

            def emptied_upto(*name):
                pe.wait_ge(emptied[J.who[J.at[name]]], J.emptied(*name))

            def turn(job, srcs):
                b = take(*job)
                for i, s in enumerate(srcs):
                    w = s.shape[1]
                    last = nc.tensor.transpose(b[0:w, i * P:(i + 1) * P], s, ident)
                last.then_inc(filled, 1)

            def rows_times(job, lhsT, w, kt, t, c0, n):
                b = take(*job)
                for k in range(kt):
                    last = nc.tensor.matmul(b[:, 0:n], lhsT[:, k, t * P:(t + 1) * P], w[:, k, c0:c0 + n],
                                            start=(k == 0), stop=(k == kt - 1))
                last.then_inc(filled, 1)

            def cols_times(job, w, c0):
                b = take(*job)
                for k in range(ND):
                    last = nc.tensor.matmul(b[:, :], w[:, k, c0:c0 + P], hT3[:, k, :],
                                            start=(k == 0), stop=(k == ND - 1))
                last.then_inc(filled, 1)

            def parts_made(n):
                pe.wait_ge(low_made, n + 1)
                pe.wait_ge(high_made, n + 1)

            def norm_turn(l, name, t):
                rows = h4 if name == "h2" else mixed
                pe.wait_ge(h_ready, (2 * l + (name == "h2")) * NT + t + 1)
                for i in range(2):
                    turn((l, name, t, i), [rows[:, t, (4 * i + k) * P:(4 * i + k + 1) * P] for k in range(4)])

            def turned_rows_stored(l, name, t):
                emptied_upto(l, name, t, 0)
                emptied_upto(l, name, t, 1)

            def prep(l, name):
                p, w = name[1], name[2]
                kind, pp = PAIRS[p]
                if kind == "B":
                    h = 2 * pp + name[3]
                    src = kvn4 if w else qn4
                    turn((l,) + name, [src[:, t, h, 0:QKB] for t in range(NT)])
                    return
                key = (l, "qk" + kind)
                arrived(key)
                cols_times((l,) + name, wview(key), (WA if kind == "A" else WC) * w + P * pp)

            def logits(t):
                turned_rows_stored(LAYERS - 1, "h2", t)
                b = take(LAYERS - 1, "lg", t)
                for k in range(ND):
                    last = nc.tensor.matmul(b[0:NE, 0:P], wr[:, k, :], hT3[:, k, t * P:(t + 1) * P],
                                            start=(k == 0), stop=(k == ND - 1))
                last.then_inc(filled, 1)

            for l in range(LAYERS):
                wb = wview((l, "b"))
                for t in range(NT + 1):
                    if t < NT:
                        norm_turn(l, "hT", t)
                    if t:
                        if t == 1:
                            arrived((l, "b"))
                        turned_rows_stored(l, "hT", t - 1)
                        rows_times((l, "cb", t - 1, 0), hT3, wb, ND, t - 1, 0, RQ)
                        rows_times((l, "cb", t - 1, 1), hT3, wb, ND, t - 1, RQ, RKV + ROPE)
                arrived((l, "v"))
                for t in range(NT):
                    rows_times((l, "v", t, 0), hT3, wview((l, "v"), 0), ND, t, 0, WA)
                    rows_times((l, "v", t, 1), hT3, wview((l, "v"), 1), ND, t, 0, WC)
                for t in range(NT):
                    pe.wait_ge(lat_ready, l * NT + t + 1)
                    turn((l, "cT", t, 0), [cn[:, t, k * P:(k + 1) * P] for k in range(3)])
                    turn((l, "cT", t, 1), [cn[:, t, (3 + k) * P:(4 + k) * P] for k in range(2)])
                arrived((l, "uq"))
                emptied_upto(l, "cT", NT - 1, 0)
                emptied_upto(l, "cT", NT - 1, 1)
                for t in range(NT):
                    for i in range(2):
                        rows_times((l, "qn", t, i), cT[:, 0:3, :], wview((l, "uq"), 0), 3, t, 3 * QKB * i, 3 * QKB)
                for t in range(NT):
                    for i in range(2):
                        rows_times((l, "kvn", t, i), cT[:, 3:5, :], wview((l, "uq"), 1), 2, t, 3 * P * i, 3 * P)
                for name, _ in prep_jobs(0):
                    prep(l, name)

                def scores(g):
                    h, t = divmod(g, NT)
                    p, i = divmod(h, 2)
                    kind = PAIRS[p][0]
                    rows = QKB if kind == "B" else HD
                    if t == 0:
                        for name, _ in prep_jobs(p):
                            emptied_upto(l, *name)
                    b = take(l, "S", g)
                    nc.tensor.matmul(b[:, :], qk5[0:rows, p % 2, 0, i, t * P:(t + 1) * P],
                                     qk5[0:rows, p % 2, 1, i, :], start=True, stop=True).then_inc(filled, 1)

                scores(0)
                scores(1)
                def weigh(g):
                    h, t = divmod(g, NT)
                    p, i = divmod(h, 2)
                    kind, pp = PAIRS[p]
                    emptied_upto(l, "PT", g)
                    if t == 0 and l * NH + h >= 2:
                        pe.wait_ge(o_out, l * NH + h - 1)
                    ob = ps[:, ROT + h % 2, :]
                    for k in range(NT):
                        if kind == "B":
                            v = kvn4[:, k, 2 * pp + i, HD:160]
                        else:
                            c = P * pp + (WA if kind == "C" else 0)
                            v = vac3[:, k, c:c + P]
                        last = nc.tensor.matmul(ob[:, t * P:t * P + v.shape[1]], pt[:, g % 2, k * P:(k + 1) * P], v,
                                                start=(k == 0), stop=(k == NT - 1))
                    last.then_inc(pv_done, 1)

                for g in range(STEPS):
                    p = g // 8
                    if g + 2 < STEPS:
                        scores(g + 2)
                    pe.wait_ge(emptied["X"], l * STEPS + g + 1)
                    turn((l, "PT", g), [pr[:, g % 3, k * P:(k + 1) * P] for k in range(NT)])
                    if g:
                        weigh(g - 1)
                    if p + 1 < len(PAIRS):
                        for name, _ in prep_at(p + 1, g % 8):
                            if PAIRS[p + 1][0] == "B":
                                pe.wait_ge(rope_ready, l + 1)
                            prep(l, name)
                weigh(STEPS - 1)
                arrived((l, "o", 0))
                for t in range(NT + 1):
                    if t < NT:
                        pe.wait_ge(y_ready, l * NT + t + 1)
                        for i in range(2):
                            turn((l, "yT", t, i), [on[:, t, (4 * i + k) * P:(4 * i + k + 1) * P] for k in range(4)])
                    if t:
                        emptied_upto(l, "yT", t - 1, 0)
                        emptied_upto(l, "yT", t - 1, 1)
                        rows_times((l, "op", t - 1, 0), hT3, wview((l, "o", 0)), ND, t - 1, 0, 512)
                arrived((l, "o", 1))
                if l == LAYERS - 1:
                    pe.wait_ge(router_in, 16)
                for t in range(NT + 2):
                    if t < NT:
                        rows_times((l, "op", t, 1), hT3, wview((l, "o", 1)), ND, t, 0, 512)
                    if 1 <= t <= NT:
                        norm_turn(l, "h2", t - 1)
                    if t >= 2 and l == LAYERS - 1:
                        logits(t - 2)
                if l == 0:
                    for j in range(2 * FT):
                        b = take(l, "gu"[j % 2], j // 2)
                        parts_made(max(split_of("w", j), split_of("x", NT - 1)))
                        for k in range(ND):
                            for w, xx in ((1, xh3), (0, xl3), (0, xh3)):
                                last = nc.tensor.matmul(b, w5[:, j % WS, w, k, :], xx[:, k, :],
                                                        start=(k == 0 and w == 1), stop=(k == ND - 1 and xx is xh3 and w == 0))
                        last.then_inc(filled, 1)
                    for i in range(2):
                        banks = []

                        def product(f, t):
                            v = v_parts[(i * FT + f) % VS]
                            parts = ((hl3[f], 0), (hh3[:, f, :], 1), (hh3[:, f, :], 0))
                            for n, (h, j) in enumerate(parts):
                                last = nc.tensor.matmul(banks[t], h[:, t * P:(t + 1) * P], v[:, j, :],
                                                        start=(f == 0 and n == 0), stop=(f == FT - 1 and n == 2))
                            return last

                        behind = VS if i else 0
                        for f in range(FT - behind):
                            parts_made(max(split_of("v", i * FT + f), split_of("h", f)))
                            for t in range(NT):
                                if f == 0:
                                    banks.append(take(l, "d", i, t))
                                last = product(f, t)
                                if f == FT - 1:
                                    last.then_inc(filled, 1)
                                elif t == NT - 1:
                                    last.then_inc(w2_used, 1)
                        if behind:
                            parts_made(len(SPLITS) - 1)
                            for t in range(NT):
                                for f in range(FT - behind, FT):
                                    last = product(f, t)
                                last.then_inc(filled, 1)

            pe.sem_inc(gu_filled, UPS)
            pe.sem_inc(y_filled, DNS)
            l = LAYERS - 1
            b = take(l, "lt")
            emptied_upto(l, "lg", NT - 1)
            for t in range(NT):
                last = nc.tensor.transpose(b[:, t * NE:(t + 1) * NE], logitT[:, t * P:(t + 1) * P], ident[0:NE, 0:NE])
            last.then_inc(filled, 1)
            pe.wait_ge(lots_ready, 1)
            b = take(l, "rk")
            every = both.rearrange("p t e -> p (t e)")
            nc.tensor.matmul(b[:, 0:NT * NE], tri, every, start=True, stop=True)
            nc.tensor.matmul(b[:, P:P + NT * NE], ones, every, start=True, stop=True).then_inc(filled, 1)

            pe.wait_ge(plan_ready, 1)
            pe.wait_ge(emptied["D"], J.emptied(l, "rk"))
            n_units = pe.value_load(plan[0:1, 2 * NU:2 * NU + 1], min_val=1, max_val=NU)

            def rows_turned(i, job):
                for k in range(2):
                    for r in range(2):
                        last = nc.tensor.transpose(ps[:, 6 + job % 2, (2 * k + r) * P:(2 * k + r + 1) * P],
                                                   rows[:, r, (2 * i + k) * P:(2 * i + k + 1) * P], ident)
                last.then_inc(turned, 1)

            def turn_one(u, what):
                kind, i = what
                job = TURN_ORDER.index(what)
                if kind == "row":
                    pe.wait_ge(rows_in, u * 16 + 32)
                else:
                    pe.wait_ge(y_out, u * ND + 2 * i + 4)
                pe.wait_ge(turn_out, u * 8 + job + 5)
                if kind == "row":
                    return rows_turned(i, job)
                for r in range(2):
                    for k in range(2):
                        last = nc.tensor.transpose(ps[:, 6 + job % 2, (2 * r + k) * P:(2 * r + k + 1) * P],
                                                   yT[:, 2 * i + k, r * P:(r + 1) * P], ident)
                last.then_inc(turned, 1)

            def unit_body(u, n):
                with pe.Fori(0, FE // UPS) as i:
                    for s in range(UPS):
                        f = u * FE + i * UPS + s
                        if s == 0:
                            pe.wait_ge(turn_out, u * 8 + 4)
                        pe.wait_ge(up_in[s], (u * (FE // UPS) + i + 1) * 32)
                        pe.wait_ge(gu_free, f + 1)
                        gb = ps[:, s, :]
                        for m in range(2):
                            for k in range(ND):
                                last = nc.tensor.matmul(gb[:, m * UNIT:m * UNIT + n], up[s][:, m, k, :], XT[:, k, 0:n],
                                                        start=(k == 0), stop=(k == ND - 1))
                        last.then_inc(gu_filled, 1)
                for d in range(ND):
                    pe.wait_ge(down_in[d % DNS], (u * (ND // DNS) + d // DNS + 1) * 16)
                    pe.wait_ge(y_out, u * ND + d + 1)
                    for f in range(FE):
                        if d == 0 and f in (0, FE - UPS):
                            pe.wait_ge(gu_free, u * FE + (f or FE - UPS) + (UPS if f else 0) + 4)
                        last = nc.tensor.matmul(ps[:, 4 + d % 2, 0:n], down[d % DNS][:, f, :], eh[:, f, 0:n],
                                                start=(f == 0), stop=(f == FE - 1))
                    last.then_inc(y_filled, 1)
                    if TURNS[d]:
                        turn_one(u, TURNS[d])
                turn_one(u, TURNS[ND])

            def choose(u, held, classes):
                if len(classes) == 1:
                    return unit_body(u, classes[0])
                half = (len(classes) + 1) // 2
                with pe.If(held < classes[half - 1] + 1):
                    choose(u, held, classes[:half])
                with pe.Else():
                    choose(u, held, classes[half:])

            pe.wait_ge(rows_in, 16)
            for i in range(4):
                pe.wait_ge(turn_out, i + 1)
                rows_turned(i, i)
            pe.wait_ge(turn_out, 6)
            with pe.Fori(0, NU) as u:
                with pe.If(u < n_units):
                    held = pe.value_load(plan[0:1, bass.ds(u + NU, 1)], min_val=0, max_val=UNIT)
                    choose(u, held, CLASSES)

        @block.scalar
        def _(act):
            def bank(*name):
                act.wait_ge(filled, J.filled(*name))
                return ps[:, J.bank(*name), :]

            def copy_out(dst, job, n=512):
                nc.scalar.copy(dst, bank(*job)[:, 0:n]).then_inc(emptied["A"], 1)

            roots = [0, 0]

            def root(n):
                roots[0] += 1
                act.wait_ge(sq_done, roots[0])
                nc.scalar.activation(rms[:, 0:n], ssq[:, 0:n], ACT.Sqrt).then_inc(rms_ready, 1)

            links = [0]

            def square(src, col, scratch=hr[:, 1, :]):
                n = src.shape[1]
                if links[0]:
                    act.wait_ge(act_link, links[0])
                links[0] += 1
                nc.scalar.activation(scratch[:, 0:n], src, ACT.Square, scale=n ** -0.5,
                                     accum_out=ssq[:, col:col + 1]).then_inc(act_link, 1)

            def own_root(c0, c1):
                roots[1] += 1
                act.wait_ge(act_link, links[0])
                nc.scalar.activation(rms[:, c0:c1], ssq[:, c0:c1], ACT.Sqrt, bias=eps).then_inc(rms_ready, 1)

            def x_root(t, *scratch):
                square(x3[:, t, :], t, *scratch)
                own_root(t, t + 1)

            def group(l, i):
                c0, c1 = GROUPS[i]
                act.wait_ge(o_out, l * NH + c1 // HD)
                for t in range(NT):
                    square(on[:, t, c0:c1], 3 * t + i)

            act.wait_ge(ident_in, 16)

            def split(job):
                l, name, t, i = job
                return hT3[:, 4 * i:4 * i + 4, t * P:(t + 1) * P]

            def prep(l, name):
                p, w = name[1], name[2]
                kind, pp = PAIRS[p]
                if kind == "B":
                    b = bank(l, *name)
                    nc.scalar.copy(qk5[0:QKB, p % 2, 0, name[3], :], b[0:QKB, :]).then_inc(emptied["A"], 1)
                    return
                b = bank(l, *name)
                for i in range(2):
                    last = nc.scalar.mul(qk5[0:HD, p % 2, 0, i, :], b[i * HD:(i + 1) * HD, :], QSCALE[kind])
                last.then_inc(emptied["A"], 1)

            def prep_mine(js, l):
                for name, who in js:
                    if who == "A":
                        prep(l, name)

            def first_norm_turned(l, t):
                if t < NT:
                    copy_out(split((l, "hT", t, 0)), (l, "hT", t, 0))
                if t:
                    copy_out(cn[:, t - 1, 0:RQ], (l, "cb", t - 1, 0), RQ)

            def second_norm_turned(l, t):
                copy_out(split((l, "h2", t, 0)), (l, "h2", t, 0))
                if l == 0:
                    high_part("x", t)

            def high_part(kind, j):
                if (kind, j) not in SPLITS:
                    return
                n = split_of(kind, j)
                act.wait_ge(masked, n + 1)
                if kind in "xh":
                    act.wait_ge(low_made, n + 1)
                else:
                    parts_free(act, kind, j)
                dst = {"x": lambda: xh3[:, :, j * P:(j + 1) * P], "w": lambda: w5[:, j % WS, 0, :, :],
                       "h": lambda: hh3[:, j, :], "v": lambda: v_parts[j % VS][:, 0, :]}[kind]()
                src = high[:, n % 2] if kind in "xw" else high[:, n % 2].rearrange("p k c -> p (k c)")[:, 0:SEQ]
                nc.scalar.copy(dst, src).then_inc(high_made, 1)

            def expo(l, g):
                h, t = divmod(g, NT)
                act.wait_ge(nmax_ready, l * STEPS + g + 1)
                if l * STEPS + g >= 3:
                    ll, gg = divmod(l * STEPS + g - 3, STEPS)
                    act.wait_ge(filled, J.filled(ll, "PT", gg))
                if t == 0 and l * NH + h >= 2:
                    act.wait_ge(o_out, l * NH + h - 1)
                src = ps[:, J.bank(l, "S", g), :] if PAIRS[h // 2][0] == "B" else sc[:, g % 2, :]
                nc.scalar.activation(pr[:, g % 3, :], src, ACT.Exp, bias=nmx[:, g % 4:g % 4 + 1],
                                     accum_out=ls[:, h % 2, t:t + 1]).then_inc(emptied["X"], 1)

            for l in range(LAYERS):
                for t in range(NT):
                    if l:
                        act.wait_ge(emptied["D"], J.emptied(l - 1, "d", 1, t))
                    else:
                        act.wait_ge(x_in[t], 16)
                    x_root(t)
                    if l == 0 and t:
                        first_norm_turned(l, t - 1)
                for t in range(NT - 1 if l == 0 else 0, NT + 1):
                    first_norm_turned(l, t)
                root(2 * NT)
                for t in range(NT):
                    copy_out(vac3[:, t, 0:WA], (l, "v", t, 0), WA)
                for t in range(NT):
                    copy_out(cT[:, 0:3, t * P:(t + 1) * P], (l, "cT", t, 0), 3 * P)
                for t in range(NT):
                    for i in range(2):
                        b = bank(l, "qn", t, i)
                        nc.scalar.mul(qn4[:, t, 3 * i:3 * i + 3, :], b[:, 0:3 * QKB], QSCALE["B"])\
                            .then_inc(emptied["A"], 1)
                prep_mine(prep_jobs(0), l)
                expo(l, 0)
                expo(l, 1)
                for g in range(STEPS):
                    if g % 2 == 0:
                        b = bank(l, "PT", g)
                        if l * STEPS + g >= 2:
                            act.wait_ge(pv_done, l * STEPS + g - 1)
                        nc.scalar.copy(pt[:, 0, :], b).then_inc(emptied["A"], 1)
                    if g + 2 < STEPS:
                        expo(l, g + 2)
                    if g // 8 + 1 < len(PAIRS):
                        prep_mine(prep_at(g // 8 + 1, g % 8), l)
                    if g in (HA * NT + 4, (HA + HB) * NT + 4):
                        group(l, 0 if g < (HA + HB) * NT else 1)
                group(l, 2)
                own_root(0, 3 * NT)
                for t in range(NT):
                    copy_out(split((l, "yT", t, 0)), (l, "yT", t, 0))
                for t in range(NT):
                    act.wait_ge(emptied["D"], J.emptied(l, "op", t, 1))
                    x_root(t, A0[:, NT * D:NT * D + D])
                    if l == 0 and t < WS:
                        high_part("w", t)
                    if t:
                        second_norm_turned(l, t - 1)
                second_norm_turned(l, NT - 1)
                if l == 0:
                    for f in range(FT):
                        high_part("w", 2 * f + WS)
                        if f == FT - 1:
                            for kj in ("h", 0), ("v", 0), ("v", 1):
                                high_part(*kj)
                        b = bank(l, "g", f)
                        if f >= 2:
                            act.wait_ge(emptied["D"], J.emptied(l, "u", f - 2))
                        nc.scalar.activation(sil[:, f % 2, :], b, ACT.Silu).then_inc(emptied["A"], 1)
                        high_part("w", 2 * f + WS + 1)
                    for kj in SPLITS[split_of("h", 1):]:
                        high_part(*kj)
            act.wait_ge(gates_sub, 1)
            nc.scalar.activation(eg, gap, ACT.Exp).then_inc(gates_exp, 1)
            act.wait_ge(plan_ready, 1)
            act.sem_inc(turn_out, 2)
            act.sem_inc(y_stored, 16)
            n_units = act.value_load(plan[0:1, 2 * NU:2 * NU + 1], min_val=1, max_val=NU)
            for i in range(4):
                act.wait_ge(turned, i + 1)
                nc.scalar.copy(XT[:, 2 * i:2 * i + 2, :], ps[:, 6 + i % 2, :]).then_inc(turn_out, 1)
            with act.Fori(0, NU) as u:
                with act.If(u < n_units):
                    with act.Fori(0, FE // UPS) as i:
                        for s in range(UPS):
                            act.wait_ge(gu_filled, u * FE + i * UPS + (s + 1 + UPS))
                            act.wait_ge(gu_free, u * FE + i * UPS + s + 3)
                            nc.scalar.activation(esil[:, s % 2, :], ps[:, s, 0:UNIT], ACT.Silu).then_inc(e_silu, 1)
                    for job, (kind, i) in enumerate(TURN_ORDER):
                        act.wait_ge(turned, u * 8 + job + 5)
                        b = ps[:, 6 + job % 2, :]
                        if kind == "row":
                            nc.scalar.copy(XT[:, 2 * i:2 * i + 2, :], b).then_inc(turn_out, 1)
                            continue
                        if i == 0:
                            act.wait_ge(y_stored, u * 16 + 16)
                        nc.scalar.copy(yrow[:, :, 2 * P * i:2 * P * (i + 1)], b.rearrange("p (r c) -> p r c", r=2))\
                            .then_inc(turn_out, 1)
                    act.wait_ge(turn_out, u * 8 + 14)
                    act.dma_start(y_dram[bass.ds(u * UNIT, UNIT), :].rearrange("(b p) d -> p b d", p=P), yrow)\
                        .then_inc(y_stored, 16)
            for t in range(NT):
                act.wait_ge(sums_ready, t + 1)
                x_root(t)

        @block.vector
        def _(dve):
            links = [0]

            def link(ins):
                links[0] += 1
                ins.then_inc(dve_link, 1)
                dve.wait_ge(dve_link, links[0])

            def bank(*name):
                dve.wait_ge(filled, J.filled(*name))
                return ps[:, J.bank(*name), :]

            def copy_out(dst, job, n=512):
                nc.vector.tensor_copy(dst, bank(*job)[:, 0:n]).then_inc(emptied["D"], 1)

            def square(src, scratch, col, width):
                link(nc.vector.tensor_tensor_reduce(scratch, src, src, 1.0 / width, 0.0, ALU.mult, ALU.add,
                                                    ssq[:, col:col + 1]))

            roots = [0]

            def roots_in(c0, c1):
                roots[0] += 1
                dve.wait_ge(rms_ready, roots[0])
                link(nc.vector.reciprocal(rr[:, c0:c1], rms[:, c0:c1]))

            def inverse(n):
                nc.vector.tensor_scalar(ssq[:, 0:n], ssq[:, 0:n], EPS, None, ALU.add).then_inc(sq_done, 1)
                roots_in(0, n)

            def norm_rows(l, name, gain, ready, between):
                out = h4 if name == "h2" else mixed
                def normed(t):
                    roots_in(t, t + 1)
                    nc.vector.scalar_tensor_tensor(out=out[:, t, :], in0=x3[:, t, :], scalar=rr[:, t:t + 1],
                                                   in1=gain, op0=ALU.mult, op1=ALU.mult).then_inc(h_ready, 1)

                if name == "h2":
                    for t in range(NT + 2):
                        if t < NT:
                            ready(t)
                            normed(t)
                        between(t)
                elif l == 0:
                    for t in range(NT + 2):
                        if t < NT:
                            ready(t)
                            normed(t)
                        if 1 <= t <= NT:
                            copy_out(hT3[:, 4:8, (t - 1) * P:t * P], (l, name, t - 1, 1))
                        if t >= 2:
                            between(t - 2)
                else:
                    for t in range(NT + 1):
                        if t < NT:
                            ready(t)
                        if t == NT:
                            copy_out(hT3[:, 4:8, 0:P], (l, name, 0, 1))
                        if t:
                            normed(t - 1)
                    for t in range(1, NT + 1):
                        if t < NT:
                            copy_out(hT3[:, 4:8, t * P:(t + 1) * P], (l, name, t, 1))
                        between(t - 1)

            def prep_mine(js, l):
                for name, who in js:
                    if who != "D":
                        continue
                    p = name[1]
                    b = bank(l, *name)
                    if PAIRS[p][0] == "B":
                        nc.vector.tensor_copy(qk5[0:QKB, p % 2, 1, name[3], :], b[0:QKB, :])\
                            .then_inc(emptied["D"], 1)
                    else:
                        for i in range(2):
                            last = nc.vector.tensor_copy(qk5[0:HD, p % 2, 1, i, :], b[i * HD:(i + 1) * HD, :])
                        last.then_inc(emptied["D"], 1)

            def row_max(l, g):
                h, t = divmod(g, NT)
                kind = PAIRS[h // 2][0]
                b = bank(l, "S", g)
                if l * STEPS + g >= 4:
                    dve.wait_ge(emptied["X"], l * STEPS + g - 3)
                m = mx[:, g % 4:g % 4 + 1]
                if kind == "B":
                    link(nc.vector.tensor_reduce(m, b, AX.X, ALU.max))
                else:
                    n = h if kind == "A" else h - HB
                    if t == 0:
                        dve.wait_ge(strip_ready, l * (HA + HC) + n + 1)
                    if l * STEPS + g >= 2:
                        dve.wait_ge(emptied["X"], l * STEPS + g - 1)
                    s = SEQ - P - P * t
                    nc.vector.tensor_tensor_reduce(sc[:, g % 2, :], b, st[:, n % 2, s:s + SEQ], 1.0, NEG * 4,
                                                   ALU.add, ALU.max, m).then_inc(emptied["D"], 1)
                    dve.wait_ge(emptied["D"], J.emptied(l, "S", g))
                nc.vector.tensor_scalar(nmx[:, g % 4:g % 4 + 1], m, -1.0, None, ALU.mult).then_inc(nmax_ready, 1)

            def head_out(l, h):
                p, i = divmod(h, 2)
                kind, pp = PAIRS[p]
                dve.wait_ge(emptied["X"], l * STEPS + NT * h + NT)
                link(nc.vector.reciprocal(rl[:, h % 2, :], ls[:, h % 2, :]))
                dve.wait_ge(pv_done, l * STEPS + NT * h + NT)
                c = ROPE if kind == "B" else HD * i
                o = ps[:, ROT + h % 2, :].rearrange("p (t c) -> p t c", t=NT)[:, :, c:c + HD]
                r = rl[:, h % 2, :].unsqueeze(2).to_broadcast([P, NT, HD])
                nc.vector.tensor_tensor(on[:, :, h * HD:(h + 1) * HD], o, r, ALU.mult).then_inc(o_out, 1)

            def rotate(x1, x2, cos, sin, n):
                w = [sc_flat[:, i * 384:i * 384 + n * 16].rearrange("p (n c) -> p n c", c=16) for i in range(2)]
                w += [st_flat[:, i * 384:i * 384 + n * 16].rearrange("p (n c) -> p n c", c=16) for i in range(2)]
                for dst, s, f in ((w[0], x1, cos), (w[1], x2, sin), (w[2], x1, sin), (w[3], x2, cos)):
                    last = nc.vector.tensor_tensor(dst, s, f, ALU.mult)
                link(last)
                nc.vector.tensor_tensor(x1, w[0], w[1], ALU.subtract)
                return nc.vector.tensor_tensor(x2, w[2], w[3], ALU.add)

            sc_flat = soft[:, 5 * SEQ:7 * SEQ]
            st_flat = soft[:, 3 * SEQ:5 * SEQ]
            def add_to_x(l, job, t, i):
                xs = x3[:, t, 512 * i:512 * i + 512]
                nc.vector.tensor_tensor(xs, bank(l, *job), xs, ALU.add).then_inc(emptied["D"], 1)

            def low_part(kind, j):
                if (kind, j) not in SPLITS:
                    return
                n = split_of(kind, j)
                f = j // 2
                if kind == "x":
                    dve.wait_ge(emptied["A"], J.emptied(0, "h2", j, 0))
                    dve.wait_ge(emptied["D"], J.emptied(0, "h2", j, 1))
                    src, dst = hT3[:, :, j * P:(j + 1) * P], xl3[:, :, j * P:(j + 1) * P]
                elif kind == "h":
                    dve.wait_ge(emptied["D"], J.emptied(0, "u", j))
                    src, dst = hid[:, j, :], hl3[j]
                else:
                    if kind == "w":
                        e, v = n_of[(0, "f", f // 2)], wview((0, "f", f // 2), j % 2)
                        src, dst = v[:, :, (f % 2) * P:(f % 2) * P + P], w5[:, j % WS, 1, :, :]
                    else:
                        i, k = divmod(j, FT)
                        c, k = divmod(k, FT // 2)
                        e, src, dst = n_of[(0, "w2", i, c)], wview((0, "w2", i, c))[:, k, :], v_parts[j % VS][:, 1, :]
                    dve.wait_ge(loaded[e % 2], full_at[e])
                top_part = high[:, n % 2] if kind in "xw" else high[:, n % 2].rearrange("p k c -> p (k c)")[:, 0:SEQ]
                if n >= 2:
                    dve.wait_ge(high_made, n - 1)
                    dve.wait_ge(low_made, n - 1)
                nc.vector.tensor_scalar(top_part.bitcast(I32), src.bitcast(I32), HIGH, None, ALU.bitwise_and)\
                    .then_inc(masked, 1)
                dve.wait_ge(masked, n + 1)
                if kind == "h" and j:
                    dve.wait_ge(filled, J.filled(0, "u", FT - 1))
                else:
                    parts_free(dve, kind, j)
                nc.vector.tensor_tensor(dst, src, top_part, ALU.subtract).then_inc(low_made, 1)

            def attention_added(t):
                add_to_x(l, ("op", t, 1), t, 1)
                if l == 0 and t < WS:
                    low_part("w", t)

            def second_norm_between(t):
                if 1 <= t <= NT:
                    copy_out(hT3[:, 4:8, (t - 1) * P:t * P], (l, "h2", t - 1, 1))
                    if l == 0:
                        low_part("x", t - 1)
                if t >= 2 and l == LAYERS - 1:
                    logits_out(t - 2)

            def logits_out(t):
                V.tensor_copy(logitT[:, t * P:(t + 1) * P], bank(LAYERS - 1, "lg", t)[0:NE, 0:P])\
                    .then_inc(emptied["D"], 1)

            tt, V = nc.vector.tensor_tensor, nc.vector
            for l in range(LAYERS):
                def latent(t):
                    copy_out(cn[:, t, RQ:DB], (l, "cb", t, 1), RKV + ROPE)

                if l:
                    dve.wait_ge(gains_in, 16 * (2 * NG - 1))
                    norm_rows(l, "hT", g_mix, lambda t: add_to_x(l - 1, ("d", 1, t), t, 1), latent)
                else:
                    dve.wait_ge(mix_in, 16)
                    norm_rows(l, "hT", g_mix, lambda t: dve.wait_ge(x_in[t], 16), latent)
                    dve.wait_ge(gains_in, 16 * (NG - 1))
                    dve.wait_ge(tab_in, 16)
                dve.wait_ge(emptied["A"], J.emptied(l, "cb", NT - 1, 0))
                dve.wait_ge(emptied["D"], J.emptied(l, "cb", NT - 1, 1))
                for t in range(NT):
                    square(cn[:, t, 0:RQ], hr[:, 0, 0:RQ], t, RQ)
                    square(cn[:, t, RQ:RQ + RKV], hr[:, 0, 0:RKV], NT + t, RKV)
                inverse(2 * NT)
                for t in range(NT):
                    nc.vector.scalar_tensor_tensor(out=cn[:, t, 0:RQ], in0=cn[:, t, 0:RQ], scalar=rr[:, t:t + 1],
                                                   in1=g_q, op0=ALU.mult, op1=ALU.mult)
                    kv = cn[:, t, RQ:RQ + RKV]
                    nc.vector.scalar_tensor_tensor(out=kv, in0=kv, scalar=rr[:, NT + t:NT + t + 1],
                                                   in1=g_kv, op0=ALU.mult, op1=ALU.mult).then_inc(lat_ready, 1)
                for t in range(NT):
                    copy_out(vac3[:, t, WA:WA + WC], (l, "v", t, 1), WC)
                kr = cn[:, :, RQ + RKV:DB]
                cosk = tab[:, T_COS:T_SIN].rearrange("p (t h c) -> p t h c", t=NT, h=HB)[:, :, 0, :]
                sink = tab[:, T_SIN:T_DIST].rearrange("p (t h c) -> p t h c", t=NT, h=HB)[:, :, 0, :]
                link(rotate(kr[:, :, 0:16], kr[:, :, 16:32], cosk, sink, NT))
                for t in range(NT):
                    copy_out(cT[:, 3:5, t * P:(t + 1) * P], (l, "cT", t, 1), 2 * P)
                for t in range(NT):
                    for i in range(2):
                        b = bank(l, "kvn", t, i)[:, 0:3 * P].rearrange("p (h w c) -> p h w c", h=3, w=2)
                        kv = kvn4[:, t, 3 * i:3 * i + 3, :]
                        nc.vector.tensor_copy(kv[:, :, 0:HD], b[:, :, 0, :])
                        nc.vector.tensor_copy(kv[:, :, QKB:160], b[:, :, 1, :]).then_inc(emptied["D"], 1)
                prep_mine(prep_jobs(0), l)
                for t in range(NT):
                    nc.vector.tensor_copy(kvn4[:, t, :, HD:QKB], kr[:, t, :].unsqueeze(1).to_broadcast([P, HB, ROPE]))
                dve.wait_ge(emptied["A"], J.emptied(l, "qn", NT - 1, 1))
                q3 = qn.rearrange("p (n c) -> p n c", c=QKB)
                cosq = tab[:, T_COS:T_SIN].rearrange("p (n c) -> p n c", c=16)
                sinq = tab[:, T_SIN:T_DIST].rearrange("p (n c) -> p n c", c=16)
                rotate(q3[:, :, HD:HD + 16], q3[:, :, HD + 16:QKB], cosq, sinq, NT * HB).then_inc(rope_ready, 1)
                dve.wait_ge(rope_ready, l + 1)
                row_max(l, 0)
                row_max(l, 1)
                for g in range(STEPS):
                    if g + 2 < STEPS:
                        row_max(l, g + 2)
                    if g % 2 == 1:
                        b = bank(l, "PT", g)
                        if l * STEPS + g >= 2:
                            dve.wait_ge(pv_done, l * STEPS + g - 1)
                        nc.vector.tensor_copy(pt[:, 1, :], b).then_inc(emptied["D"], 1)
                    if g % NT == 1 and g > 1:
                        head_out(l, g // NT - 1)
                    if g // 8 + 1 < len(PAIRS):
                        prep_mine(prep_at(g // 8 + 1, g % 8), l)
                head_out(l, NH - 1)
                dve.wait_ge(o_out, (l + 1) * NH)
                roots_in(0, 3 * NT)
                for t in range(NT + 2):
                    if t < NT:
                        for i, (c0, c1) in enumerate(GROUPS):
                            last = nc.vector.scalar_tensor_tensor(out=on[:, t, c0:c1], in0=on[:, t, c0:c1],
                                                                  scalar=rr[:, 3 * t + i:3 * t + i + 1],
                                                                  in1=g_out[:, c0:c1], op0=ALU.mult, op1=ALU.mult)
                        last.then_inc(y_ready, 1)
                    if 1 <= t <= NT:
                        copy_out(hT3[:, 4:8, (t - 1) * P:t * P], (l, "yT", t - 1, 1))
                    if t >= 2:
                        add_to_x(l, ("op", t - 2, 0), t - 2, 0)
                norm_rows(l, "h2", g_ffn, attention_added, second_norm_between)
                if l == 0:
                    nc.vector.memset(small[:, 255:256], 0.0).then_inc(gains_free, 1)
                    for f in range(FT):
                        low_part("w", 2 * f + WS)
                        if f == FT - 1:
                            for kj in ("h", 0), ("v", 0), ("v", 1):
                                low_part(*kj)
                        b = bank(l, "u", f)
                        dve.wait_ge(emptied["A"], J.emptied(l, "g", f))
                        nc.vector.tensor_tensor(hid[:, f, :], b, sil[:, f % 2, :], ALU.mult)\
                            .then_inc(emptied["D"], 1)
                        low_part("w", 2 * f + WS + 1)
                    for kj in SPLITS[split_of("h", 1):]:
                        if kj == ("v", FT + 2):
                            for t in range(NT):
                                add_to_x(l, ("d", 0, t), t, 0)
                        low_part(*kj)

            l = LAYERS - 1
            V.tensor_copy(logit, bank(l, "lt")[:, 0:NT * NE].rearrange("p (t e) -> p t e", t=NT))\
                .then_inc(emptied["D"], 1)
            dve.wait_ge(emptied["D"], J.emptied(l, "lt"))
            for t in range(NT):
                last = V.max(top[:, t, :], logit[:, t, :])
            link(last)
            for t in range(NT):
                last = V.max_index(pick[:, t, :], top[:, t, :], logit[:, t, :])
            link(last)
            tt(gap, top[:, :, 1], top[:, :, 0], ALU.subtract).then_inc(gates_sub, 1)
            link(V.tensor_copy(pickf, pick[:, :, 0:2]))
            eno = tab[:, T_E:T_E + NE].unsqueeze(1).to_broadcast([P, NT, NE])
            for j, lot in enumerate((lot0, lot1)):
                last = tt(lot, eno, pickf[:, :, j:j + 1].to_broadcast([P, NT, NE]), ALU.is_equal)
            link(last)
            tt(both, lot0, lot1, ALU.add).then_inc(lots_ready, 1)
            dve.wait_ge(gates_exp, 1)
            link(V.tensor_scalar(den, eg, 1.0, None, ALU.add))
            link(V.reciprocal(g0, den))
            link(tt(g1, eg, g0, ALU.mult))
            b = bank(l, "rk")
            V.tensor_copy(rank, b[:, 0:NT * NE].rearrange("p (t e) -> p t e", t=NT))
            V.tensor_copy(tile_cnt, b[:, P:P + NT * NE].rearrange("p (t e) -> p t e", t=NT)).then_inc(emptied["D"], 1)
            dve.wait_ge(emptied["D"], J.emptied(l, "rk"))
            for t in range(1, NT):
                link(tt(tile_cnt[:, t, :], tile_cnt[:, t, :], tile_cnt[:, t - 1, :], ALU.add))
            tt(rank[:, 1:, :], rank[:, 1:, :], tile_cnt[:, 0:NT - 1, :], ALU.add)
            link(V.tensor_copy(cnt, tile_cnt[:, NT - 1, :]))
            V.tensor_scalar(more, cnt, float(UNIT), None, ALU.is_gt)
            link(V.tensor_scalar(units, cnt, 0.0, None, ALU.is_gt))
            link(tt(units, units, more, ALU.add))
            link(V.tensor_scalar(units[:, 0:1], units[:, 0:1], 1.0, None, ALU.max))
            link(V.tensor_tensor_scan(incl, tab[:, T_ONES:T_ONES + NE], units, 0.0, ALU.mult, ALU.add))
            link(tt(excl, incl, units, ALU.subtract))
            link(V.tensor_scalar(first, excl, float(UNIT), None, ALU.mult))
            link(tt(rank, rank, first.unsqueeze(1).to_broadcast([P, NT, NE]), ALU.add))
            for j, lot in enumerate((lot0, lot1)):
                link(tt(hit, lot, rank, ALU.mult))
                link(V.tensor_reduce(slotf[:, :, j], hit, AX.X, ALU.add))
            V.tensor_copy(slot, slotf.rearrange("p t j -> p (t j)")).then_inc(slots_ready, 1)
            unit = tab[:, T_UNIT:T_UNIT + NU * NE].rearrange("p (u e) -> p u e", u=NU)

            def over(v):
                return v.unsqueeze(1).to_broadcast([P, NU, NE])

            tt(past, unit, over(incl), ALU.is_ge)
            link(tt(owns, unit, over(excl), ALU.is_ge))
            link(tt(owns, owns, past, ALU.subtract))
            link(V.tensor_reduce(planf[:, 0:NU], past, AX.X, ALU.add))
            link(tt(tot, cnt, first, ALU.add))
            link(V.scalar_tensor_tensor(out=left, in0=unit, scalar=-float(UNIT), in1=over(tot),
                                        op0=ALU.mult, op1=ALU.add))
            link(tt(left, left, owns, ALU.mult))
            link(V.tensor_reduce(planf[:, NU:2 * NU], left, AX.X, ALU.add))
            link(V.tensor_scalar(planf[:, 0:NU], planf[:, 0:NU], float(NE - 1), None, ALU.min))
            link(V.tensor_scalar(planf[:, NU:2 * NU], planf[:, NU:2 * NU], float(UNIT), None, ALU.min))
            V.tensor_copy(planf[:, 2 * NU + 1:3 * NU], planf[:, 1:NU])
            V.memset(planf[:, 3 * NU:3 * NU + 2], 0.0)
            link(V.tensor_copy(planf[:, 2 * NU:2 * NU + 1], incl[:, NE - 1:NE]))
            V.tensor_copy(plan, planf).then_inc(plan_ready, 1)
            dve.wait_ge(plan_ready, 1)
            dve.sem_inc(gu_free, 4)
            dve.sem_inc(y_out, 2)
            n_units = dve.value_load(plan[0:1, 2 * NU:2 * NU + 1], min_val=1, max_val=NU)
            with dve.Fori(0, NU) as u:
                with dve.If(u < n_units):
                    with dve.Fori(0, FE // UPS) as i:
                        for s in range(UPS):
                            dve.wait_ge(e_silu, u * FE + i * UPS + s + 1)
                            tt(eh[:, bass.ds(i * UPS + s, 1), :], ps[:, s:s + 1, UNIT:2 * UNIT],
                               esil[:, s % 2:s % 2 + 1, :], ALU.mult).then_inc(gu_free, 1)
                    with dve.Fori(0, ND // 2) as j:
                        for s in range(2):
                            dve.wait_ge(y_filled, u * ND + j * 2 + s + 1 + DNS)
                            V.tensor_copy(yT[:, bass.ds(j * 2 + s, 1), :], ps[:, 4 + s:5 + s, 0:UNIT]).then_inc(y_out, 1)
            dve.wait_ge(final_gain, 16)
            for t in range(NT + 1):
                if t < NT:
                    dve.wait_ge(gathered[t], 32)
                    for j, gt in enumerate((g0, g1)):
                        last = V.scalar_tensor_tensor(out=x3[:, t, :], in0=back[:, 2 * t + j, :], scalar=gt[:, t:t + 1],
                                                      in1=x3[:, t, :], op0=ALU.mult, op1=ALU.add)
                        if j == 0:
                            link(last)
                    last.then_inc(sums_ready, 1)
                if t:
                    roots_in(t - 1, t)
                    V.scalar_tensor_tensor(out=x3[:, t - 1, :], in0=x3[:, t - 1, :], scalar=rr[:, t - 1:t],
                                           in1=g_mix, op0=ALU.mult, op1=ALU.mult).then_inc(fin_ready, 1)


def shape_tables():
    import numpy as np

    tab = np.zeros((P, T_W), np.float32)
    tab[:, T_ID:T_ID + P] = np.eye(P)
    tab[:, T_EPS] = EPS
    inv = np.float32(10000.0) ** (-np.arange(0, ROPE, 2, dtype=np.float32) / np.float32(ROPE))
    ang = np.arange(SEQ, dtype=np.float32)[:, None] * inv.astype(np.float32)[None, :]
    for at, f in ((T_COS, np.cos), (T_SIN, np.sin)):
        v = f(ang).astype(np.float32).reshape(NT, P, 1, 16).transpose(1, 0, 2, 3)
        tab[:, at:at + NT * HB * 16] = np.broadcast_to(v, (P, NT, HB, 16)).reshape(P, -1)
    gap = np.abs(np.arange(STRIP)[None, :] - (SEQ - P) - np.arange(P)[:, None])
    reach = (gap <= 64).astype(int) + ((gap % 4 == 0) & (gap <= 256)) + ((gap % 16 == 0) & (gap <= 1024))
    tab[:, T_DIST:T_DIST + STRIP] = gap
    tab[:, T_AMASK:T_AMASK + STRIP] = np.where(reach > 0, np.log(np.maximum(reach, 1)), NEG)
    qc = np.arange(P)[:, None] % GRID
    first = np.clip(qc - NAC // 2, 0, GRID - NAC)
    kc = np.arange(GRID)[None, :]
    tab[:, T_CMASK:T_CMASK + GRID] = np.where((kc >= first) & (kc < first + NAC), 0.0, NEG)
    tab[:, T_TRI:T_TRI + P] = np.arange(P)[:, None] < np.arange(P)[None, :]
    tab[:, T_ONES:T_ONES + P] = 1.0
    tab[:, T_UNIT:T_UNIT + NU * NE] = np.repeat(np.arange(NU), NE)[None, :]
    tab[:, T_E:T_E + NE] = np.arange(NE)[None, :]
    return tab


_INS = ["x", "g_mix", "w_in", "g_q", "g_kv", "w_uq", "w_ukv", "rpb", "g_out_a", "g_out_b", "g_out_c", "w_o",
        "g_ffn", "w1", "w3", "w2", "w_router", "e_w1", "e_w3", "e_w2", "g_final"]


def kernel(**inputs):
    import numpy as _np
    import concourse.bacc as _bacc
    from concourse import mybir as _mybir
    from concourse.bass_utils import run_bass_kernel_spmd as _run

    nc = _bacc.Bacc("TRN2", target_bir_lowering=False, num_devices=1)
    arrays, aps = {}, {}
    for name in _INS + ["tables"]:
        v = shape_tables() if name == "tables" else _np.ascontiguousarray(inputs[name])
        arrays[f"in_{name}_dram"] = v
        aps[name] = nc.dram_tensor(f"in_{name}_dram", v.shape, _mybir.dt.from_np(v.dtype), kind="ExternalInput").ap()
    aps["out"] = nc.dram_tensor("out_0_dram", (1, SEQ, D), F32, kind="ExternalOutput").ap()
    trunk(nc, aps)
    r = _run(nc, [arrays], core_ids=[0])
    return r.results[0]["out_0_dram"]
```
